# Optimizing a Trainium2 kernel written in Bass

```python
import jax, jax.numpy as jnp
from jax import lax
import numpy as np

D_MODEL = 1024
BATCH = 1
SEQ = 1024
DEPTH = 2
DEC_BATCH = 8
DEC_SEQ = 8
PAST_LEN = 4096
PAGE_SIZE = 128

HEAD_DIM = 64
H_RET = 6
H_SB = 5
H_FOX = 5
D_RET = H_RET * HEAD_DIM
D_SB = H_SB * HEAD_DIM
D_FOX = H_FOX * HEAD_DIM
D_MIX = D_RET + D_SB + D_FOX
IN_WIDTHS = (D_RET, D_RET, D_RET, D_RET, D_SB, D_SB, D_SB, D_SB, D_FOX, D_FOX, D_FOX, D_FOX, H_FOX)
IN_COLS = 4 * D_MIX + H_FOX
PLE_DIM = 256
Q_BLOCK = 128
RET_CHUNK = 128
ROPE_BASE = 10000.0
EPS = 1e-6

kernel_name = "hymba_retention_stickbreak_fox_step"

F32 = jnp.float32

def rms_norm(x, g):
    xf = x.astype(F32)
    y = xf * lax.rsqrt(jnp.mean(xf * xf, axis=-1, keepdims=True) + EPS)
    return (y * g.astype(F32)).astype(x.dtype)

def group_norm_heads(x, g):
    xf = x.astype(F32)
    mu = jnp.mean(xf, axis=-1, keepdims=True)
    var = jnp.mean(jnp.square(xf - mu), axis=-1, keepdims=True)
    y = (xf - mu) * lax.rsqrt(var + EPS)
    return (y * g.astype(F32).reshape(x.shape[2], x.shape[3])).astype(x.dtype)

def heads(a, h):
    return a.reshape(a.shape[0], a.shape[1], h, HEAD_DIM)

def rotary(x, pos):
    half = HEAD_DIM // 2
    inv = ROPE_BASE ** (-jnp.arange(half, dtype=F32) / half)
    ang = pos.astype(F32)[:, None] * inv[None, :]
    cos = jnp.cos(ang)[None, :, None, :]
    sin = jnp.sin(ang)[None, :, None, :]
    xf = x.astype(F32)
    x1, x2 = xf[..., :half], xf[..., half:]
    return jnp.concatenate([x1 * cos - x2 * sin, x1 * sin + x2 * cos], axis=-1).astype(x.dtype)

def to_blocks(a, blk):
    b, t = a.shape[0], a.shape[1]
    return jnp.moveaxis(a.reshape(b, t // blk, blk, *a.shape[2:]), 1, 0)

def from_blocks(a):
    a = jnp.moveaxis(a, 0, 1)
    return a.reshape(a.shape[0], a.shape[1] * a.shape[2], *a.shape[3:])

def retention(q, k, v, s0):
    h = q.shape[2]
    t = q.shape[1]
    blk = min(RET_CHUNK, t)
    log_g = jnp.log1p(-jnp.exp2(-5.0 - jnp.arange(h, dtype=F32)))
    i = jnp.arange(blk, dtype=F32)
    diff = i[:, None] - i[None, :]
    dmask = jnp.where(diff[None] >= 0,
                      jnp.exp(jnp.maximum(diff, 0.0)[None] * log_g[:, None, None]), 0.0)
    q_dec = jnp.exp((i + 1.0)[:, None] * log_g[None, :])
    k_dec = jnp.exp((blk - 1.0 - i)[:, None] * log_g[None, :])
    c_dec = jnp.exp(blk * log_g)

    def step(s, inp):
        qc, kc, vc = inp
        sc = jnp.einsum('bihd,bjhd->bhij', qc, kc) * dmask[None]
        inner = jnp.einsum('bhij,bjhe->bihe', sc, vc)
        cross = jnp.einsum('bihd,bhde->bihe', qc, s) * q_dec[None, :, :, None]
        s_new = s * c_dec[None, :, None, None] + jnp.einsum('bjhd,bjhe->bhde', kc * k_dec[None, :, :, None], vc)
        return s_new, inner + cross

    s_fin, out = lax.scan(step, s0.astype(F32), (to_blocks(q, blk), to_blocks(k, blk), to_blocks(v, blk)))
    return from_blocks(out), s_fin

def stick_breaking(q, k, v, q_pos, k_pos):
    blk = min(Q_BLOCK, q.shape[1])
    scale = HEAD_DIM ** -0.5

    def one(args):
        qb, pb = args
        z = (jnp.einsum('bthd,bshd->bhts', qb, k) * scale).astype(F32)
        mask = k_pos[None, :] < pb[:, None]
        ln1m = jnp.where(mask, jax.nn.log_sigmoid(-z), 0.0)
        rc = lax.cumsum(ln1m, axis=3, reverse=True)
        excl = jnp.concatenate([rc[..., 1:], jnp.zeros_like(rc[..., :1])], axis=-1)
        a = jnp.where(mask, jnp.exp(jax.nn.log_sigmoid(z) + excl), 0.0)
        return jnp.einsum('bhts,bshd->bthd', a.astype(v.dtype), v)

    out = lax.map(one, (to_blocks(q, blk), q_pos.reshape(-1, blk)))
    return from_blocks(out)

def forgetting_attention(q, k, v, q_pos, k_pos, c_q, c_k):
    blk = min(Q_BLOCK, q.shape[1])
    scale = HEAD_DIM ** -0.5
    ck = jnp.transpose(c_k, (0, 2, 1))[:, :, None, :]

    def one(args):
        qb, pb, cb = args
        s = (jnp.einsum('bthd,bshd->bhts', qb, k) * scale).astype(F32)
        s = s + jnp.transpose(cb, (0, 2, 1))[..., None] - ck
        mask = k_pos[None, :] <= pb[:, None]
        p = jax.nn.softmax(jnp.where(mask, s, -jnp.inf), axis=-1)
        return jnp.einsum('bhts,bshd->bthd', p.astype(v.dtype), v)

    out = lax.map(one, (to_blocks(q, blk), q_pos.reshape(-1, blk), to_blocks(c_q, blk)))
    return from_blocks(out)

def mixer(h, q_pos, ret_s0, sb_pk, sb_pv, fox_pk, fox_pv, fox_plogf,
          w_in, b_f, g_ret_gn, g_fox_q, g_fox_k, w_out):
    b, t, _ = h.shape
    proj = h @ w_in
    splits = np.cumsum(IN_WIDTHS)[:-1].tolist()
    (q_r, k_r, v_r, g_r, q_s, k_s, v_s, g_s, q_f, k_f, v_f, g_f, f_logit) = jnp.split(proj, splits, axis=-1)

    qr = rotary(heads(q_r, H_RET), q_pos)
    kr = rotary(heads(k_r, H_RET), q_pos) * (HEAD_DIM ** -0.5)
    o_r, s_new = retention(qr, kr, heads(v_r, H_RET), ret_s0)
    o_r = group_norm_heads(o_r.astype(h.dtype), g_ret_gn).reshape(b, t, D_RET)

    ks_new, vs_new = heads(k_s, H_SB), heads(v_s, H_SB)
    past = sb_pk.shape[1]
    k_pos = jnp.arange(past + t, dtype=jnp.int32)
    ks_all = jnp.concatenate([sb_pk.astype(ks_new.dtype), ks_new], axis=1)
    vs_all = jnp.concatenate([sb_pv.astype(vs_new.dtype), vs_new], axis=1)
    o_s = stick_breaking(heads(q_s, H_SB), ks_all, vs_all, q_pos, k_pos).reshape(b, t, D_SB)

    qf = rms_norm(heads(q_f, H_FOX), g_fox_q)
    kf_new = rms_norm(heads(k_f, H_FOX), g_fox_k)
    vf_new = heads(v_f, H_FOX)
    logf_new = jax.nn.log_sigmoid((f_logit + b_f).astype(F32))
    kf_all = jnp.concatenate([fox_pk.astype(kf_new.dtype), kf_new], axis=1)
    vf_all = jnp.concatenate([fox_pv.astype(vf_new.dtype), vf_new], axis=1)
    logf_all = jnp.concatenate([fox_plogf.astype(F32), logf_new], axis=1)
    c_all = lax.cumsum(logf_all, axis=1)
    o_f = forgetting_attention(qf, kf_all, vf_all, q_pos, k_pos, c_all[:, -t:], c_all).reshape(b, t, D_FOX)

    o = jnp.concatenate([o_r * jax.nn.silu(g_r), o_s * jax.nn.silu(g_s), o_f * jax.nn.silu(g_f)], axis=-1)
    return (o @ w_out, s_new, ks_new, vs_new, kf_new, vf_new, logf_new)

def per_layer_embed(x, p, w_pe, g_pe, w_pg):
    gate = jax.nn.sigmoid((rms_norm(x, g_pe) @ w_pg).astype(F32)).astype(x.dtype)
    return x + (p @ w_pe) * gate

def gather_pages(pool, page_table):
    g = pool[page_table]
    return g.reshape(g.shape[0], g.shape[1] * g.shape[2], *g.shape[3:])

def setup_inputs(seed: int = 0) -> dict:
    key = jax.random.key(seed)
    ks = jax.random.split(key, 24)
    n_pages = PAST_LEN // PAGE_SIZE
    used = DEC_BATCH * n_pages
    n_pool = used + max(1, used // 4)
    perm = jax.random.permutation(ks[0], n_pool)
    page_table = perm[:used].reshape(DEC_BATCH, n_pages).astype(jnp.int32)
    nrm = jax.random.normal
    return {
        "x_prompt": nrm(ks[1], (BATCH, SEQ, D_MODEL), F32),
        "x_sample": nrm(ks[2], (DEC_BATCH, DEC_SEQ, D_MODEL), F32),
        "state_ret": 0.3 * nrm(ks[3], (DEPTH, DEC_BATCH, H_RET, HEAD_DIM, HEAD_DIM), F32),
        "cache_sb_k": nrm(ks[4], (DEPTH, n_pool, PAGE_SIZE, H_SB, HEAD_DIM), F32),
        "cache_sb_v": nrm(ks[5], (DEPTH, n_pool, PAGE_SIZE, H_SB, HEAD_DIM), F32),
        "cache_fox_k": nrm(ks[6], (DEPTH, n_pool, PAGE_SIZE, H_FOX, HEAD_DIM), F32),
        "cache_fox_v": nrm(ks[7], (DEPTH, n_pool, PAGE_SIZE, H_FOX, HEAD_DIM), F32),
        "cache_fox_logf": jax.nn.log_sigmoid(3.0 + nrm(ks[8], (DEPTH, n_pool, PAGE_SIZE, H_FOX), F32)),
        "page_table": page_table,
        "p_prompt": nrm(ks[9], (DEPTH, BATCH, SEQ, PLE_DIM), F32),
        "p_sample": nrm(ks[10], (DEPTH, DEC_BATCH, DEC_SEQ, PLE_DIM), F32),
        "g_norm": 1.0 + 0.05 * nrm(ks[11], (DEPTH, D_MODEL), F32),
        "w_in": nrm(ks[12], (DEPTH, D_MODEL, IN_COLS), F32) * D_MODEL ** -0.5,
        "b_f": jax.random.uniform(ks[13], (DEPTH, H_FOX), F32, 1.0, 5.0),
        "g_ret_gn": 1.0 + 0.05 * nrm(ks[14], (DEPTH, D_RET), F32),
        "g_fox_q": 1.0 + 0.05 * nrm(ks[15], (DEPTH, HEAD_DIM), F32),
        "g_fox_k": 1.0 + 0.05 * nrm(ks[16], (DEPTH, HEAD_DIM), F32),
        "w_out": nrm(ks[17], (DEPTH, D_MIX, D_MODEL), F32) * D_MIX ** -0.5,
        "w_pe": nrm(ks[18], (DEPTH, PLE_DIM, D_MODEL), F32) * PLE_DIM ** -0.5,
        "g_pe": 1.0 + 0.05 * nrm(ks[19], (DEPTH, D_MODEL), F32),
        "w_pg": nrm(ks[20], (DEPTH, D_MODEL, D_MODEL), F32) * D_MODEL ** -0.5,
    }

def reference(x_prompt, x_sample, state_ret, cache_sb_k, cache_sb_v, cache_fox_k, cache_fox_v,
              cache_fox_logf, page_table, p_prompt, p_sample,
              g_norm, w_in, b_f, g_ret_gn, g_fox_q, g_fox_k, w_out, w_pe, g_pe, w_pg):
    bp, tp = x_prompt.shape[0], x_prompt.shape[1]
    ts = x_sample.shape[1]
    past_len = page_table.shape[1] * PAGE_SIZE
    pos_p = jnp.arange(tp, dtype=jnp.int32)
    pos_s = past_len + jnp.arange(ts, dtype=jnp.int32)
    dt = x_prompt.dtype
    zero_ret = jnp.zeros((bp, H_RET, HEAD_DIM, HEAD_DIM), F32)
    empty_sb = jnp.zeros((bp, 0, H_SB, HEAD_DIM), dt)
    empty_fox = jnp.zeros((bp, 0, H_FOX, HEAD_DIM), dt)
    empty_logf = jnp.zeros((bp, 0, H_FOX), F32)

    y_p, y_s = x_prompt, x_sample
    rs_p, rs_s, skp, svp, sks, svs = [], [], [], [], [], []
    fkp, fvp, flp, fks, fvs, fls = [], [], [], [], [], []
    for i in range(DEPTH):
        w = (w_in[i], b_f[i], g_ret_gn[i], g_fox_q[i], g_fox_k[i], w_out[i])
        m, s_new, k1, v1, k2, v2, l2 = mixer(rms_norm(y_p, g_norm[i]), pos_p, zero_ret,
                                             empty_sb, empty_sb, empty_fox, empty_fox, empty_logf, *w)
        y_p = per_layer_embed(y_p + m, p_prompt[i], w_pe[i], g_pe[i], w_pg[i])
        rs_p.append(s_new); skp.append(k1); svp.append(v1); fkp.append(k2); fvp.append(v2); flp.append(l2)
        m, s_new, k1, v1, k2, v2, l2 = mixer(
            rms_norm(y_s, g_norm[i]), pos_s, state_ret[i],
            gather_pages(cache_sb_k[i], page_table), gather_pages(cache_sb_v[i], page_table),
            gather_pages(cache_fox_k[i], page_table), gather_pages(cache_fox_v[i], page_table),
            gather_pages(cache_fox_logf[i], page_table), *w)
        y_s = per_layer_embed(y_s + m, p_sample[i], w_pe[i], g_pe[i], w_pg[i])
        rs_s.append(s_new); sks.append(k1); svs.append(v1); fks.append(k2); fvs.append(v2); fls.append(l2)

    st = lambda lst: jnp.stack(lst, axis=0)
    return (y_p, y_s, st(rs_p), st(rs_s), st(skp), st(svp), st(sks), st(svs),
            st(fkp), st(fvp), st(flp), st(fks), st(fvs), st(fls))


_drawn_inputs = setup_inputs


def setup_inputs(seed=0):
    import zlib

    import numpy as np

    out = dict(_drawn_inputs(seed))
    spreads = {}
    factors = {'cache_fox_logf': 3.857, 'g_ret_gn': 2.69, 'g_fox_q': 8.0, 'g_pe': 4.871}
    for name, (base, spread) in spreads.items():
        noise = np.random.default_rng([zlib.crc32(name.encode()), seed]).standard_normal(out[name].shape)
        drawn = base * np.exp(spread * noise) if base else spread * noise
        out[name] = __import__('jax').numpy.asarray(drawn.astype(out[name].dtype))
    for name, factor in factors.items():
        out[name] = (out[name] * factor).astype(out[name].dtype)
    return out
```

```python
from contextlib import ExitStack

import numpy as np

import concourse.bass as bass
from concourse import mybir

F32 = mybir.dt.float32
BF16 = mybir.dt.bfloat16
I32 = mybir.dt.int32
ALU = mybir.AluOpType
ACT = mybir.ActivationFunctionType
AX = mybir.AxisListType.X

P = 128
D = 1024
KC = D // P
SEQ = 1024
NT = SEQ // P
SAMPLE = NT
TILES = NT + 1
DEPTH = 2
SEQS, NEW = 8, 8
ROWS = SEQS * NEW
HD = 64
HR, HA = 6, 5
DR, DA = HR * HD, HA * HD
PAGES = 32
PAST = PAGES * P
PLE = 256
EPS = 1e-6
NEG = -1e30
PG8 = 8
GROUPS = PAGES // PG8
HI = HA * NEW
SLOT = PAGES + 1
QP = HR // 2

SEG_NAMES = ["rq", "rk", "rv", "rg", "sq", "sk", "sv", "sg", "fg", "fq", "fk", "fv"]
SEG_COL = dict(rq=0, rk=DR, rv=2 * DR, rg=3 * DR, sq=4 * DR, sk=4 * DR + DA, sv=4 * DR + 2 * DA,
               sg=4 * DR + 3 * DA, fq=4 * DR + 4 * DA, fk=4 * DR + 5 * DA, fv=4 * DR + 6 * DA,
               fg=4 * DR + 7 * DA)
SEG_W = {s: DR if s[0] == "r" else DA for s in SEG_NAMES}
SEG_W["fg"] = DA + HA
ALL_SEGS = SEG_NAMES + ["out0", "out1", "pg0", "pe0", "pg1", "pe1"]
DVE_EVACUATES = {"rq", "rk", "rg", "sg", "fg", "out0", "out1", "pe0", "pe1"}
TURNED = {"rq": TILES, "rk": TILES, "sq": NT, "sk": NT, "fq": NT, "fk": NT}
GATE_AT = {"rg": 0, "sg": DR, "fg": DR + DA}


def rows(t):
    return ROWS if t == SAMPLE else P


def evac_count(seg, t):
    same = (seg in DVE_EVACUATES)
    before = [s for s in ALL_SEGS[:ALL_SEGS.index(seg)] if (s in DVE_EVACUATES) == same]
    return len(before) * TILES + t + 1


def turn_index(seg, t):
    return sum(n for s, n in TURNED.items() if ALL_SEGS.index(s) < ALL_SEGS.index(seg)) + t


def nat_count(seg, t):
    made = ["rq", "rk", "fq", "fk"]
    return TILES * made.index(seg) + t + 1


def tables():
    j, i = np.arange(P)[:, None], np.arange(P)[None, :]
    r = np.arange(P)
    log_g = np.log1p(-np.exp2(-5.0 - np.arange(HR)))
    inv = 10000.0 ** (-np.arange(HD // 2) / (HD // 2))
    pos = np.zeros((P, TILES))
    pos[:, :NT] = r[:, None] + P * np.arange(NT)[None, :]
    pos[:, SAMPLE] = PAST + r % NEW
    ang = pos[:, :, None].astype(np.float32) * inv.astype(np.float32)[None, None, :]
    ang = ang.astype(np.float64)
    b, k = r // NEW, r % NEW
    pair_head = 2 * np.arange(QP)[None, :] + (r // HD)[:, None]
    t = {}
    t["ident"] = np.eye(P)
    t["earlier"] = j < i
    t["negones"] = -np.ones((P, P))
    t["ones"] = np.ones((P, P))
    t["neg_upto"] = -1.0 * (j <= i)
    t["later_page"] = (j // PAGES == i // PAGES) & (j > i)
    t["neg_upto_new"] = (-1.0 * ((j // NEW == i // NEW) & (j <= i)))[:, :ROWS]
    t["cos"] = np.concatenate([np.cos(ang), np.cos(ang)], -1)
    t["sin"] = np.concatenate([-np.sin(ang), np.sin(ang)], -1)
    t["row_grow"] = np.exp((r[:, None] + 1.0) * log_g)
    t["col_grow"] = np.exp(-(r[:, None] + 1.0) * log_g) / 8
    t["key_decay"] = np.exp((P - 1.0 - r[:, None]) * log_g) / 8
    t["row_grow_new"] = np.exp((k[:, None] + 1.0) * log_g)
    t["col_grow_new"] = np.exp(-(k[:, None] + 1.0) * log_g) / 8
    t["key_decay_new"] = np.exp((NEW - 1.0 - k[:, None]) * log_g) / 8
    t["chunk_decay"] = np.exp(P * log_g)[pair_head]
    t["chunk_decay_new"] = np.exp(NEW * log_g)[pair_head]
    t["upto"] = j <= i
    t["upto_new"] = ((j // NEW == i // NEW) & (j <= i))[:, :ROWS]
    t["own_seq"] = b[:, None] == np.arange(SEQS)[None, :]
    t["before"] = i < j
    t["after_neg"] = np.where(i > j, NEG, 0.0)
    q = np.arange(NEW)[None, None, :]
    same = b[:, None, None] == np.arange(SEQS)[None, :, None]
    t["new_neg_sb"] = np.where(same & (k[:, None, None] < q), 0.0, NEG)
    t["new_neg_fox"] = np.where(same & (k[:, None, None] <= q), 0.0, NEG)
    return {n: np.asarray(v, np.float32).reshape(P, -1) for n, v in t.items()}


def table_places():
    at, places = 0, {}
    for name, v in tables().items():
        places[name] = (at, v.shape[1])
        at += v.shape[1]
    return places, at


STORES = 2 + QP + TILES + 2 + TILES

DECODE_STEPS = {"sb": 3, "fox": 3}


class Steps:

    def __init__(self, eng, sem):
        self.eng, self.sem, self.n, self.base = eng, sem, 0, 0

    def __call__(self, ins):
        self.n += 1
        ins.then_inc(self.sem, 1)
        self.eng.wait_ge(self.sem, self.base + self.n)

    def turn(self, b, per, first):
        self.base, self.n = b * per + first, 0


def step_program(nc, x_prompt, x_sample, state_ret, cache_sb_k, cache_sb_v, cache_fox_k,
                 cache_fox_v, cache_fox_logf, page_table, p_prompt, p_sample, g_norm, w_in, b_f,
                 g_ret_gn, g_fox_q, g_fox_k, w_out, w_pe, g_pe, w_pg, consts,
                 y_prompt, y_sample, rs_prompt, rs_sample, sbk_prompt, sbv_prompt, sbk_sample,
                 sbv_sample, foxk_prompt, foxv_prompt, foxl_prompt, foxk_sample, foxv_sample,
                 foxl_sample):
    n_pool = cache_sb_k.shape[1]
    residual_dram = nc.dram_tensor("residual_scratch", (TILES * P, D), F32, kind="Internal").ap()
    decoded_dram = nc.dram_tensor("decoded_scratch", (2, ROWS, DA), F32, kind="Internal").ap()
    logf_dram = nc.dram_tensor("logf_scratch", (SEQS * PAGES, P * HA), F32, kind="Internal").ap()
    places, n_consts = table_places()

    with ExitStack() as ctx:
        def sb(name, shape, dt=F32):
            return ctx.enter_context(nc.sbuf_tensor(name, shape, dt))

        def sem(name):
            return ctx.enter_context(nc.semaphore(name))

        xT = sb("xT", [P, KC, SEQ + ROWS])
        O = sb("O", [P, TILES, D])
        W = [sb(f"W{i}", [P, KC, 512]) for i in range(2)]
        C = sb("C", [P, n_consts])
        reset = sb("reset", [P, HI * SLOT], BF16)
        pages = sb("pages", [1, SEQS * PAGES], I32)
        gT = sb("gT", [P, 2, KC])
        g_ret_b = sb("g_ret_b", [P, DR])
        g_fq_b = sb("g_fq_b", [P, HD])
        g_fk_b = sb("g_fk_b", [P, HD])
        b_f_b = sb("b_f_b", [P, HA])
        eps = sb("eps", [P, 1])
        small = sb("small", [P, 256])
        row_max = sb("row_max", [P, P])
        q_new = sb("q_new", [ROWS, DA + HD])
        k_new = sb("k_new", [ROWS, DA])
        v_new = sb("v_new", [ROWS, DA])
        branch = sb("branch", [P, 15520])
        work = sb("work", [P, 5504])

        def cut(region, at, *shape):
            n = int(np.prod(shape))
            v = region[:, at:at + n]
            if len(shape) == 2:
                v = v.rearrange("p (a b) -> p a b", a=shape[0])
            if len(shape) == 3:
                v = v.rearrange("p (a b c) -> p a b c", a=shape[0], b=shape[1])
            if len(shape) == 4:
                v = v.rearrange("p (a b c d) -> p a b c d", a=shape[0], b=shape[1], c=shape[2])
            return v

        def const(name, *shape):
            at, n = places[name]
            return cut(C, at, *shape) if shape else C[:, at:at + n]

        ident = const("ident")
        ones = const("ones")
        cos_t, sin_t = const("cos", TILES, HD), const("sin", TILES, HD)

        TR = SEQ + ROWS
        qT_r, kT_r = cut(branch, 0, QP, TR), cut(branch, QP * TR, QP, TR)
        v_r = cut(branch, 2 * QP * TR, TILES, DR)
        kd_r = cut(branch, 2 * QP * TR + TILES * DR, TILES, DR)
        at = 2 * QP * TR + 2 * TILES * DR
        s0 = cut(branch, at, QP, SEQS, HD)
        state = cut(branch, at + QP * SEQS * HD, QP, HD)
        qT_s, kT_s = cut(branch, 0, QP, SEQ), cut(branch, QP * SEQ, QP, SEQ)
        v_s = cut(branch, 2 * QP * SEQ, NT, DA)
        at = 2 * QP * SEQ + NT * DA
        sig = cut(branch, at, 2, SEQ)
        att = cut(branch, at + 2 * SEQ, 2, SEQ)
        rest = branch[:, at + 4 * SEQ:at + 5 * SEQ]
        prod = branch[:, at + 5 * SEQ:at + 6 * SEQ + 1]
        qT_f, kT_f = cut(branch, 0, HA, SEQ), cut(branch, HA * SEQ, HA, SEQ)
        v_f = cut(branch, 2 * HA * SEQ, NT, DA)
        junk = work[:, 0:D]
        scaled = cut(work, D, 2, D)
        nat = cut(work, 0, 2, DR)
        rot_a, rot_b = work[:, 768:768 + DR], work[:, 1152:1152 + DR]
        aug = cut(work, 1536, 2, HA, HD + 1)
        squares = cut(work, 2200, HA, HD)
        logit = cut(work, 2600, TILES, HA)
        ltmp = cut(work, 2650, TILES, HA)
        logf_padded = cut(work, 2700, NT - 1 + TILES, HA)
        logf = logf_padded[:, NT - 1:]
        neg_c = cut(small, 64, TILES, HA)
        masked = cut(work, 0, 2, P)
        ret_o, ret_sq = cut(work, 256, HR, HD), cut(work, 640, HR, HD)
        cross = cut(work, 1024, SEQS, HD)
        v_seq = cut(work, 1536, 2, SEQS * HD)
        expd = cut(work, 0, 2, SEQ)
        attT = cut(work, 2 * SEQ, 2, SEQ)
        ringK = cut(branch, 0, 2, PG8 * DA)
        ringV = cut(branch, 2 * PG8 * DA, 2, PG8 * DA)
        at = 4 * PG8 * DA
        NZ = HI * SLOT
        zs = branch[:, at:at + NZ]
        soft = branch[:, at + NZ:at + 2 * NZ]
        later = branch[:, at + 2 * NZ:at + 3 * NZ]
        probs = branch[:, at + 3 * NZ:at + 4 * NZ]
        kT_d = cut(work, 0, 4, 512)
        qd = cut(work, 2048, SEQS, 5, 2 * NEW)
        kT_new = cut(work, 2688, 3, ROWS)
        decoded = cut(work, 2880, SEQS, 2, HD)
        forget = cut(work, 3904, HA, SEQS * PAGES)
        new_bias = cut(work, 5184, SEQS, HA, NEW)
        page_logf = cut(branch, 0, 2, P, HA)
        page_sum = cut(branch, 1280, 2, HA, P)
        x_half = cut(work, 0, 2, 512)
        p_nat = cut(branch, 0, TILES, PLE)
        pT = cut(branch, TILES * PLE, 2, TR)
        gate = cut(branch, TILES * PLE + 2 * TR, TILES, 512)
        gated = cut(work, 1024, 2, 512)

        ps = ctx.enter_context(nc.psum_tensor("ps", [P, 8, 512], F32))

        arrived = sem("arrived")
        layer_go = sem("layer_go")
        consts_in = sem("consts_in")
        set_up = sem("set_up")
        x_in = sem("x_in")
        y_out = sem("y_out")
        x_saved = sem("x_saved")
        k_saved = [sem(f"k_saved{i}") for i in range(2)]
        saved = sem("saved")
        logf_gathered = sem("logf_gathered")
        logf_in = sem("logf_in")
        stored = {k: sem(f"stored_{k}") for k in ("sb", "fox")}
        phase_sem = sem("phase_sem")
        w_loaded = [sem(f"w_loaded{i}") for i in range(2)]
        vec_loaded = sem("vec_loaded")
        pool_ready = sem("pool_ready")
        squared = sem("squared")
        rooted = sem("rooted")
        scaled_ready = sem("scaled_ready")
        norm_turned = sem("norm_turned")
        norm_out = sem("norm_out")
        proj_ready = sem("proj_ready")
        emptied_dve = sem("emptied_dve")
        emptied_act = sem("emptied_act")
        nat_ready = sem("nat_ready")
        turned = sem("turned")
        turned_out = sem("turned_out")
        sigmoid_ready = sem("sigmoid_ready")
        head_sums = sem("head_sums")
        head_roots = sem("head_roots")
        logit_ready = sem("logit_ready")
        logf_act = sem("logf_act")
        logf_ready = sem("logf_ready")
        cum_ready = sem("cum_ready")
        neg_c_ready = sem("neg_c_ready")
        scores_r = sem("scores_r")
        masked_r = sem("masked_r")
        inner_r = sem("inner_r")
        ret_emptied = sem("ret_emptied")
        kv_r = sem("kv_r")
        state_r = sem("state_r")
        centred_r = sem("centred_r")
        squares_r = sem("squares_r")
        sums_r = sem("sums_r")
        roots_r = sem("roots_r")
        state_in = sem("state_in")
        cross_ready = sem("cross_ready")
        cross_emptied = sem("cross_emptied")
        v_seq_ready = sem("v_seq_ready")
        new_state_ready = sem("new_state_ready")
        new_state_out = sem("new_state_out")
        att_scores = {k: sem(f"att_scores_{k}") for k in ("sb", "fox")}
        att_first = {k: sem(f"att_first_{k}") for k in ("sb", "fox")}
        att_probs = {"sb": sem("att_probs_sb")}
        att_max = sem("att_max")
        att_emptied = sem("att_emptied")
        att_turned = {k: sem(f"att_turned_{k}") for k in ("sb", "fox")}
        attT_ready = {k: sem(f"attT_ready_{k}") for k in ("sb", "fox")}
        att_out = {k: sem(f"att_out_{k}") for k in ("sb", "fox")}
        att_done = {k: sem(f"att_done_{k}") for k in ("sb", "fox")}
        steps_sem = sem("steps_sem")
        dec = {}
        for k in ("sb", "fox"):
            dec[k] = {n: sem(f"{n}_{k}") for n in (
                "k0", "k1", "v0", "v1", "new_turned", "new_ready", "kt_ready", "kt_act", "kt_dve",
                "scores_done", "z_ready", "z_emptied", "fold_ready", "fold_out", "bias_ready",
                "soft_in", "soft_act", "soft_ready", "sum_ready", "expo_ready", "probs_ready",
                "v_used", "pv_done", "o_emptied", "loaded", "den_ready")}
        page_ready = sem("page_ready")
        page_carry = sem("page_carry")
        forget_part = sem("forget_part")
        forget_turned = sem("forget_turned")
        forget_ready = sem("forget_ready")
        mixed_turned = sem("mixed_turned")
        mixed_out = sem("mixed_out")
        x_half_in = [sem(f"x_half_in{i}") for i in range(2)]
        p_in = sem("p_in")
        p_turned = sem("p_turned")
        p_out = sem("p_out")
        pool_waits = sem("pool_waits")
        last_sem = sem("last_sem")

        def phase_over(eng, n):
            eng.drain().then_inc(phase_sem, 1)
            eng.wait_ge(phase_sem, 4 * (n + 1))

        def layer_over(eng, L):
            eng.drain().then_inc(arrived, 1)
            eng.wait_ge(layer_go, L + 1)

        (NORM1, PROJ_R, RET, PROJ_S, ATT_S, DEC_S, PROJ_F, ATT_F, DEC_F, MIXED, OUT, NORM2, PLE_T,
         GATED) = range(14)
        NORMS = {NORM1: 0, NORM2: 1}
        PROJ_SEGS = {PROJ_R: SEG_NAMES[0:4], PROJ_S: SEG_NAMES[4:8], PROJ_F: SEG_NAMES[8:12],
                     OUT: ["out0", "out1"], GATED: ["pg0", "pe0", "pg1", "pe1"]}
        KIND = {ATT_S: "sb", ATT_F: "fox", DEC_S: "sb", DEC_F: "fox"}
        CACHE = {"sb": (cache_sb_k, cache_sb_v), "fox": (cache_fox_k, cache_fox_v)}
        UNITS = [(t, h) for t in range(NT) for h in range(HA)]

        def bank2(first, n=1024):
            return ps[:, first:first + 2, :].rearrange("p b c -> p (b c)")[:, 0:n]

        def flat3(first=2):
            return ps[:, first:first + 3, :].rearrange("p b c -> p (b c)")

        block = ctx.enter_context(nc.Block())

        @block.sync
        def _(sp):
            sp.dma_start(C[:], consts).then_inc(consts_in, 16)
            sp.dma_start(pages[:], page_table.rearrange("b p -> (b p)").unsqueeze(0)).then_inc(consts_in, 16)
            sp.dma_start(O[:, 0:NT, :], x_prompt[0].rearrange("(t p) d -> p t d", p=P)).then_inc(x_in, 16)
            sp.dma_start(O[0:ROWS, SAMPLE, :], x_sample.rearrange("b s d -> (b s) d")).then_inc(x_in, 16)
            sp.wait_ge(consts_in, 32)

            def load_weights(L, seg):
                i = ALL_SEGS.index(seg)
                if i >= 2:
                    sp.wait_ge(proj_ready, TILES * (i - 1))
                if seg in SEG_COL:
                    n = SEG_W[seg]
                    src = w_in[L, :, SEG_COL[seg]:SEG_COL[seg] + n]
                    kc = KC
                else:
                    n, c = 512, int(seg[-1])
                    src = {"ou": w_out, "pg": w_pg, "pe": w_pe}[seg[:2]][L, :, c * 512:(c + 1) * 512]
                    kc = PLE // P if seg[:2] == "pe" else KC
                sp.dma_start(W[i % 2][:, 0:kc, 0:n], src.rearrange("(k p) n -> p k n", p=P))\
                    .then_inc(w_loaded[i % 2], 16)

            def load_page(L, cache, dst, b, p, done):
                at = b * PAGES + p
                pg = sp.value_load(pages[0:1, bass.ds(at, 1)], min_val=0, max_val=n_pool - 1)
                src = cache[L, bass.ds(pg, 1)].rearrange("a s h d -> s (a h d)")
                sp.dma_start(dst, src).then_inc(done, 16)

            def load_k(L, kind, b, g):
                s = dec[kind]
                if not (isinstance(b, int) and 4 * b + g < 2):
                    sp.wait_ge(s["kt_ready"], b * 20 + 5 * (g - 1))
                for p in range(PG8):
                    load_page(L, CACHE[kind][0], ringK[:, g % 2, p * DA:(p + 1) * DA], b,
                              g * PG8 + p, s[f"k{g % 2}"])

            def load_v(L, kind, b, g):
                s = dec[kind]
                sp.wait_ge(s["v_used"], b * GROUPS + g + 1)
                for p in range(PG8):
                    load_page(L, CACHE[kind][1], ringV[:, g % 2, p * DA:(p + 1) * DA], b,
                              g * PG8 + p, s[f"v{g % 2}"])

            def decode_loads(L, kind):
                for g in range(GROUPS):
                    load_k(L, kind, 0, g)
                with sp.Fori(1, SEQS) as b:
                    for g in range(2):
                        load_k(L, kind, b, g)
                        load_v(L, kind, b - 1, g)
                    for g in range(2, GROUPS):
                        load_k(L, kind, b, g)
                    for g in range(2, GROUPS):
                        load_v(L, kind, b - 1, g)
                for g in range(GROUPS):
                    load_v(L, kind, SEQS - 1, g)
                sp.wait_ge(stored[kind], 16 * HA * (L + 1))
                sp.dma_start(work[0:ROWS, 0:DA], decoded_dram[0 if kind == "sb" else 1])\
                    .then_inc(dec[kind]["loaded"], 16)

            with sp.Fori(0, DEPTH) as L:
                load_weights(L, "rq")
                load_weights(L, "rk")
                for dst, src in (
                        (gT[:, 0, :], g_norm[L].rearrange("(k p) -> p k", p=P)),
                        (gT[:, 1, :], g_pe[L].rearrange("(k p) -> p k", p=P)),
                        (g_ret_b[:], g_ret_gn[L].partition_broadcast(P)),
                        (g_fq_b[:], g_fox_q[L].partition_broadcast(P)),
                        (g_fk_b[:], g_fox_k[L].partition_broadcast(P)),
                        (b_f_b[:], b_f[L].partition_broadcast(P))):
                    sp.dma_start(dst, src, allow_slow_non_contiguous=True).then_inc(vec_loaded, 16)
                for pr in range(QP):
                    sp.dma_start(s0[:, pr], state_ret[L, :, 2 * pr:2 * pr + 2].rearrange(
                        "b h d e -> (h d) b e")).then_inc(state_in, 16)
                for seg in SEG_NAMES[2:10]:
                    load_weights(L, seg)
                sp.wait_ge(phase_sem, 4 * (ATT_S + 1))
                decode_loads(L, "sb")
                for seg in ALL_SEGS[10:14]:
                    load_weights(L, seg)
                sp.wait_ge(phase_sem, 4 * (ATT_F + 1))
                sp.wait_ge(forget_ready, HA)
                decode_loads(L, "fox")
                sp.wait_ge(phase_sem, 4 * (MIXED + 1))
                sp.wait_ge(x_saved, 32 * (L + 1))
                for c in range(2):
                    for t in range(TILES):
                        n = c * TILES + t
                        if n >= 2:
                            sp.wait_ge(emptied_dve, evac_count("out0", 0) + n - 2)
                        sp.dma_start(x_half[0:rows(t), n % 2, :], residual_dram[
                            t * P:t * P + rows(t), c * 512:(c + 1) * 512]).then_inc(x_half_in[n % 2], 16)
                sp.wait_ge(phase_sem, 4 * (NORM2 + 1))
                sp.dma_start(p_nat[:, 0:NT, :], p_prompt[L, 0].rearrange("(t p) c -> p t c", p=P))\
                    .then_inc(p_in, 16)
                sp.dma_start(p_nat[0:ROWS, SAMPLE, :], p_sample[L].rearrange("b s c -> (b s) c"))\
                    .then_inc(p_in, 16)
                for seg in ALL_SEGS[14:18]:
                    load_weights(L, seg)
                sp.wait_ge(arrived, 4 * (L + 1))
                sp.sem_inc(last_sem, 1)
                sp.sem_clear(range(phase_sem.num, last_sem.num + 1))
                sp.sem_inc(layer_go, 1)

        @block.gpsimd
        def _(pool):
            def await_dma(done, value):
                pool.wait_ge(done, value)
                pool.sem_inc(pool_waits, 1)

            nc.gpsimd.memset(eps[:], EPS).then_inc(set_up, 1)
            nc.gpsimd.memset(reset[:], 1.0).then_inc(set_up, 1)
            pool.wait_ge(set_up, 2)
            nc.gpsimd.memset(reset[:].rearrange("p (r s) -> p r s", s=SLOT)[:, :, SLOT - 1:SLOT],
                             0.0).then_inc(set_up, 1)
            pool.wait_ge(consts_in, 32)
            pool.wait_ge(x_in, 32)
            with pool.Fori(0, DEPTH) as L:
                stores = 0
                pool.dma_start(residual_dram[0:SEQ].rearrange("(t p) d -> p t d", p=P),
                               O[:, 0:NT, :]).then_inc(x_saved, 16)
                pool.dma_start(residual_dram[SEQ:SEQ + ROWS], O[0:ROWS, SAMPLE, :]).then_inc(x_saved, 16)
                await_dma(x_saved, 32 * (L + 1))
                phase_over(pool, NORM1)
                with pool.Fori(0, SEQS * PAGES) as p:
                    pg = pool.value_load(pages[0:1, bass.ds(p, 1)], min_val=0, max_val=n_pool - 1)
                    pool.dma_start(logf_dram[bass.ds(p, 1)],
                                   cache_fox_logf[L, bass.ds(pg, 1)].rearrange("a s h -> a (s h)"))\
                        .then_inc(logf_gathered, 16)
                phase_over(pool, PROJ_R)
                pool.wait_ge(state_r, NT)
                for h2 in range(2):
                    pool.dma_start(rs_prompt[L, 0].rearrange("(pr h) d e -> h d pr e", h=2)[h2],
                                   state[h2 * HD:(h2 + 1) * HD]).then_inc(saved, 16)
                    stores += 1
                pool.wait_ge(new_state_out, HR)
                for pr in range(QP):
                    pool.dma_start(rs_sample[L, :, 2 * pr:2 * pr + 2].rearrange("b h d e -> (h d) b e"),
                                   s0[:, pr]).then_inc(saved, 16)
                    stores += 1
                await_dma(saved, L * 16 * STORES + 16 * stores)
                phase_over(pool, RET)

                def store_kv(seg, t, src, prompt, sample, done, ready, count):
                    pool.wait_ge(ready, count)
                    if t == SAMPLE:
                        dst = sample[L].rearrange("b s h d -> (b s) (h d)")
                    else:
                        dst = prompt[L, 0, t * P:(t + 1) * P].rearrange("p h d -> p (h d)")
                    pool.dma_start(dst, src).then_inc(done, 16)

                for t in range(TILES):
                    src = k_new[:] if t == SAMPLE else nat[:, turn_index("sk", t) % 2, 0:DA]
                    store_kv("sk", t, src, sbk_prompt, sbk_sample, k_saved[t % 2],
                             emptied_act, evac_count("sk", t))
                for t in range(TILES):
                    src = v_new[:] if t == SAMPLE else v_s[:, t]
                    store_kv("sv", t, src, sbv_prompt, sbv_sample, saved, emptied_act,
                             evac_count("sv", t))
                    stores += 1
                await_dma(k_saved[0], L * 160 + 16 * 5)
                await_dma(k_saved[1], L * 128 + 16 * 4)
                await_dma(saved, L * 16 * STORES + 16 * stores)
                phase_over(pool, PROJ_S)
                phase_over(pool, ATT_S)

                def decoded_store(kind):
                    pool.wait_ge(dec[kind]["o_emptied"], SEQS + 1)
                    dst = decoded_dram[0 if kind == "sb" else 1].rearrange("(b i) c -> i b c", b=SEQS)
                    for h in range(HA):
                        q = 32 * (h % 4)
                        pool.dma_start(dst[:, :, h * HD:(h + 1) * HD], decoded[q:q + NEW, :, h // 4, :])\
                            .then_inc(stored[kind], 16)

                decoded_store("sb")
                phase_over(pool, DEC_S)
                pool.wait_ge(logf_ready, 1)
                pool.dma_start(foxl_prompt[L, 0].rearrange("(t p) h -> p t h", p=P), logf[:, 0:NT, :])\
                    .then_inc(saved, 16)
                pool.dma_start(foxl_sample[L].rearrange("b s h -> (b s) h"), logf[0:ROWS, SAMPLE, :])\
                    .then_inc(saved, 16)
                stores += 2
                for t in range(TILES):
                    src = k_new[:].rearrange("p (h d) -> p h d", h=HA) if t == SAMPLE else \
                        aug[:, turn_index("fk", t) % 2, :, 0:HD]
                    pool.wait_ge(nat_ready, nat_count("fk", t))
                    dst = foxk_sample[L].rearrange("b s h d -> (b s) h d") if t == SAMPLE else \
                        foxk_prompt[L, 0, t * P:(t + 1) * P]
                    pool.dma_start(dst, src).then_inc(k_saved[t % 2], 16)
                for t in range(TILES):
                    src = v_new[:] if t == SAMPLE else v_f[:, t]
                    store_kv("fv", t, src, foxv_prompt, foxv_sample, saved, emptied_act,
                             evac_count("fv", t))
                    stores += 1
                await_dma(k_saved[0], L * 160 + 16 * 10)
                await_dma(k_saved[1], L * 128 + 16 * 8)
                await_dma(saved, L * 16 * STORES + 16 * stores)
                phase_over(pool, PROJ_F)
                phase_over(pool, ATT_F)
                await_dma(logf_gathered, 16 * SEQS * PAGES * (L + 1))
                pool.dma_start(page_logf.rearrange("p a s h -> p a (s h)"),
                               logf_dram.rearrange("(a p) n -> p a n", p=P)).then_inc(logf_in, 16)
                decoded_store("fox")
                phase_over(pool, DEC_F)
                for n in (MIXED, OUT, NORM2, PLE_T, GATED):
                    phase_over(pool, n)
                assert stores == STORES
                layer_over(pool, L)
            pool.dma_start(y_prompt[0].rearrange("(t p) d -> p t d", p=P), O[:, 0:NT, :]).then_inc(y_out, 16)
            pool.dma_start(y_sample.rearrange("b s d -> (b s) d"), O[0:ROWS, SAMPLE, :]).then_inc(y_out, 16)
            pool.wait_ge(y_out, 32)

        @block.tensor
        def _(pe):
            pe.wait_ge(consts_in, 32)
            pe.wait_ge(set_up, 3)

            def norm(phase):
                for t in range(TILES):
                    m, R = NORMS[phase] * TILES + t, rows(t)
                    pe.wait_ge(scaled_ready, m + 1)
                    if m >= 2:
                        pe.wait_ge(norm_out, m - 1)
                    for k in range(KC):
                        ins = pe.transpose(ps[:, 2 * (m % 2) + k // 4, (k % 4) * P:(k % 4) * P + R],
                                           scaled[0:R, m % 2, k * P:(k + 1) * P], ident[0:R, 0:R])
                    ins.then_inc(norm_turned, 1)
                phase_over(pe, phase)

            def segment_tile(seg, t):
                i = ALL_SEGS.index(seg)
                n = i * TILES + t
                R, N = rows(t), SEG_W.get(seg, 512)
                if t == 0:
                    pe.wait_ge(w_loaded[i % 2], 16 * (i // 2 + 1))
                if n >= 3:
                    s3, t3 = ALL_SEGS[(n - 3) // TILES], (n - 3) % TILES
                    pe.wait_ge(emptied_dve if s3 in DVE_EVACUATES else emptied_act, evac_count(s3, t3))
                src = pT if seg[:2] == "pe" else xT
                kc = PLE // P if seg[:2] == "pe" else KC
                for k in range(kc):
                    ins = pe.matmul(ps[0:R, n % 3, 0:N], src[:, k, t * P:t * P + R],
                                    W[i % 2][:, k, 0:N], start=(k == 0), stop=(k == kc - 1))
                ins.then_inc(proj_ready, 1)

            def turn_tile(seg, t):
                m, R = turn_index(seg, t), rows(t)
                if seg[0] == "s":
                    pe.wait_ge(emptied_act, evac_count(seg, t))
                else:
                    pe.wait_ge(nat_ready, nat_count(seg, t))
                if m >= 2:
                    pe.wait_ge(turned_out, m - 1)
                bank = 3 + 2 * (m % 2)
                if seg[0] == "f":
                    for h in range(HA):
                        ins = pe.transpose(ps[0:HD + 1, bank + h // 4, (h % 4) * P:(h % 4) * P + R],
                                           aug[0:R, m % 2, h, :], ident[0:R, 0:R])
                else:
                    for c in range(QP):
                        w = min(P, SEG_W[seg] - c * P)
                        ins = pe.transpose(ps[0:w, bank, c * P:c * P + R],
                                           nat[0:R, m % 2, c * P:c * P + w], ident[0:R, 0:R])
                ins.then_inc(turned, 1)

            def project(phase):
                for seg in PROJ_SEGS[phase]:
                    for t in range(TILES):
                        segment_tile(seg, t)
                        if t >= 1 and t - 1 < TURNED.get(seg, 0):
                            turn_tile(seg, t - 1)
                    if TURNED.get(seg, 0) == TILES:
                        turn_tile(seg, TILES - 1)
                    if seg == "fg":
                        pe.wait_ge(logf_ready, 1)
                        padded = logf_padded.rearrange("p t h -> p (t h)")
                        lf = padded[:, (NT - 1) * HA:]
                        out = ps[:, 7, 0:NT * HA]
                        pe.matmul(out, const("neg_upto"), lf[:, 0:NT * HA], start=True, stop=False)
                        for d in range(1, NT):
                            pe.matmul(out, const("negones"),
                                      padded[:, (NT - 1 - d) * HA:(2 * NT - 1 - d) * HA],
                                      start=False, stop=(d == NT - 1))
                        pe.matmul(ps[0:ROWS, 7, 64:64 + HA], const("neg_upto_new")[0:ROWS],
                                  lf[0:ROWS, NT * HA:], start=True, stop=True).then_inc(cum_ready, 1)
                phase_over(pe, phase)

            def retention():
                units = [(t, h) for t in range(TILES) for h in range(HR)]

                def at(h):
                    return h // 2, slice((h % 2) * HD, (h % 2) * HD + HD)

                def scores(u):
                    t, h = units[u]
                    pr, q = at(h)
                    R = rows(t)
                    if u >= 2:
                        pe.wait_ge(masked_r, u - 1)
                    pe.matmul(ps[0:R, u % 2, 0:R], kT_r[q, pr, t * P:t * P + R],
                              qT_r[q, pr, t * P:t * P + R], start=True, stop=True).then_inc(scores_r, 1)

                scores(0)
                for u, (t, h) in enumerate(units):
                    pr, q = at(h)
                    R = rows(t)
                    if u + 1 < len(units):
                        scores(u + 1)
                    pe.wait_ge(masked_r, u + 1)
                    if h == 0 and t >= 2:
                        pe.wait_ge(ret_emptied, t - 1)
                    with_state = 0 < t < SAMPLE
                    bank, c = (2, h) if t == SAMPLE else (2 + t % 2 + 4 * (h % 2), h // 2)
                    out = ps[0:R, bank, c * HD:(c + 1) * HD]
                    ins = pe.matmul(out, masked[0:R, u % 2, 0:R], v_r[0:R, t, h * HD:(h + 1) * HD],
                                    start=True, stop=not with_state)
                    if with_state:
                        if h == 0:
                            pe.wait_ge(state_r, t)
                        ins = pe.matmul(out, qT_r[q, pr, t * P:t * P + R], state[q, pr, :],
                                        start=False, stop=True)
                    ins.then_inc(inner_r, 1)
                    if h == HR - 1 and t < SAMPLE:
                        if t >= 2:
                            pe.wait_ge(state_r, t - 1)
                        for c in range(QP):
                            ins = pe.matmul(ps[:, 4 + t % 2, c * P:(c + 1) * P],
                                            kd_r[:, t, c * P:(c + 1) * P], v_r[:, t, c * P:(c + 1) * P],
                                            start=True, stop=True)
                        ins.then_inc(kv_r, 1)
                pe.wait_ge(state_in, 16 * QP)
                for h in range(HR):
                    pr, q = at(h)
                    if h >= 2:
                        pe.wait_ge(cross_emptied, h - 1)
                    pe.matmul(ps[0:ROWS, 6 + h % 2, :], qT_r[q, pr, SEQ:TR],
                              s0[q, pr].rearrange("p b e -> p (b e)"), start=True, stop=True)\
                        .then_inc(cross_ready, 1)
                for h in range(HR):
                    pr, q = at(h)
                    pe.wait_ge(v_seq_ready, h + 1)
                    if h >= 2:
                        pe.wait_ge(new_state_out, h - 1)
                    if h < 2:
                        pe.wait_ge(state_r, NT)
                    pe.matmul(ps[q, 4 + h % 2, :], kd_r[0:ROWS, SAMPLE, h * HD:(h + 1) * HD],
                              v_seq[0:ROWS, h % 2, :], start=True, stop=True,
                              tile_position=(0, q.start)).then_inc(new_state_ready, 1)
                phase_over(pe, RET)

            def attention(phase):
                kind = KIND[phase]
                qT, kT, v = (qT_s, kT_s, v_s) if kind == "sb" else (qT_f, kT_f, v_f)

                def scores(u):
                    t, h = UNITS[u]
                    n = (t + 1) * P
                    q = slice((h % 2) * HD, (h % 2) * HD + HD) if kind == "sb" else slice(0, HD + 1)
                    a = h // 2 if kind == "sb" else h
                    if u >= 2:
                        pe.wait_ge(att_first[kind], u - 1)
                    for c in range(0, n, 512):
                        w = min(512, n - c)
                        ins = pe.matmul(ps[:, 2 * (u % 2) + c // 512, 0:w], qT[q, a, t * P:(t + 1) * P],
                                        kT[q, a, c:c + w], start=True, stop=True)
                    ins.then_inc(att_scores[kind], 1)

                def turn(u):
                    t, h = UNITS[u]
                    pe.wait_ge(att_probs[kind] if kind == "sb" else att_first[kind], u + 1)
                    if u >= 1:
                        pe.wait_ge(attT_ready[kind], u)
                    src = att if kind == "sb" else expd
                    for j in range(t + 1):
                        ins = pe.transpose(ps[:, 4 + j // 4, (j % 4) * P:(j % 4 + 1) * P],
                                           src[:, u % 2, j * P:(j + 1) * P], ident)
                    ins.then_inc(att_turned[kind], 1)

                def weigh(u):
                    t, h = UNITS[u]
                    pe.wait_ge(attT_ready[kind], u + 1)
                    if h == 0 and t >= 2:
                        pe.wait_ge(att_done[kind], t - 1)
                    for j in range(t + 1):
                        ins = pe.matmul(ps[:, 6 + t % 2, h * HD:(h + 1) * HD],
                                        attT[:, u % 2, j * P:(j + 1) * P], v[:, j, h * HD:(h + 1) * HD],
                                        start=(j == 0), stop=(j == t))
                    ins.then_inc(att_out[kind], 1)

                scores(0)
                for u in range(len(UNITS)):
                    if u + 1 < len(UNITS):
                        scores(u + 1)
                    if u >= 1:
                        weigh(u - 1)
                    turn(u)
                weigh(len(UNITS) - 1)
                phase_over(pe, phase)

            def forget_sums():
                for half in range(2):
                    pe.wait_ge(page_ready, half + 1)
                    pe.matmul(ps[:, 6 + half, 0:HA], const("later_page"), page_sum[:, half, :, 0],
                              start=True, stop=True).then_inc(page_carry, 1)
                for h in range(HA):
                    pe.wait_ge(forget_part, 2)
                    if h >= 2:
                        pe.wait_ge(forget_ready, h - 1)
                    for half in range(2):
                        ins = pe.transpose(ps[:, h % 2, half * P:(half + 1) * P], page_sum[:, half, h, :],
                                           ident)
                    ins.then_inc(forget_turned, 1)
                pe.wait_ge(forget_ready, HA)

            def decode(phase):
                kind = KIND[phase]
                s = dec[kind]
                if kind == "fox":
                    forget_sums()
                for c, at in enumerate((0, 2 * HD, 4 * HD, HD, 3 * HD)):
                    pe.transpose(ps[:, 0, c * ROWS:(c + 1) * ROWS], q_new[:, at:at + P], ident[0:ROWS, 0:ROWS])
                for c in range(3):
                    w = min(P, DA - c * P)
                    ins = pe.transpose(ps[0:w, 1, c * ROWS:(c + 1) * ROWS], k_new[:, c * P:c * P + w],
                                       ident[0:ROWS, 0:ROWS])
                ins.then_inc(s["new_turned"], 1)
                pe.sem_inc(s["v_used"], 2)
                pe.wait_ge(s["new_ready"], 1)

                def turn_block(b, n):
                    g, kk = n // 5, n % 5
                    if kk == 0:
                        pe.wait_ge(s[f"k{g % 2}"], PG8 * 16 * (b * 2 + g // 2 + 1))
                    if not (isinstance(b, int) and b * 20 + n < 2):
                        pe.wait_ge(s["kt_act"] if n % 2 == 0 else s["kt_dve"], b * 10 + n // 2)
                    for j in range(4):
                        at = (4 * kk + j) * P
                        ins = pe.transpose(ps[:, n % 2, j * P:(j + 1) * P], ringK[:, g % 2, at:at + P], ident)
                    ins.then_inc(s["kt_ready"], 1)

                def score_block(b, n):
                    pe.wait_ge(s["kt_act"] if n % 2 == 0 else s["kt_dve"], b * 10 + n // 2 + 1)
                    if n == 0 and not (isinstance(b, int) and b == 0):
                        pe.wait_ge(s["z_emptied"], b)
                    for j in range(4):
                        c = 4 * n + j
                        bank, col = 2 + c * 2 * NEW // 512, c * 2 * NEW % 512
                        ins = pe.matmul(ps[:, bank, col:col + 2 * NEW], kT_d[:, n % 4, j * P:(j + 1) * P],
                                        qd[:, b, c % 5, :], start=True, stop=True)
                    ins.then_inc(s["scores_done"], 1)

                def scores(b):
                    for n in range(22):
                        if n < 20:
                            turn_block(b, n)
                        if n >= 2:
                            score_block(b, n - 2)
                    z_new = flat3()[0:ROWS, PAGES * HI:PAGES * HI + HI]
                    pe.matmul(z_new[:, 0:16], kT_new[:, 0, :], qd[:, b, 0, :], start=True, stop=True)
                    pe.matmul(z_new[:, 16:32], kT_new[:, 1, :], qd[:, b, 1, :], start=True, stop=True)
                    pe.matmul(z_new[:, 32:40], kT_new[:, 2, :], qd[:, b, 2, 0:NEW], start=True,
                              stop=True).then_inc(s["z_ready"], 1)

                def fold(b):
                    if kind == "sb":
                        pe.wait_ge(s["sum_ready"], b + 1)
                        for c in range(3):
                            cols = slice(c * 440, c * 440 + 440)
                            pe.matmul(ps[:, 2 + c, 0:440], const("earlier"), soft[:, cols], start=True, stop=False)
                            ins = pe.matmul(ps[:, 2 + c, 0:440], const("negones"), later[:, cols], start=False,
                                            stop=True)
                        ins.then_inc(s["expo_ready"], 1)
                    else:
                        pe.wait_ge(s["soft_in"], b + 1)
                        pe.transpose(ps[:, 6, 0:P], row_max[:], ident).then_inc(s["fold_ready"], 1)
                        pe.wait_ge(s["fold_out"], b + 1)
                        pe.matmul(ps[:, 6, P:P + HI], ones[0:HI, :], small[0:HI, 120:120 + HI], start=True,
                                  stop=True).then_inc(s["bias_ready"], 1)

                def weigh(b):
                    pe.wait_ge(s["probs_ready"], b + 1)
                    pe.wait_ge(s["o_emptied"], b + 1)
                    pr = probs.rearrange("p (h i s) -> p h i s", h=HA, i=NEW)

                    def out(h):
                        q = 32 * (h % 4)
                        return ps[q:q + NEW, 5, (h // 4) * HD:(h // 4 + 1) * HD]

                    for g in range(GROUPS):
                        pe.wait_ge(s[f"v{g % 2}"], PG8 * 16 * (b * 2 + g // 2 + 1))
                        for p in range(PG8):
                            for h in range(HA):
                                c = p * DA + h * HD
                                ins = pe.matmul(out(h), pr[:, h, :, g * PG8 + p], ringV[:, g % 2, c:c + HD],
                                                start=(g == 0 and p == 0), stop=False,
                                                tile_position=(0, 32 * (h % 4)), skip_group_check=True)
                        ins.then_inc(s["v_used"], 1)
                    for h in range(HA):
                        ins = pe.matmul(out(h), pr[0:ROWS, h, :, PAGES], v_new[:, h * HD:(h + 1) * HD],
                                        start=False, stop=True, tile_position=(0, 32 * (h % 4)),
                                        skip_group_check=True)
                    if kind == "fox":
                        pe.wait_ge(s["den_ready"], b + 1)
                        for h in range(HA):
                            q = 32 * (h % 4)
                            ins = pe.matmul(ps[q:q + NEW, 5, P + h // 4:P + h // 4 + 1],
                                            small[:, 40 + h * NEW:40 + (h + 1) * NEW], ones[:, 0:1],
                                            start=True, stop=True, tile_position=(0, q),
                                            skip_group_check=True)
                    ins.then_inc(s["pv_done"], 1)

                scores(0)
                fold(0)
                with pe.Fori(1, SEQS) as b:
                    scores(b)
                    weigh(b - 1)
                    fold(b)
                weigh(SEQS - 1)
                phase_over(pe, phase)

            with pe.Fori(0, DEPTH) as L:
                norm(NORM1)
                project(PROJ_R)
                retention()
                project(PROJ_S)
                attention(ATT_S)
                decode(DEC_S)
                project(PROJ_F)
                attention(ATT_F)
                decode(DEC_F)
                for t in range(TILES):
                    R = rows(t)
                    if t >= 2:
                        pe.wait_ge(mixed_out, t - 1)
                    for k in range(KC):
                        ins = pe.transpose(ps[:, 2 * (t % 2) + k // 4, (k % 4) * P:(k % 4) * P + R],
                                           O[0:R, t, k * P:(k + 1) * P], ident[0:R, 0:R])
                    ins.then_inc(mixed_turned, 1)
                phase_over(pe, MIXED)
                project(OUT)
                norm(NORM2)
                pe.wait_ge(p_in, 32)
                for t in range(TILES):
                    R = rows(t)
                    if t >= 2:
                        pe.wait_ge(p_out, t - 1)
                    for k in range(2):
                        ins = pe.transpose(ps[:, 3 + t % 2, k * P:k * P + R],
                                           p_nat[0:R, t, k * P:(k + 1) * P], ident[0:R, 0:R])
                    ins.then_inc(p_turned, 1)
                phase_over(pe, PLE_T)
                project(GATED)
                layer_over(pe, L)

        @block.scalar
        def _(act):
            act.wait_ge(consts_in, 32)
            act.wait_ge(set_up, 3)
            act.wait_ge(x_in, 32)

            def norm(phase):
                for t in range(TILES):
                    m, R = NORMS[phase] * TILES + t, rows(t)
                    act.activation(junk[0:R], O[0:R, t, :], ACT.Square, accum_out=small[0:R, 200 + t:201 + t])\
                        .then_inc(squared, 1)
                    act.wait_ge(squared, m + 1)
                    act.activation(small[0:R, 210 + t:211 + t], small[0:R, 200 + t:201 + t], ACT.Sqrt,
                                   bias=eps[0:R], scale=1.0 / D).then_inc(rooted, 1)
                phase_over(act, phase)

            def turned_to(seg, t):
                m, R = turn_index(seg, t), rows(t)
                act.wait_ge(turned, m + 1)
                bank = 3 + 2 * (m % 2)
                if seg[0] == "f":
                    dst = qT_f if seg == "fq" else kT_f
                    ins = act.activation(
                        dst[0:HD + 1, :, t * P:(t + 1) * P],
                        bank2(bank, HA * P)[0:HD + 1].rearrange("p (h n) -> p h n", h=HA), ACT.Copy)
                elif seg[0] == "r":
                    dst = qT_r if seg == "rq" else kT_r
                    ins = act.activation(
                        dst[:, :, t * P:t * P + R],
                        ps[:, bank, 0:QP * P].rearrange("p (c n) -> p c n", c=QP)[:, :, 0:R], ACT.Copy)
                else:
                    dst = qT_s if seg == "sq" else kT_s
                    src = ps[:, bank, 0:QP * P].rearrange("p (c n) -> p c n", c=QP)
                    act.activation(dst[:, 0:2, t * P:(t + 1) * P], src[:, 0:2], ACT.Copy)
                    ins = act.activation(dst[0:HD, 2, t * P:(t + 1) * P], src[0:HD, 2], ACT.Copy)
                ins.then_inc(turned_out, 1)

            def project(phase, L):
                for seg in PROJ_SEGS[phase]:
                    i = ALL_SEGS.index(seg)
                    for t in range(TILES):
                        n, R, N = i * TILES + t, rows(t), SEG_W.get(seg, 512)
                        src = ps[0:R, n % 3, 0:N]
                        if seg in GATE_AT:
                            act.wait_ge(proj_ready, n + 1)
                            w = DR if seg == "rg" else DA
                            act.activation(O[0:R, t, GATE_AT[seg]:GATE_AT[seg] + w], src[:, 0:w], ACT.Sigmoid)\
                                .then_inc(sigmoid_ready, 1)
                        elif seg in ("rv", "sv", "fv"):
                            act.wait_ge(proj_ready, n + 1)
                            dst = v_r[0:R, t] if seg == "rv" else v_new[:] if t == SAMPLE else \
                                (v_s if seg == "sv" else v_f)[:, t]
                            act.activation(dst, src, ACT.Copy).then_inc(emptied_act, 1)
                        elif seg in ("sq", "sk"):
                            act.wait_ge(proj_ready, n + 1)
                            m = turn_index(seg, t)
                            scale = HD ** -0.5 if seg == "sq" else 1.0
                            if t == SAMPLE:
                                dst = q_new[:, 0:DA] if seg == "sq" else k_new[:]
                                if seg == "sq":
                                    act.activation(q_new[:, DA:DA + HD], src[:, 0:HD], ACT.Copy, scale=scale)
                            else:
                                dst = nat[:, m % 2, 0:DA]
                                act.wait_ge(turned, m - 1)
                                if seg == "sk" and t >= 2:
                                    act.wait_ge(k_saved[t % 2], L * 16 * (10, 8)[t % 2] + 16 * (t // 2))
                            act.activation(dst, src, ACT.Copy, scale=scale).then_inc(emptied_act, 1)
                        elif seg in ("fq", "fk"):
                            act.wait_ge(proj_ready, n + 1)
                            m = turn_index(seg, t)
                            if not (seg == "fq" and t < 2) and t < SAMPLE:
                                act.wait_ge(turned, m - 1)
                            if t == SAMPLE:
                                act.wait_ge(turned, m - 1)
                            if seg == "fk":
                                if t == 0:
                                    act.wait_ge(nat_ready, nat_count("fq", SAMPLE))
                                if t >= 2:
                                    act.wait_ge(k_saved[t % 2], L * 16 * (10, 8)[t % 2] + 16 * ((5, 4)[t % 2] + t // 2))
                            act.activation(aug[0:R, m % 2, :, 0:HD], src.rearrange("p (h d) -> p h d", h=HA),
                                           ACT.Copy).then_inc(emptied_act, 1)
                            u = (0 if seg == "fq" else TILES) + t
                            act.wait_ge(head_sums, u + 1)
                            act.activation(small[0:R, 10:15], small[0:R, 5:10], ACT.Sqrt, bias=eps[0:R],
                                           scale=1.0 / HD).then_inc(head_roots, 1)
                        elif seg[:2] == "pg":
                            act.wait_ge(proj_ready, n + 1)
                            if seg == "pg1":
                                act.wait_ge(emptied_dve, evac_count("pe0", t))
                            act.activation(gate[0:R, t, :], src, ACT.Sigmoid).then_inc(emptied_act, 1)
                        if t >= 1 and t - 1 < TURNED.get(seg, 0):
                            turned_to(seg, t - 1)
                    if TURNED.get(seg, 0) == TILES:
                        turned_to(seg, TILES - 1)
                    if seg == "fg":
                        act.wait_ge(logit_ready, 1)
                        act.activation(ltmp, ltmp, ACT.Exp).then_inc(logf_act, 1)
                        act.wait_ge(logf_act, 1)
                        act.activation(ltmp, ltmp, ACT.Ln, bias=1.0).then_inc(logf_act, 1)
                phase_over(act, phase)

            def retention():
                for t in range(TILES):
                    R = rows(t)
                    act.wait_ge(centred_r, t + 1)
                    act.activation(ret_sq[0:R], ret_o[0:R], ACT.Square).then_inc(squares_r, 1)
                    act.wait_ge(sums_r, t + 1)
                    act.activation(small[0:R, 20:26], small[0:R, 30:36], ACT.Sqrt, bias=eps[0:R],
                                   scale=1.0 / HD).then_inc(roots_r, 1)
                phase_over(act, RET)

            def attention(phase):
                kind = KIND[phase]

                def first(u):
                    t, h = UNITS[u]
                    n = (t + 1) * P
                    if kind == "sb":
                        act.wait_ge(att_scores[kind], u + 1)
                        if u >= 2:
                            act.wait_ge(att_probs[kind], u - 1)
                        act.activation(sig[:, u % 2, 0:n], bank2(2 * (u % 2), n), ACT.Sigmoid)\
                            .then_inc(att_first[kind], 1)
                    else:
                        act.wait_ge(att_max, u + 1)
                        if u >= 2:
                            act.wait_ge(att_turned[kind], u - 1)
                        if h == 0 and t >= 2:
                            act.wait_ge(att_done[kind], t - 1)
                        act.activation(expd[:, u % 2, 0:n], bank2(2 * (u % 2), n), ACT.Exp,
                                       bias=small[:, 40 + u % 4:41 + u % 4],
                                       accum_out=small[:, 50 + (t % 2) * HA + h:51 + (t % 2) * HA + h])\
                            .then_inc(att_first[kind], 1)

                def to_sbuf(u):
                    t, h = UNITS[u]
                    act.wait_ge(att_turned[kind], u + 1)
                    if u >= 2:
                        act.wait_ge(att_out[kind], u - 1)
                    n = (t + 1) * P
                    act.activation(attT[:, u % 2, 0:n], bank2(4, n), ACT.Copy).then_inc(attT_ready[kind], 1)

                first(0)
                for u in range(len(UNITS)):
                    if u + 1 < len(UNITS):
                        first(u + 1)
                    to_sbuf(u)
                phase_over(act, phase)

            def decode(phase):
                kind = KIND[phase]
                s = dec[kind]

                def blocks(b):
                    for n in range(0, 20, 2):
                        act.wait_ge(s["kt_ready"], b * 20 + n + 1)
                        if not (isinstance(b, int) and b * 20 + n < 4):
                            act.wait_ge(s["scores_done"], b * 20 + n - 3)
                        act.activation(kT_d[:, n % 4, :], ps[:, n % 2, :], ACT.Copy).then_inc(s["kt_act"], 1)

                def soften(b):
                    if kind == "sb":
                        act.wait_ge(s["soft_in"], b + 1)
                        act.activation(soft, soft, ACT.Exp).then_inc(s["soft_act"], 1)
                        act.wait_ge(s["soft_act"], b * 2 + 1)
                        act.activation(soft, soft, ACT.Ln, bias=1.0).then_inc(s["soft_act"], 1)

                def exponentiate(b):
                    act.wait_ge(s["soft_ready"], b + 1)
                    act.wait_ge(s["pv_done"], b)
                    act.activation(probs, zs, ACT.Exp).then_inc(s["probs_ready"], 1)

                blocks(0)
                soften(0)
                exponentiate(0)
                with act.Fori(1, SEQS) as b:
                    blocks(b)
                    soften(b)
                    exponentiate(b)
                phase_over(act, phase)

            with act.Fori(0, DEPTH) as L:
                norm(NORM1)
                project(PROJ_R, L)
                retention()
                project(PROJ_S, L)
                attention(ATT_S)
                decode(DEC_S)
                project(PROJ_F, L)
                attention(ATT_F)
                decode(DEC_F)
                for t in range(1, TILES, 2):
                    R = rows(t)
                    act.wait_ge(mixed_turned, t + 1)
                    act.wait_ge(mixed_out, t)
                    act.activation(xT[:, :, t * P:t * P + R],
                                   bank2(2 * (t % 2)).rearrange("p (k n) -> p k n", k=KC)[:, :, 0:R],
                                   ACT.Copy).then_inc(mixed_out, 1)
                phase_over(act, MIXED)
                project(OUT, L)
                norm(NORM2)
                for t in range(TILES):
                    R = rows(t)
                    act.wait_ge(p_turned, t + 1)
                    act.activation(pT[:, :, t * P:t * P + R],
                                   ps[:, 3 + t % 2, 0:2 * P].rearrange("p (k n) -> p k n", k=2)[:, :, 0:R],
                                   ACT.Copy).then_inc(p_out, 1)
                phase_over(act, PLE_T)
                project(GATED, L)
                layer_over(act, L)

        @block.vector
        def _(dve):
            dve.wait_ge(consts_in, 32)
            dve.wait_ge(set_up, 3)
            dve.wait_ge(x_in, 32)
            link = Steps(dve, steps_sem)

            def bc(ap, shape):
                return ap.unsqueeze(len(shape) - 1).broadcast_to(shape)

            def norm(phase):
                def scale(t):
                    m, R = NORMS[phase] * TILES + t, rows(t)
                    dve.wait_ge(rooted, m + 1)
                    link(dve.reciprocal(small[0:R, 220 + t:221 + t], small[0:R, 210 + t:211 + t]))
                    if m >= 2:
                        dve.wait_ge(norm_turned, m - 1)
                    dve.tensor_scalar(scaled[0:R, m % 2, :], O[0:R, t, :], small[0:R, 220 + t:221 + t], None,
                                      ALU.mult).then_inc(scaled_ready, 1)

                def out(t):
                    m, R = NORMS[phase] * TILES + t, rows(t)
                    dve.wait_ge(norm_turned, m + 1)
                    dve.tensor_tensor(xT[:, :, t * P:t * P + R],
                                      bank2(2 * (m % 2)).rearrange("p (k n) -> p k n", k=KC)[:, :, 0:R],
                                      bc(gT[:, NORMS[phase], :], [P, KC, R]), ALU.mult).then_inc(norm_out, 1)

                for t in range(TILES):
                    scale(t)
                    if t >= 1:
                        out(t - 1)
                out(SAMPLE)
                phase_over(dve, phase)

            def project(phase):
                for seg in PROJ_SEGS[phase]:
                    i = ALL_SEGS.index(seg)
                    if seg == "fg":
                        link(dve.memset(logit, 0.0))
                        link(dve.memset(logf_padded[:, 0:NT - 1], 0.0))
                    for t in range(TILES):
                        n, R = i * TILES + t, rows(t)
                        src = ps[0:R, n % 3, :]
                        if seg in ("rq", "rk"):
                            m = turn_index(seg, t)
                            new = t == SAMPLE
                            xh = src[:, 0:DR].rearrange("p (h c d) -> p h c d", h=HR, c=2)
                            ra = rot_a[0:R].rearrange("p (h d) -> p h d", h=HR)
                            rb = rot_b[0:R].rearrange("p (h c d) -> p h c d", h=HR, c=2)
                            cosb = cos_t[0:R, t, :].unsqueeze(1).broadcast_to([R, HR, HD])
                            dve.wait_ge(proj_ready, n + 1)
                            link(dve.tensor_tensor(ra, src[:, 0:DR].rearrange("p (h d) -> p h d", h=HR), cosb,
                                                   ALU.mult))
                            sinb = sin_t[0:R, t, :].rearrange("p (c d) -> p c d", c=2)
                            for c in range(2):
                                ins = dve.tensor_tensor(rb[:, :, c, :], xh[:, :, 1 - c, :],
                                                        sinb[:, c, :].unsqueeze(1).broadcast_to([R, HR, HD // 2]),
                                                        ALU.mult)
                                ins.then_inc(*((emptied_dve, 1) if c else (steps_sem, 1)))
                            link.n += 1
                            dve.wait_ge(steps_sem, link.base + link.n)
                            dve.wait_ge(emptied_dve, evac_count(seg, t))
                            if m >= 2:
                                dve.wait_ge(turned, m - 1)
                            dve.tensor_tensor(nat[0:R, m % 2, :], rot_a[0:R], rot_b[0:R], ALU.add)\
                                .then_inc(nat_ready, 1)
                            dve.wait_ge(nat_ready, nat_count(seg, t))
                            if seg == "rk":
                                decay = const("key_decay_new" if new else "key_decay")
                                link(dve.tensor_tensor(
                                    kd_r[0:R, t].rearrange("p (h d) -> p h d", h=HR),
                                    nat[0:R, m % 2, :].rearrange("p (h d) -> p h d", h=HR),
                                    bc(decay[0:R], [R, HR, HD]), ALU.mult))
                        elif seg in GATE_AT:
                            w = DR if seg == "rg" else DA
                            gates = {"rg": 0, "sg": 1, "fg": 2}[seg]
                            dve.wait_ge(proj_ready, n + 1)
                            dve.wait_ge(sigmoid_ready, gates * TILES + t + 1)
                            if seg == "fg":
                                link(dve.tensor_tensor(logit[0:R, t, :], src[:, DA:DA + HA], b_f_b[0:R], ALU.add))
                            out = O[0:R, t, GATE_AT[seg]:GATE_AT[seg] + w]
                            dve.tensor_tensor(out, out, src[:, 0:w], ALU.mult).then_inc(emptied_dve, 1)
                        elif seg in ("fq", "fk"):
                            m = turn_index(seg, t)
                            dve.wait_ge(emptied_act, evac_count(seg, t))
                            x = aug[0:R, m % 2, :, 0:HD]
                            link(dve.tensor_tensor(squares[0:R], x, x, ALU.mult))
                            dve.tensor_reduce(small[0:R, 5:10], squares[0:R], AX, ALU.add).then_inc(head_sums, 1)
                            last = aug[0:R, m % 2, :, HD:HD + 1]
                            if seg == "fq":
                                link(dve.memset(last, 1.0))
                            else:
                                link(dve.tensor_copy(last, neg_c[0:R, t, :].unsqueeze(2)))
                            u = (0 if seg == "fq" else TILES) + t
                            dve.wait_ge(head_roots, u + 1)
                            link(dve.reciprocal(small[0:R, 15:20], small[0:R, 10:15]))
                            link(dve.tensor_tensor(x, x, bc(small[0:R, 15:20], [R, HA, HD]), ALU.mult))
                            g = (g_fq_b if seg == "fq" else g_fk_b)[0:R].unsqueeze(1).broadcast_to([R, HA, HD])
                            if t < SAMPLE:
                                dst = x
                            else:
                                dst = (q_new[:, 0:DA] if seg == "fq" else k_new[:]).rearrange("p (h d) -> p h d", h=HA)
                            if t == SAMPLE and seg == "fq":
                                link(dve.tensor_tensor(q_new[:, DA:DA + HD], x[:, 0, :], g_fq_b[0:R], ALU.mult))
                            dve.tensor_tensor(dst, x, g, ALU.mult).then_inc(nat_ready, 1)
                            dve.wait_ge(nat_ready, nat_count(seg, t))
                        elif seg[:3] == "out":
                            m = (i - ALL_SEGS.index("out0")) * TILES + t
                            c = int(seg[-1])
                            dve.wait_ge(proj_ready, n + 1)
                            dve.wait_ge(x_half_in[m % 2], 16 * (m // 2 + 1))
                            dve.tensor_tensor(O[0:R, t, c * 512:(c + 1) * 512], src, x_half[0:R, m % 2, :], ALU.add)\
                                .then_inc(emptied_dve, 1)
                        elif seg[:2] == "pe":
                            c = int(seg[-1])
                            dve.wait_ge(proj_ready, n + 1)
                            dve.wait_ge(emptied_act, evac_count("pg" + seg[-1], t))
                            dve.tensor_tensor(gated[0:R, t % 2, :], src, gate[0:R, t, :], ALU.mult)\
                                .then_inc(emptied_dve, 1)
                            dve.wait_ge(emptied_dve, evac_count(seg, t))
                            out = O[0:R, t, c * 512:(c + 1) * 512]
                            link(dve.tensor_tensor(out, out, gated[0:R, t % 2, :], ALU.add))
                    if seg == "fg":
                        dve.scalar_tensor_tensor(ltmp, logit, -1.0, logit, ALU.mult, ALU.min).then_inc(logit_ready, 1)
                        dve.wait_ge(logf_act, 2)
                        dve.scalar_tensor_tensor(logf, logit, 0.0, ltmp, ALU.min, ALU.subtract)\
                            .then_inc(logf_ready, 1)
                        dve.wait_ge(cum_ready, 1)
                        link(dve.tensor_copy(neg_c[:, 0:NT, :], ps[:, 7, 0:NT * HA].rearrange(
                            "p (t h) -> p t h", h=HA)))
                        link(dve.tensor_copy(neg_c[0:ROWS, SAMPLE, :], ps[0:ROWS, 7, 64:64 + HA]))
                phase_over(dve, phase)

            def retention():
                def mask(t, h):
                    u, R, new = t * HR + h, rows(t), t == SAMPLE
                    dve.wait_ge(scores_r, u + 1)
                    if u >= 2:
                        dve.wait_ge(inner_r, u - 1)
                    grow = const("col_grow_new" if new else "col_grow")[0:R, h:h + 1]
                    upto = const("upto_new" if new else "upto")[0:R, 0:R]
                    dve.scalar_tensor_tensor(masked[0:R, u % 2, 0:R], ps[0:R, u % 2, 0:R], grow, upto, ALU.mult,
                                             ALU.mult).then_inc(masked_r, 1)

                def update(t):
                    dve.wait_ge(kv_r, t + 1)
                    kv = ps[:, 4 + t % 2, 0:QP * P].rearrange("p (c n) -> p c n", c=QP)
                    if t > 0:
                        dve.wait_ge(state_r, t)
                        link(dve.tensor_tensor(state, state, bc(const("chunk_decay"), [P, QP, HD]), ALU.mult))
                    for h2 in range(2):
                        q = slice(h2 * HD, (h2 + 1) * HD)
                        mine = kv[q, :, h2 * HD:(h2 + 1) * HD]
                        if t > 0:
                            ins = dve.tensor_tensor(state[q], state[q], mine, ALU.add)
                        else:
                            ins = dve.tensor_copy(state[q], mine)
                        if h2 == 0:
                            link(ins)
                    ins.then_inc(state_r, 1)

                def group_norm(t):
                    R, new = rows(t), t == SAMPLE
                    dve.wait_ge(inner_r, HR * (t + 1))
                    grow = const("row_grow_new" if new else "row_grow")
                    o = ret_o[0:R]
                    if new:
                        out = ps[0:R, 2, 0:DR].rearrange("p (h d) -> p h d", h=HR)
                        link(dve.tensor_tensor(o, out, ret_sq[0:R], ALU.add))
                        dve.tensor_tensor(o, o, bc(grow[0:R], [R, HR, HD]), ALU.mult).then_inc(ret_emptied, 1)
                    else:
                        for h2 in range(2):
                            out = ps[:, 2 + t % 2 + 4 * h2, 0:QP * HD].rearrange("p (c d) -> p c d", c=QP)
                            ins = dve.tensor_tensor(
                                o.rearrange("p (c a) d -> p c a d", a=2)[:, :, h2, :], out,
                                bc(grow.rearrange("p (c a) -> p c a", a=2)[:, :, h2], [P, QP, HD]), ALU.mult)
                            if h2 == 0:
                                link(ins)
                        ins.then_inc(ret_emptied, 1)
                    dve.wait_ge(ret_emptied, t + 1)
                    link(dve.tensor_reduce(small[0:R, 36:42], o, AX, ALU.add))
                    link(dve.tensor_scalar(small[0:R, 36:42], small[0:R, 36:42], 1.0 / HD, None, ALU.mult))
                    dve.tensor_tensor(o, o, bc(small[0:R, 36:42], [R, HR, HD]), ALU.subtract).then_inc(centred_r, 1)
                    dve.wait_ge(squares_r, t + 1)
                    dve.tensor_reduce(small[0:R, 30:36], ret_sq[0:R], AX, ALU.add).then_inc(sums_r, 1)
                    dve.wait_ge(roots_r, t + 1)
                    link(dve.reciprocal(small[0:R, 42:48], small[0:R, 20:26]))
                    link(dve.tensor_tensor(o, o, bc(small[0:R, 42:48], [R, HR, HD]), ALU.mult))
                    mixed = O[0:R, t, 0:DR]
                    link(dve.tensor_tensor(mixed, mixed, g_ret_b[0:R], ALU.mult))
                    link(dve.tensor_tensor(mixed, mixed, o.rearrange("p h d -> p (h d)"), ALU.mult))

                for t in range(NT):
                    for h in range(HR):
                        mask(t, h)
                    update(t)
                    group_norm(t)
                for h in range(HR):
                    mask(SAMPLE, h)
                own = const("own_seq")[0:ROWS]
                for h in range(HR):
                    dve.wait_ge(cross_ready, h + 1)
                    dve.tensor_tensor(cross[0:ROWS], ps[0:ROWS, 6 + h % 2, :].rearrange("p (b e) -> p b e", b=SEQS),
                                      bc(own, [ROWS, SEQS, HD]), ALU.mult).then_inc(cross_emptied, 1)
                    dve.wait_ge(cross_emptied, h + 1)
                    link(dve.tensor_reduce(ret_sq[0:ROWS, h, :], cross[0:ROWS].rearrange("p b e -> p e b"), AX,
                                           ALU.add))
                group_norm(SAMPLE)
                for h in range(HR):
                    pr, q = h // 2, slice((h % 2) * HD, (h % 2) * HD + HD)
                    if h >= 2:
                        dve.wait_ge(new_state_ready, h - 1)
                    dve.tensor_tensor(v_seq[0:ROWS, h % 2, :].rearrange("p (b e) -> p b e", b=SEQS),
                                      v_r[0:ROWS, SAMPLE, h * HD:(h + 1) * HD].unsqueeze(1).broadcast_to(
                                          [ROWS, SEQS, HD]),
                                      bc(own, [ROWS, SEQS, HD]), ALU.mult).then_inc(v_seq_ready, 1)
                    dve.wait_ge(new_state_ready, h + 1)
                    mine = s0[q, pr].rearrange("p b e -> p (b e)")
                    dve.scalar_tensor_tensor(mine, mine, const("chunk_decay_new")[q, pr:pr + 1],
                                             ps[q, 4 + h % 2, :], ALU.mult, ALU.add).then_inc(new_state_out, 1)
                phase_over(dve, RET)

            def attention(phase):
                kind = KIND[phase]
                if kind == "sb":
                    link(dve.memset(prod[:, SEQ:SEQ + 1], 1.0))

                def stick(u):
                    t, h = UNITS[u]
                    n = (t + 1) * P
                    s = sig[:, u % 2, 0:n]
                    r, e = rest[:, 0:n], SEQ - n
                    dve.wait_ge(att_first[kind], u + 1)
                    link(dve.tensor_tensor(s[:, t * P:n], s[:, t * P:n], const("before"), ALU.mult))
                    link(dve.tensor_scalar(r, s, -1.0, 1.0, ALU.mult, ALU.add))
                    dve.wait_ge(att_probs[kind], u)
                    link(dve.tensor_tensor_scan(prod[:, e:SEQ][:, ::-1], r[:, ::-1], r[:, ::-1], 1.0, ALU.mult,
                                                ALU.bypass))
                    if u >= 2:
                        dve.wait_ge(att_turned[kind], u - 1)
                    dve.tensor_tensor(att[:, u % 2, 0:n], s, prod[:, e + 1:SEQ + 1], ALU.mult)\
                        .then_inc(att_probs[kind], 1)

                def largest(u):
                    t, h = UNITS[u]
                    n = (t + 1) * P
                    dve.wait_ge(att_scores[kind], u + 1)
                    diag = bank2(2 * (u % 2), n)[:, t * P:n]
                    link(dve.tensor_tensor(diag, diag, const("after_neg"), ALU.add))
                    if u >= 4:
                        dve.wait_ge(att_first[kind], u - 3)
                    dve.tensor_reduce(small[:, 40 + u % 4:41 + u % 4], bank2(2 * (u % 2), n), AX, ALU.max,
                                      negate=True).then_inc(att_max, 1)

                def finish(t):
                    dve.wait_ge(att_out[kind], HA * (t + 1))
                    at = DR if kind == "sb" else DR + DA
                    out = O[:, t, at:at + DA]
                    o = ps[:, 6 + t % 2, 0:DA]
                    if kind == "fox":
                        link(dve.reciprocal(small[:, 60:65], small[:, 50 + (t % 2) * HA:50 + (t % 2 + 1) * HA]))
                        o3 = out.rearrange("p (h d) -> p h d", h=HA)
                        link(dve.tensor_tensor(o3, o3, bc(small[:, 60:65], [P, HA, HD]), ALU.mult))
                    dve.tensor_tensor(out, out, o, ALU.mult).then_inc(att_done[kind], 1)

                for u, (t, h) in enumerate(UNITS):
                    (stick if kind == "sb" else largest)(u)
                    if h == 2 and t >= 1:
                        finish(t - 1)
                finish(NT - 1)
                phase_over(dve, phase)

            def forget_sums(L):
                for half in range(2):
                    dve.wait_ge(logf_in, 16 * (L + 1))
                    for h in range(HA):
                        x = page_logf[:, half, :, h][:, ::-1]
                        ins = dve.tensor_tensor_scan(page_sum[:, half, h, :][:, ::-1], ones, x, 0.0, ALU.mult,
                                                     ALU.add)
                        if h < HA - 1:
                            link(ins)
                    ins.then_inc(page_ready, 1)
                    dve.wait_ge(page_ready, half + 1)
                    dve.wait_ge(page_carry, half + 1)
                    link(dve.tensor_tensor(page_sum[:, half], page_sum[:, half],
                                           page_logf[:, half].rearrange("p s h -> p h s"), ALU.subtract))
                    dve.tensor_tensor(page_sum[:, half], page_sum[:, half],
                                      bc(ps[:, 6 + half, 0:HA], [P, HA, P]), ALU.add).then_inc(forget_part, 1)
                for h in range(HA):
                    dve.wait_ge(forget_turned, h + 1)
                    dve.tensor_copy(forget[:, h, :], ps[:, h % 2, 0:2 * P]).then_inc(forget_ready, 1)

            def decode(phase, L):
                kind = KIND[phase]
                s = dec[kind]
                if kind == "fox":
                    forget_sums(L)
                link(dve.memset(qd, 0.0))
                link(dve.memset(kT_new, 0.0))
                link(dve.memset(row_max[:], 0.0))
                dve.memset(ps[:, 5, :], 1.0).then_inc(s["o_emptied"], 1)
                dve.wait_ge(s["o_emptied"], 1)
                zr = zs.rearrange("p (r s) -> p r s", s=SLOT)
                z4 = zs.rearrange("p (h i s) -> p h i s", h=HA, i=NEW)
                link(dve.memset(zr[ROWS:P, :, PAGES:SLOT], NEG))
                neg = const("new_neg_" + kind, SEQS, NEW)[0:ROWS]
                for h in range(HA):
                    link(dve.tensor_copy(new_bias[0:ROWS, :, h, :], neg))
                if kind == "fox":
                    for h in range(HA):
                        link(dve.tensor_scalar(new_bias[0:ROWS, :, h, :], new_bias[0:ROWS, :, h, :],
                                               neg_c[0:ROWS, SAMPLE, h:h + 1], None, ALU.add))
                dve.wait_ge(s["new_turned"], 1)
                qsrc = ps[:, 0, 0:5 * ROWS].rearrange("p (c b i) -> p b c i", c=5, b=SEQS)
                link(dve.tensor_copy(qd[0:HD, :, :, 0:NEW], qsrc[0:HD]))
                link(dve.tensor_copy(qd[HD:P, :, :, NEW:2 * NEW], qsrc[HD:P]))
                link(dve.tensor_copy(kT_new[:, 0:2, :], ps[:, 1, 0:2 * ROWS].rearrange("p (c n) -> p c n", c=2)))
                dve.tensor_copy(kT_new[0:HD, 2, :], ps[0:HD, 1, 2 * ROWS:3 * ROWS]).then_inc(s["new_ready"], 1)

                def blocks(b):
                    for n in range(1, 20, 2):
                        dve.wait_ge(s["kt_ready"], b * 20 + n + 1)
                        if not (isinstance(b, int) and b * 20 + n < 4):
                            dve.wait_ge(s["scores_done"], b * 20 + n - 3)
                        dve.tensor_copy(kT_d[:, n % 4, :], ps[:, n % 2, :]).then_inc(s["kt_dve"], 1)

                def soften(b):
                    zp = flat3()[:, 0:PAGES * HI]
                    zn = flat3()[0:ROWS, PAGES * HI:SLOT * HI]
                    dve.wait_ge(s["z_ready"], b + 1)
                    bias = new_bias[0:ROWS, b].rearrange("p h i -> p (h i)")
                    if kind == "sb":
                        link(dve.tensor_copy(zr[:, :, 0:PAGES], zp.rearrange("p (s r) -> p r s", r=HI)))
                        link(dve.tensor_tensor(zr[0:ROWS, :, PAGES], zn, bias, ALU.add))
                        dve.scalar_tensor_tensor(soft, zs, -1.0, zs, ALU.mult, ALU.min).then_inc(s["soft_in"], 1)
                        dve.wait_ge(s["soft_act"], 2 * b + 2)
                        link(dve.scalar_tensor_tensor(soft, zs, 0.0, soft, ALU.max, ALU.add))
                        dve.tensor_tensor_scan(later[:, ::-1], reset[:, ::-1], soft[:, ::-1], 0.0, ALU.mult,
                                               ALU.add).then_inc(s["sum_ready"], 1)
                        dve.wait_ge(s["expo_ready"], b + 1)
                        x3 = ps[:, 2:5, 0:440]
                        z3 = zs.rearrange("p (c n) -> p c n", c=3)
                        dve.tensor_tensor(z3, z3, x3, ALU.add).then_inc(s["soft_ready"], 1)
                        dve.wait_ge(s["soft_ready"], b + 1)
                        dve.sem_inc(s["z_emptied"], 1)
                    else:
                        fb = forget[:, :, bass.ds(b * PAGES, PAGES)].unsqueeze(2).broadcast_to(
                            [P, HA, NEW, PAGES])
                        z = zp.rearrange("p (s h i) -> p h i s", h=HA, i=NEW)
                        link(dve.tensor_tensor(z4[:, :, :, 0:PAGES], z, fb, ALU.add))
                        dve.tensor_tensor(zr[0:ROWS, :, PAGES], zn, bias, ALU.add).then_inc(s["z_emptied"], 1)
                        dve.wait_ge(s["z_emptied"], b + 1)
                        dve.tensor_reduce(row_max[:, 0:HI], zr, AX, ALU.max).then_inc(s["soft_in"], 1)
                        dve.wait_ge(s["fold_ready"], b + 1)
                        link(dve.tensor_reduce(small[0:HI, 180:181], ps[0:HI, 6, 0:P], AX, ALU.max, negate=True))
                        dve.tensor_scalar(small[0:HI, 120:120 + HI], ident[0:HI, 0:HI], small[0:HI, 180:181], None,
                                          ALU.mult).then_inc(s["fold_out"], 1)
                        dve.wait_ge(s["bias_ready"], b + 1)
                        dve.tensor_tensor(zr, zr, bc(ps[:, 6, P:P + HI], [P, HI, SLOT]), ALU.add)\
                            .then_inc(s["soft_ready"], 1)

                def denominators(b):
                    dve.wait_ge(s["probs_ready"], b + 1)
                    if kind == "fox":
                        dve.tensor_reduce(small[:, 40:40 + HI], probs.rearrange("p (r s) -> p r s", s=SLOT), AX,
                                          ALU.add).then_inc(s["den_ready"], 1)

                def take(b):
                    dve.wait_ge(s["pv_done"], b + 1)
                    o = ps[:, 5, 0:P].rearrange("p (a d) -> p a d", a=2)
                    if kind == "sb":
                        dve.tensor_copy(decoded[:, b], o).then_inc(s["o_emptied"], 1)
                    else:
                        link(dve.reciprocal(small[:, 182:184], ps[:, 5, P:P + 2]))
                        dve.tensor_tensor(decoded[:, b], o, bc(small[:, 182:184], [P, 2, HD]), ALU.mult)\
                            .then_inc(s["o_emptied"], 1)

                blocks(0)
                soften(0)
                denominators(0)
                first = link.n - DECODE_STEPS[kind]
                with dve.Fori(1, SEQS) as b:
                    link.turn(b, DECODE_STEPS[kind], first)
                    blocks(b)
                    take(b - 1)
                    soften(b)
                    denominators(b)
                    assert link.n == DECODE_STEPS[kind], (kind, link.n)
                link.turn(SEQS, DECODE_STEPS[kind], first)
                take(SEQS - 1)
                link.base, link.n = 0, link.base + link.n
                dve.wait_ge(s["loaded"], 16)
                at = DR if kind == "sb" else DR + DA
                out = O[0:ROWS, SAMPLE, at:at + DA]
                link(dve.tensor_tensor(out, out, work[0:ROWS, 0:DA], ALU.mult))
                phase_over(dve, phase)

            with dve.Fori(0, DEPTH) as L:
                link.base, link.n = 0, 0
                dve.wait_ge(vec_loaded, 6 * 16)
                link(dve.tensor_scalar(g_fq_b[:], g_fq_b[:], HD ** -0.5, None, ALU.mult))
                norm(NORM1)
                project(PROJ_R)
                retention()
                project(PROJ_S)
                attention(ATT_S)
                decode(DEC_S, L)
                project(PROJ_F)
                attention(ATT_F)
                decode(DEC_F, L)
                for t in range(0, TILES, 2):
                    R = rows(t)
                    dve.wait_ge(mixed_turned, t + 1)
                    if t >= 1:
                        dve.wait_ge(mixed_out, t)
                    dve.tensor_copy(xT[:, :, t * P:t * P + R],
                                    bank2(2 * (t % 2)).rearrange("p (k n) -> p k n", k=KC)[:, :, 0:R])\
                        .then_inc(mixed_out, 1)
                phase_over(dve, MIXED)
                project(OUT)
                norm(NORM2)
                phase_over(dve, PLE_T)
                project(GATED)
                layer_over(dve, L)


_INS = ["x_prompt", "x_sample", "state_ret", "cache_sb_k", "cache_sb_v", "cache_fox_k", "cache_fox_v",
        "cache_fox_logf", "page_table", "p_prompt", "p_sample", "g_norm", "w_in", "b_f", "g_ret_gn",
        "g_fox_q", "g_fox_k", "w_out", "w_pe", "g_pe", "w_pg"]
_OUTS = [(1, SEQ, D), (SEQS, NEW, D), (DEPTH, 1, HR, HD, HD), (DEPTH, SEQS, HR, HD, HD),
         (DEPTH, 1, SEQ, HA, HD), (DEPTH, 1, SEQ, HA, HD), (DEPTH, SEQS, NEW, HA, HD),
         (DEPTH, SEQS, NEW, HA, HD), (DEPTH, 1, SEQ, HA, HD), (DEPTH, 1, SEQ, HA, HD),
         (DEPTH, 1, SEQ, HA), (DEPTH, SEQS, NEW, HA, HD), (DEPTH, SEQS, NEW, HA, HD),
         (DEPTH, SEQS, NEW, HA)]


def kernel(**inputs):
    import concourse.bacc as _bacc
    from concourse import mybir as _mybir
    from concourse.bass_utils import run_bass_kernel_spmd as _run

    nc = _bacc.Bacc("TRN2", target_bir_lowering=False, num_devices=1)
    arrays, args = {}, []
    for name in _INS:
        a = np.ascontiguousarray(inputs[name])
        arrays[f"in_{name}_dram"] = a
        args.append(nc.dram_tensor(f"in_{name}_dram", a.shape, _mybir.dt.from_np(a.dtype),
                                   kind="ExternalInput").ap())
    consts = np.concatenate(list(tables().values()), axis=1)
    arrays["in_consts_dram"] = consts
    args.append(nc.dram_tensor("in_consts_dram", consts.shape, F32, kind="ExternalInput").ap())
    for i, shape in enumerate(_OUTS):
        args.append(nc.dram_tensor(f"out_{i}_dram", shape, F32, kind="ExternalOutput").ap())
    step_program(nc, *args)
    r = _run(nc, [arrays], core_ids=[0])
    return tuple(r.results[0][f"out_{i}_dram"] for i in range(len(_OUTS)))
```

```python
from contextlib import ExitStack

import numpy as np

import concourse.bass as bass
from concourse import mybir

F32 = mybir.dt.float32
BF16 = mybir.dt.bfloat16
I32 = mybir.dt.int32
ALU = mybir.AluOpType
ACT = mybir.ActivationFunctionType
AX = mybir.AxisListType.X

P = 128
D = 1024
KC = D // P
SEQ = 1024
NT = SEQ // P
SAMPLE = NT
TILES = NT + 1
DEPTH = 2
SEQS, NEW = 8, 8
ROWS = SEQS * NEW
HD = 64
HR, HA = 6, 5
DR, DA = HR * HD, HA * HD
PAGES = 32
PAST = PAGES * P
PLE = 256
EPS = 1e-6
NEG = -1e30
PG8 = 8
GROUPS = PAGES // PG8
HI = HA * NEW
SLOT = PAGES + 1
QP = HR // 2

SEG_NAMES = ["rq", "rk", "rv", "rg", "sq", "sk", "sv", "sg", "fg", "fq", "fk", "fv"]
SEG_COL = dict(rq=0, rk=DR, rv=2 * DR, rg=3 * DR, sq=4 * DR, sk=4 * DR + DA, sv=4 * DR + 2 * DA,
               sg=4 * DR + 3 * DA, fq=4 * DR + 4 * DA, fk=4 * DR + 5 * DA, fv=4 * DR + 6 * DA,
               fg=4 * DR + 7 * DA)
SEG_W = {s: DR if s[0] == "r" else DA for s in SEG_NAMES}
SEG_W["fg"] = DA + HA
ALL_SEGS = SEG_NAMES + ["out0", "out1", "pg0", "pe0", "pg1", "pe1"]
DVE_EVACUATES = {"rq", "rk", "rg", "sg", "fg", "out0", "out1", "pe0", "pe1"}
TURNED = {"rq": TILES, "rk": TILES, "sq": NT, "sk": NT, "fq": NT, "fk": NT}
GATE_AT = {"rg": 0, "sg": DR, "fg": DR + DA}


def rows(t):
    return ROWS if t == SAMPLE else P


def evac_count(seg, t):
    same = (seg in DVE_EVACUATES)
    before = [s for s in ALL_SEGS[:ALL_SEGS.index(seg)] if (s in DVE_EVACUATES) == same]
    return len(before) * TILES + t + 1


def turn_index(seg, t):
    return sum(n for s, n in TURNED.items() if ALL_SEGS.index(s) < ALL_SEGS.index(seg)) + t


def nat_count(seg, t):
    made = ["rq", "rk", "fq", "fk"]
    return TILES * made.index(seg) + t + 1


def tables():
    j, i = np.arange(P)[:, None], np.arange(P)[None, :]
    r = np.arange(P)
    log_g = np.log1p(-np.exp2(-5.0 - np.arange(HR)))
    inv = 10000.0 ** (-np.arange(HD // 2) / (HD // 2))
    pos = np.zeros((P, TILES))
    pos[:, :NT] = r[:, None] + P * np.arange(NT)[None, :]
    pos[:, SAMPLE] = PAST + r % NEW
    ang = pos[:, :, None].astype(np.float32) * inv.astype(np.float32)[None, None, :]
    ang = ang.astype(np.float64)
    b, k = r // NEW, r % NEW
    pair_head = 2 * np.arange(QP)[None, :] + (r // HD)[:, None]
    t = {}
    t["ident"] = np.eye(P)
    t["earlier"] = j < i
    t["negones"] = -np.ones((P, P))
    t["ones"] = np.ones((P, P))
    t["neg_upto"] = -1.0 * (j <= i)
    t["later_page"] = (j // PAGES == i // PAGES) & (j > i)
    t["neg_upto_new"] = (-1.0 * ((j // NEW == i // NEW) & (j <= i)))[:, :ROWS]
    t["cos"] = np.concatenate([np.cos(ang), np.cos(ang)], -1)
    t["sin"] = np.concatenate([-np.sin(ang), np.sin(ang)], -1)
    t["row_grow"] = np.exp((r[:, None] + 1.0) * log_g)
    t["col_grow"] = np.exp(-(r[:, None] + 1.0) * log_g) / 8
    t["key_decay"] = np.exp((P - 1.0 - r[:, None]) * log_g) / 8
    t["row_grow_new"] = np.exp((k[:, None] + 1.0) * log_g)
    t["col_grow_new"] = np.exp(-(k[:, None] + 1.0) * log_g) / 8
    t["key_decay_new"] = np.exp((NEW - 1.0 - k[:, None]) * log_g) / 8
    t["chunk_decay"] = np.exp(P * log_g)[pair_head]
    t["chunk_decay_new"] = np.exp(NEW * log_g)[pair_head]
    t["upto"] = j <= i
    t["upto_new"] = ((j // NEW == i // NEW) & (j <= i))[:, :ROWS]
    t["own_seq"] = b[:, None] == np.arange(SEQS)[None, :]
    t["before"] = i < j
    t["after_neg"] = np.where(i > j, NEG, 0.0)
    q = np.arange(NEW)[None, None, :]
    same = b[:, None, None] == np.arange(SEQS)[None, :, None]
    t["new_neg_sb"] = np.where(same & (k[:, None, None] < q), 0.0, NEG)
    t["new_neg_fox"] = np.where(same & (k[:, None, None] <= q), 0.0, NEG)
    return {n: np.asarray(v, np.float32).reshape(P, -1) for n, v in t.items()}


def table_places():
    at, places = 0, {}
    for name, v in tables().items():
        places[name] = (at, v.shape[1])
        at += v.shape[1]
    return places, at


STORES = 2 + QP + TILES + 2 + TILES

BLOCKS = 5 * GROUPS
SLOTS = 8
DVE_BLOCKS = (7, 9, 11, 13, 15, 17, 19)

DECODE_STEPS = {"sb": 2, "fox": 4}


def taken(engine_blocks, b, n):
    if n < 0:
        b, n = b - 1, n + BLOCKS
    return b * len(engine_blocks) + sum(m <= n for m in engine_blocks)


ACT_BLOCKS = tuple(n for n in range(BLOCKS) if n not in DVE_BLOCKS)


class Steps:

    def __init__(self, eng, sem):
        self.eng, self.sem, self.n, self.base = eng, sem, 0, 0

    def __call__(self, ins):
        self.n += 1
        ins.then_inc(self.sem, 1)
        self.eng.wait_ge(self.sem, self.base + self.n)

    def turn(self, b, per, first):
        self.base, self.n = b * per + first, 0


def step_program(nc, x_prompt, x_sample, state_ret, cache_sb_k, cache_sb_v, cache_fox_k,
                 cache_fox_v, cache_fox_logf, page_table, p_prompt, p_sample, g_norm, w_in, b_f,
                 g_ret_gn, g_fox_q, g_fox_k, w_out, w_pe, g_pe, w_pg, consts,
                 y_prompt, y_sample, rs_prompt, rs_sample, sbk_prompt, sbv_prompt, sbk_sample,
                 sbv_sample, foxk_prompt, foxv_prompt, foxl_prompt, foxk_sample, foxv_sample,
                 foxl_sample):
    n_pool = cache_sb_k.shape[1]
    residual_dram = nc.dram_tensor("residual_scratch", (TILES * P, D), F32, kind="Internal").ap()
    decoded_dram = nc.dram_tensor("decoded_scratch", (2, ROWS, DA), F32, kind="Internal").ap()
    logf_dram = nc.dram_tensor("logf_scratch", (SEQS * PAGES, P * HA), F32, kind="Internal").ap()
    places, n_consts = table_places()

    with ExitStack() as ctx:
        def sb(name, shape, dt=F32):
            return ctx.enter_context(nc.sbuf_tensor(name, shape, dt))

        def sem(name):
            return ctx.enter_context(nc.semaphore(name))

        xT = sb("xT", [P, KC, SEQ + ROWS])
        O = sb("O", [P, TILES, D])
        W = [sb(f"W{i}", [P, KC, 512]) for i in range(2)]
        C = sb("C", [P, n_consts])
        reset = sb("reset", [P, HI * SLOT], BF16)
        pages = sb("pages", [1, SEQS * PAGES], I32)
        gT = sb("gT", [P, 2, KC])
        g_ret_b = sb("g_ret_b", [P, DR])
        g_fq_b = sb("g_fq_b", [P, HD])
        g_fk_b = sb("g_fk_b", [P, HD])
        b_f_b = sb("b_f_b", [P, HA])
        eps = sb("eps", [P, 1])
        small = sb("small", [P, 256])
        row_max = sb("row_max", [P, P])
        q_new = sb("q_new", [ROWS, DA + HD])
        k_new = sb("k_new", [ROWS, DA])
        v_new = sb("v_new", [ROWS, DA])
        branch = sb("branch", [P, 15520])
        work = sb("work", [P, 5504])

        def cut(region, at, *shape):
            n = int(np.prod(shape))
            v = region[:, at:at + n]
            if len(shape) == 2:
                v = v.rearrange("p (a b) -> p a b", a=shape[0])
            if len(shape) == 3:
                v = v.rearrange("p (a b c) -> p a b c", a=shape[0], b=shape[1])
            if len(shape) == 4:
                v = v.rearrange("p (a b c d) -> p a b c d", a=shape[0], b=shape[1], c=shape[2])
            return v

        def const(name, *shape):
            at, n = places[name]
            return cut(C, at, *shape) if shape else C[:, at:at + n]

        ident = const("ident")
        ones = const("ones")
        cos_t, sin_t = const("cos", TILES, HD), const("sin", TILES, HD)

        TR = SEQ + ROWS
        qT_r, kT_r = cut(branch, 0, QP, TR), cut(branch, QP * TR, QP, TR)
        v_r = cut(branch, 2 * QP * TR, TILES, DR)
        kd_r = cut(branch, 2 * QP * TR + TILES * DR, TILES, DR)
        at = 2 * QP * TR + 2 * TILES * DR
        s0 = cut(branch, at, QP, SEQS, HD)
        state = cut(branch, at + QP * SEQS * HD, QP, HD)
        qT_s, kT_s = cut(branch, 0, QP, SEQ), cut(branch, QP * SEQ, QP, SEQ)
        v_s = cut(branch, 2 * QP * SEQ, NT, DA)
        at = 2 * QP * SEQ + NT * DA
        sig = cut(branch, at, 2, SEQ)
        att = cut(branch, at + 2 * SEQ, 2, SEQ)
        rest = branch[:, at + 4 * SEQ:at + 5 * SEQ]
        prod = branch[:, at + 5 * SEQ:at + 6 * SEQ + 1]
        qT_f, kT_f = cut(branch, 0, HA, SEQ), cut(branch, HA * SEQ, HA, SEQ)
        v_f = cut(branch, 2 * HA * SEQ, NT, DA)
        junk = work[:, 0:D]
        scaled = cut(work, D, 2, D)
        nat = cut(work, 0, 2, DR)
        rot_a, rot_b = work[:, 768:768 + DR], work[:, 1152:1152 + DR]
        aug = cut(work, 1536, 2, HA, HD + 1)
        squares = cut(work, 2200, HA, HD)
        logit = cut(work, 2600, TILES, HA)
        ltmp = cut(work, 2650, TILES, HA)
        logf_padded = cut(work, 2700, NT - 1 + TILES, HA)
        logf = logf_padded[:, NT - 1:]
        neg_c = cut(small, 64, TILES, HA)
        masked = cut(work, 0, 2, P)
        ret_o, ret_sq = cut(work, 256, HR, HD), cut(work, 640, HR, HD)
        cross = cut(work, 1024, SEQS, HD)
        v_seq = cut(work, 1536, 2, SEQS * HD)
        expd = cut(work, 0, 2, SEQ)
        attT = cut(work, 2 * SEQ, 2, SEQ)
        ringK = cut(branch, 0, 2, PG8 * DA)
        ringV = cut(branch, 2 * PG8 * DA, 2, PG8 * DA)
        at = 4 * PG8 * DA
        NZ = HI * SLOT
        zs = branch[:, at:at + NZ]
        soft = branch[:, at + NZ:at + 2 * NZ]
        later = branch[:, at + 2 * NZ:at + 3 * NZ]
        probs = branch[:, at + 3 * NZ:at + 4 * NZ]
        kT_d = W[1]
        z_rows = cut(work, 0, 3, 512)
        q_now = cut(work, 1536, 5, 32)
        qd = cut(work, 2048, SEQS, 5, 2 * NEW)
        kT_new = cut(work, 2688, 3, ROWS)
        decoded = cut(work, 2880, SEQS, 2, HD)
        forget = cut(work, 3904, HA, SEQS * PAGES)
        new_bias = cut(work, 5184, SEQS, HA, NEW)
        page_logf = cut(branch, 0, 2, P, HA)
        page_sum = cut(branch, 1280, 2, HA, P)
        x_half = cut(work, 0, 2, 512)
        p_nat = cut(branch, 0, TILES, PLE)
        pT = cut(branch, TILES * PLE, 2, TR)
        gate = cut(branch, TILES * PLE + 2 * TR, TILES, 512)
        gated = cut(work, 1024, 2, 512)

        ps = ctx.enter_context(nc.psum_tensor("ps", [P, 8, 512], F32))

        arrived = sem("arrived")
        layer_go = sem("layer_go")
        consts_in = sem("consts_in")
        set_up = sem("set_up")
        x_in = sem("x_in")
        y_out = sem("y_out")
        x_saved = sem("x_saved")
        k_saved = [sem(f"k_saved{i}") for i in range(2)]
        saved = sem("saved")
        logf_gathered = sem("logf_gathered")
        logf_in = sem("logf_in")
        stored = {k: sem(f"stored_{k}") for k in ("sb", "fox")}
        v_in = {k: [sem(f"v_in{i}_{k}") for i in range(2)] for k in ("sb", "fox")}
        phase_sem = sem("phase_sem")
        w_loaded = [sem(f"w_loaded{i}") for i in range(2)]
        vec_loaded = sem("vec_loaded")
        pool_ready = sem("pool_ready")
        squared = sem("squared")
        rooted = sem("rooted")
        scaled_ready = sem("scaled_ready")
        norm_turned = sem("norm_turned")
        norm_out = sem("norm_out")
        proj_ready = sem("proj_ready")
        emptied_dve = sem("emptied_dve")
        emptied_act = sem("emptied_act")
        nat_ready = sem("nat_ready")
        turned = sem("turned")
        turned_out = sem("turned_out")
        sigmoid_ready = sem("sigmoid_ready")
        head_sums = sem("head_sums")
        head_roots = sem("head_roots")
        logit_ready = sem("logit_ready")
        logf_act = sem("logf_act")
        logf_ready = sem("logf_ready")
        cum_ready = sem("cum_ready")
        neg_c_ready = sem("neg_c_ready")
        scores_r = sem("scores_r")
        masked_r = sem("masked_r")
        inner_r = sem("inner_r")
        ret_emptied = sem("ret_emptied")
        kv_r = sem("kv_r")
        state_r = sem("state_r")
        centred_r = sem("centred_r")
        squares_r = sem("squares_r")
        sums_r = sem("sums_r")
        roots_r = sem("roots_r")
        state_in = sem("state_in")
        cross_ready = sem("cross_ready")
        cross_emptied = sem("cross_emptied")
        v_seq_ready = sem("v_seq_ready")
        new_state_ready = sem("new_state_ready")
        new_state_out = sem("new_state_out")
        att_scores = {k: sem(f"att_scores_{k}") for k in ("sb", "fox")}
        att_first = {k: sem(f"att_first_{k}") for k in ("sb", "fox")}
        att_probs = {"sb": sem("att_probs_sb")}
        att_max = sem("att_max")
        att_emptied = sem("att_emptied")
        att_turned = {k: sem(f"att_turned_{k}") for k in ("sb", "fox")}
        attT_ready = {k: sem(f"attT_ready_{k}") for k in ("sb", "fox")}
        att_out = {k: sem(f"att_out_{k}") for k in ("sb", "fox")}
        att_done = {k: sem(f"att_done_{k}") for k in ("sb", "fox")}
        steps_sem = sem("steps_sem")
        dec = {}
        for k in ("sb", "fox"):
            dec[k] = {n: sem(f"{n}_{k}") for n in (
                "k0", "k1", "new_turned", "new_ready", "new_scored", "q_ready", "kt_ready",
                "kt_act", "kt_dve", "scores_done", "rows_out", "z_turned", "z_drained", "fold_ready", "fold_out", "bias_ready",
                "soft_in", "soft_act", "soft_ready", "sum_ready", "expo_ready", "probs_ready",
                "v_used", "pv_done", "o_emptied", "loaded", "den_ready")}
        page_ready = sem("page_ready")
        page_carry = sem("page_carry")
        forget_part = sem("forget_part")
        forget_turned = sem("forget_turned")
        forget_ready = sem("forget_ready")
        mixed_turned = sem("mixed_turned")
        mixed_out = sem("mixed_out")
        x_half_in = [sem(f"x_half_in{i}") for i in range(2)]
        p_in = sem("p_in")
        p_turned = sem("p_turned")
        p_out = sem("p_out")
        pool_waits = sem("pool_waits")
        last_sem = sem("last_sem")

        def phase_over(eng, n):
            eng.drain().then_inc(phase_sem, 1)
            eng.wait_ge(phase_sem, 4 * (n + 1))

        def layer_over(eng, L):
            eng.drain().then_inc(arrived, 1)
            eng.wait_ge(layer_go, L + 1)

        (NORM1, PROJ_R, RET, PROJ_S, ATT_S, DEC_S, PROJ_F, ATT_F, DEC_F, MIXED, OUT, NORM2, PLE_T,
         GATED) = range(14)
        NORMS = {NORM1: 0, NORM2: 1}
        PROJ_SEGS = {PROJ_R: SEG_NAMES[0:4], PROJ_S: SEG_NAMES[4:8], PROJ_F: SEG_NAMES[8:12],
                     OUT: ["out0", "out1"], GATED: ["pg0", "pe0", "pg1", "pe1"]}
        KIND = {ATT_S: "sb", ATT_F: "fox", DEC_S: "sb", DEC_F: "fox"}
        CACHE = {"sb": (cache_sb_k, cache_sb_v), "fox": (cache_fox_k, cache_fox_v)}
        UNITS = [(t, h) for t in range(NT) for h in range(HA)]

        def bank2(first, n=1024):
            return ps[:, first:first + 2, :].rearrange("p b c -> p (b c)")[:, 0:n]

        block = ctx.enter_context(nc.Block())

        @block.sync
        def _(sp):
            sp.dma_start(C[:], consts).then_inc(consts_in, 16)
            sp.dma_start(pages[:], page_table.rearrange("b p -> (b p)").unsqueeze(0)).then_inc(consts_in, 16)
            sp.dma_start(O[:, 0:NT, :], x_prompt[0].rearrange("(t p) d -> p t d", p=P)).then_inc(x_in, 16)
            sp.dma_start(O[0:ROWS, SAMPLE, :], x_sample.rearrange("b s d -> (b s) d")).then_inc(x_in, 16)
            sp.wait_ge(consts_in, 32)

            def load_weights(L, seg):
                i = ALL_SEGS.index(seg)
                if i >= 2:
                    sp.wait_ge(proj_ready, TILES * (i - 1))
                if seg in SEG_COL:
                    n = SEG_W[seg]
                    src = w_in[L, :, SEG_COL[seg]:SEG_COL[seg] + n]
                    kc = KC
                else:
                    n, c = 512, int(seg[-1])
                    src = {"ou": w_out, "pg": w_pg, "pe": w_pe}[seg[:2]][L, :, c * 512:(c + 1) * 512]
                    kc = PLE // P if seg[:2] == "pe" else KC
                sp.dma_start(W[i % 2][:, 0:kc, 0:n], src.rearrange("(k p) n -> p k n", p=P))\
                    .then_inc(w_loaded[i % 2], 16)

            def load_k(L, kind, b, g):
                cache = CACHE[kind][0]
                s = dec[kind]
                if not (isinstance(b, int) and 4 * b + g < 2):
                    sp.wait_ge(s["kt_ready"], b * 20 + 5 * (g - 1))
                for p in range(PG8):
                    at = b * PAGES + g * PG8 + p
                    pg = sp.value_load(pages[0:1, bass.ds(at, 1)])
                    sp.dma_start(ringK[:, g % 2, p * DA:(p + 1) * DA],
                                 cache[L, bass.ds(pg, 1)].rearrange("a s h d -> s (a h d)"))\
                        .then_inc(s[f"k{g % 2}"], 16)

            def decode_loads(L, kind):
                for g in range(GROUPS):
                    load_k(L, kind, 0, g)
                with sp.Fori(1, SEQS) as b:
                    for g in range(GROUPS):
                        load_k(L, kind, b, g)
                sp.wait_ge(stored[kind], 16 * HA * (L + 1))
                sp.dma_start(work[0:ROWS, 0:DA], decoded_dram[0 if kind == "sb" else 1])\
                    .then_inc(dec[kind]["loaded"], 16)

            with sp.Fori(0, DEPTH) as L:
                load_weights(L, "rq")
                load_weights(L, "rk")
                for dst, src in (
                        (gT[:, 0, :], g_norm[L].rearrange("(k p) -> p k", p=P)),
                        (gT[:, 1, :], g_pe[L].rearrange("(k p) -> p k", p=P)),
                        (g_ret_b[:], g_ret_gn[L].partition_broadcast(P)),
                        (g_fq_b[:], g_fox_q[L].partition_broadcast(P)),
                        (g_fk_b[:], g_fox_k[L].partition_broadcast(P)),
                        (b_f_b[:], b_f[L].partition_broadcast(P))):
                    sp.dma_start(dst, src, allow_slow_non_contiguous=True).then_inc(vec_loaded, 16)
                for pr in range(QP):
                    sp.dma_start(s0[:, pr], state_ret[L, :, 2 * pr:2 * pr + 2].rearrange(
                        "b h d e -> (h d) b e")).then_inc(state_in, 16)
                for seg in SEG_NAMES[2:9]:
                    load_weights(L, seg)
                sp.wait_ge(phase_sem, 4 * (ATT_S + 1))
                decode_loads(L, "sb")
                sp.wait_ge(phase_sem, 4 * (DEC_S + 1))
                for seg in ALL_SEGS[9:13]:
                    load_weights(L, seg)
                sp.wait_ge(phase_sem, 4 * (ATT_F + 1))
                sp.wait_ge(forget_ready, HA)
                decode_loads(L, "fox")
                sp.wait_ge(phase_sem, 4 * (DEC_F + 1))
                load_weights(L, "out1")
                sp.wait_ge(phase_sem, 4 * (MIXED + 1))
                sp.wait_ge(x_saved, 32 * (L + 1))
                for c in range(2):
                    for t in range(TILES):
                        n = c * TILES + t
                        if n >= 2:
                            sp.wait_ge(emptied_dve, evac_count("out0", 0) + n - 2)
                        sp.dma_start(x_half[0:rows(t), n % 2, :], residual_dram[
                            t * P:t * P + rows(t), c * 512:(c + 1) * 512]).then_inc(x_half_in[n % 2], 16)
                sp.wait_ge(phase_sem, 4 * (NORM2 + 1))
                sp.dma_start(p_nat[:, 0:NT, :], p_prompt[L, 0].rearrange("(t p) c -> p t c", p=P))\
                    .then_inc(p_in, 16)
                sp.dma_start(p_nat[0:ROWS, SAMPLE, :], p_sample[L].rearrange("b s c -> (b s) c"))\
                    .then_inc(p_in, 16)
                for seg in ALL_SEGS[14:18]:
                    load_weights(L, seg)
                sp.wait_ge(arrived, 4 * (L + 1))
                sp.sem_inc(last_sem, 1)
                sp.sem_clear(range(phase_sem.num, last_sem.num + 1))
                sp.sem_inc(layer_go, 1)

        @block.gpsimd
        def _(pool):
            def await_dma(done, value):
                pool.wait_ge(done, value)
                pool.sem_inc(pool_waits, 1)

            nc.gpsimd.memset(eps[:], EPS).then_inc(set_up, 1)
            nc.gpsimd.memset(reset[:], 1.0).then_inc(set_up, 1)
            pool.wait_ge(set_up, 2)
            nc.gpsimd.memset(reset[:].rearrange("p (r s) -> p r s", s=SLOT)[:, :, SLOT - 1:SLOT],
                             0.0).then_inc(set_up, 1)
            pool.wait_ge(consts_in, 32)
            pool.wait_ge(x_in, 32)
            with pool.Fori(0, DEPTH) as L:
                stores = 0
                pool.dma_start(residual_dram[0:SEQ].rearrange("(t p) d -> p t d", p=P),
                               O[:, 0:NT, :]).then_inc(x_saved, 16)
                pool.dma_start(residual_dram[SEQ:SEQ + ROWS], O[0:ROWS, SAMPLE, :]).then_inc(x_saved, 16)
                await_dma(x_saved, 32 * (L + 1))
                phase_over(pool, NORM1)
                pool.sem_inc(phase_sem, 1)
                with pool.Fori(0, SEQS * PAGES) as p:
                    pg = pool.value_load(pages[0:1, bass.ds(p, 1)])
                    pool.dma_start(logf_dram[bass.ds(p, 1)],
                                   cache_fox_logf[L, bass.ds(pg, 1)].rearrange("a s h -> a (s h)"))\
                        .then_inc(logf_gathered, 16)
                pool.wait_ge(state_r, NT)
                for h2 in range(2):
                    pool.dma_start(rs_prompt[L, 0].rearrange("(pr h) d e -> h d pr e", h=2)[h2],
                                   state[h2 * HD:(h2 + 1) * HD]).then_inc(saved, 16)
                    stores += 1
                pool.wait_ge(new_state_out, HR)
                for pr in range(QP):
                    pool.dma_start(rs_sample[L, :, 2 * pr:2 * pr + 2].rearrange("b h d e -> (h d) b e"),
                                   s0[:, pr]).then_inc(saved, 16)
                    stores += 1
                await_dma(saved, L * 16 * STORES + 16 * stores)
                phase_over(pool, RET)

                def store_kv(seg, t, src, prompt, sample, done, ready, count):
                    pool.wait_ge(ready, count)
                    if t == SAMPLE:
                        dst = sample[L].rearrange("b s h d -> (b s) (h d)")
                    else:
                        dst = prompt[L, 0, t * P:(t + 1) * P].rearrange("p h d -> p (h d)")
                    pool.dma_start(dst, src).then_inc(done, 16)

                for t in range(TILES):
                    src = k_new[:] if t == SAMPLE else nat[:, turn_index("sk", t) % 2, 0:DA]
                    store_kv("sk", t, src, sbk_prompt, sbk_sample, k_saved[t % 2],
                             emptied_act, evac_count("sk", t))
                for t in range(TILES):
                    src = v_new[:] if t == SAMPLE else v_s[:, t]
                    store_kv("sv", t, src, sbv_prompt, sbv_sample, saved, emptied_act,
                             evac_count("sv", t))
                    stores += 1
                await_dma(k_saved[0], L * 160 + 16 * 5)
                await_dma(k_saved[1], L * 128 + 16 * 4)
                await_dma(saved, L * 16 * STORES + 16 * stores)
                phase_over(pool, PROJ_S)
                phase_over(pool, ATT_S)

                def load_values(kind):
                    cache = CACHE[kind][1]
                    with pool.Fori(0, SEQS) as b:
                        for g in range(GROUPS):
                            await_dma(dec[kind]["v_used"], b * GROUPS + g + 1)
                            for p in range(PG8):
                                at = b * PAGES + g * PG8 + p
                                pg = pool.value_load(pages[0:1, bass.ds(at, 1)])
                                pool.dma_start(ringV[:, g % 2, p * DA:(p + 1) * DA],
                                               cache[L, bass.ds(pg, 1)].rearrange("a s h d -> s (a h d)"))\
                                    .then_inc(v_in[kind][g % 2], 16)

                def decoded_store(kind):
                    pool.wait_ge(dec[kind]["o_emptied"], SEQS + 1)
                    dst = decoded_dram[0 if kind == "sb" else 1].rearrange("(b i) c -> i b c", b=SEQS)
                    for h in range(HA):
                        q = 32 * (h % 4)
                        pool.dma_start(dst[:, :, h * HD:(h + 1) * HD], decoded[q:q + NEW, :, h // 4, :])\
                            .then_inc(stored[kind], 16)

                load_values("sb")
                decoded_store("sb")
                phase_over(pool, DEC_S)
                pool.wait_ge(logf_ready, 1)
                pool.dma_start(foxl_prompt[L, 0].rearrange("(t p) h -> p t h", p=P), logf[:, 0:NT, :])\
                    .then_inc(saved, 16)
                pool.dma_start(foxl_sample[L].rearrange("b s h -> (b s) h"), logf[0:ROWS, SAMPLE, :])\
                    .then_inc(saved, 16)
                stores += 2
                for t in range(TILES):
                    src = k_new[:].rearrange("p (h d) -> p h d", h=HA) if t == SAMPLE else \
                        aug[:, turn_index("fk", t) % 2, :, 0:HD]
                    pool.wait_ge(nat_ready, nat_count("fk", t))
                    dst = foxk_sample[L].rearrange("b s h d -> (b s) h d") if t == SAMPLE else \
                        foxk_prompt[L, 0, t * P:(t + 1) * P]
                    pool.dma_start(dst, src).then_inc(k_saved[t % 2], 16)
                for t in range(TILES):
                    src = v_new[:] if t == SAMPLE else v_f[:, t]
                    store_kv("fv", t, src, foxv_prompt, foxv_sample, saved, emptied_act,
                             evac_count("fv", t))
                    stores += 1
                await_dma(k_saved[0], L * 160 + 16 * 10)
                await_dma(k_saved[1], L * 128 + 16 * 8)
                await_dma(saved, L * 16 * STORES + 16 * stores)
                phase_over(pool, PROJ_F)
                phase_over(pool, ATT_F)
                await_dma(logf_gathered, 16 * SEQS * PAGES * (L + 1))
                pool.dma_start(page_logf.rearrange("p a s h -> p a (s h)"),
                               logf_dram.rearrange("(a p) n -> p a n", p=P)).then_inc(logf_in, 16)
                load_values("fox")
                decoded_store("fox")
                phase_over(pool, DEC_F)
                for n in (MIXED, OUT, NORM2, PLE_T, GATED):
                    phase_over(pool, n)
                assert stores == STORES
                layer_over(pool, L)
            pool.dma_start(y_prompt[0].rearrange("(t p) d -> p t d", p=P), O[:, 0:NT, :]).then_inc(y_out, 16)
            pool.dma_start(y_sample.rearrange("b s d -> (b s) d"), O[0:ROWS, SAMPLE, :]).then_inc(y_out, 16)
            pool.wait_ge(y_out, 32)

        @block.tensor
        def _(pe):
            pe.wait_ge(consts_in, 32)
            pe.wait_ge(set_up, 3)

            def norm(phase):
                for t in range(TILES):
                    m, R = NORMS[phase] * TILES + t, rows(t)
                    pe.wait_ge(scaled_ready, m + 1)
                    if m >= 2:
                        pe.wait_ge(norm_out, m - 1)
                    for k in range(KC):
                        ins = pe.transpose(ps[:, 2 * (m % 2) + k // 4, (k % 4) * P:(k % 4) * P + R],
                                           scaled[0:R, m % 2, k * P:(k + 1) * P], ident[0:R, 0:R])
                    ins.then_inc(norm_turned, 1)
                phase_over(pe, phase)

            def segment_tile(seg, t):
                i = ALL_SEGS.index(seg)
                n = i * TILES + t
                R, N = rows(t), SEG_W.get(seg, 512)
                if t == 0:
                    pe.wait_ge(w_loaded[i % 2], 16 * (i // 2 + 1))
                if n >= 3:
                    s3, t3 = ALL_SEGS[(n - 3) // TILES], (n - 3) % TILES
                    pe.wait_ge(emptied_dve if s3 in DVE_EVACUATES else emptied_act, evac_count(s3, t3))
                src = pT if seg[:2] == "pe" else xT
                kc = PLE // P if seg[:2] == "pe" else KC
                for k in range(kc):
                    ins = pe.matmul(ps[0:R, n % 3, 0:N], src[:, k, t * P:t * P + R],
                                    W[i % 2][:, k, 0:N], start=(k == 0), stop=(k == kc - 1))
                ins.then_inc(proj_ready, 1)

            def turn_tile(seg, t):
                m, R = turn_index(seg, t), rows(t)
                if seg[0] == "s":
                    pe.wait_ge(emptied_act, evac_count(seg, t))
                else:
                    pe.wait_ge(nat_ready, nat_count(seg, t))
                if m >= 2:
                    pe.wait_ge(turned_out, m - 1)
                bank = 3 + 2 * (m % 2)
                if seg[0] == "f":
                    for h in range(HA):
                        ins = pe.transpose(ps[0:HD + 1, bank + h // 4, (h % 4) * P:(h % 4) * P + R],
                                           aug[0:R, m % 2, h, :], ident[0:R, 0:R])
                else:
                    for c in range(QP):
                        w = min(P, SEG_W[seg] - c * P)
                        ins = pe.transpose(ps[0:w, bank, c * P:c * P + R],
                                           nat[0:R, m % 2, c * P:c * P + w], ident[0:R, 0:R])
                ins.then_inc(turned, 1)

            def project(phase):
                for seg in PROJ_SEGS[phase]:
                    for t in range(TILES):
                        segment_tile(seg, t)
                        if t >= 1 and t - 1 < TURNED.get(seg, 0):
                            turn_tile(seg, t - 1)
                    if TURNED.get(seg, 0) == TILES:
                        turn_tile(seg, TILES - 1)
                    if seg == "fg":
                        pe.wait_ge(logf_ready, 1)
                        padded = logf_padded.rearrange("p t h -> p (t h)")
                        lf = padded[:, (NT - 1) * HA:]
                        out = ps[:, 7, 0:NT * HA]
                        pe.matmul(out, const("neg_upto"), lf[:, 0:NT * HA], start=True, stop=False)
                        for d in range(1, NT):
                            pe.matmul(out, const("negones"),
                                      padded[:, (NT - 1 - d) * HA:(2 * NT - 1 - d) * HA],
                                      start=False, stop=(d == NT - 1))
                        pe.matmul(ps[0:ROWS, 7, 64:64 + HA], const("neg_upto_new")[0:ROWS],
                                  lf[0:ROWS, NT * HA:], start=True, stop=True).then_inc(cum_ready, 1)
                phase_over(pe, phase)

            def retention():
                units = [(t, h) for t in range(TILES) for h in range(HR)]

                def at(h):
                    return h // 2, slice((h % 2) * HD, (h % 2) * HD + HD)

                def scores(u):
                    t, h = units[u]
                    pr, q = at(h)
                    R = rows(t)
                    if u >= 2:
                        pe.wait_ge(masked_r, u - 1)
                    pe.matmul(ps[0:R, u % 2, 0:R], kT_r[q, pr, t * P:t * P + R],
                              qT_r[q, pr, t * P:t * P + R], start=True, stop=True).then_inc(scores_r, 1)

                scores(0)
                for u, (t, h) in enumerate(units):
                    pr, q = at(h)
                    R = rows(t)
                    if u + 1 < len(units):
                        scores(u + 1)
                    pe.wait_ge(masked_r, u + 1)
                    if h == 0 and t >= 2:
                        pe.wait_ge(ret_emptied, t - 1)
                    with_state = 0 < t < SAMPLE
                    bank, c = (2, h) if t == SAMPLE else (2 + t % 2 + 4 * (h % 2), h // 2)
                    out = ps[0:R, bank, c * HD:(c + 1) * HD]
                    ins = pe.matmul(out, masked[0:R, u % 2, 0:R], v_r[0:R, t, h * HD:(h + 1) * HD],
                                    start=True, stop=not with_state)
                    if with_state:
                        if h == 0:
                            pe.wait_ge(state_r, t)
                        ins = pe.matmul(out, qT_r[q, pr, t * P:t * P + R], state[q, pr, :],
                                        start=False, stop=True)
                    ins.then_inc(inner_r, 1)
                    if h == HR - 1 and t < SAMPLE:
                        if t >= 2:
                            pe.wait_ge(state_r, t - 1)
                        for c in range(QP):
                            ins = pe.matmul(ps[:, 4 + t % 2, c * P:(c + 1) * P],
                                            kd_r[:, t, c * P:(c + 1) * P], v_r[:, t, c * P:(c + 1) * P],
                                            start=True, stop=True)
                        ins.then_inc(kv_r, 1)
                pe.wait_ge(state_in, 16 * QP)
                for h in range(HR):
                    pr, q = at(h)
                    if h >= 2:
                        pe.wait_ge(cross_emptied, h - 1)
                    pe.matmul(ps[0:ROWS, 6 + h % 2, :], qT_r[q, pr, SEQ:TR],
                              s0[q, pr].rearrange("p b e -> p (b e)"), start=True, stop=True)\
                        .then_inc(cross_ready, 1)
                for h in range(HR):
                    pr, q = at(h)
                    pe.wait_ge(v_seq_ready, h + 1)
                    if h >= 2:
                        pe.wait_ge(new_state_out, h - 1)
                    if h < 2:
                        pe.wait_ge(state_r, NT)
                    pe.matmul(ps[q, 4 + h % 2, :], kd_r[0:ROWS, SAMPLE, h * HD:(h + 1) * HD],
                              v_seq[0:ROWS, h % 2, :], start=True, stop=True,
                              tile_position=(0, q.start)).then_inc(new_state_ready, 1)
                phase_over(pe, RET)

            def attention(phase):
                kind = KIND[phase]
                qT, kT, v = (qT_s, kT_s, v_s) if kind == "sb" else (qT_f, kT_f, v_f)

                def scores(u):
                    t, h = UNITS[u]
                    n = (t + 1) * P
                    q = slice((h % 2) * HD, (h % 2) * HD + HD) if kind == "sb" else slice(0, HD + 1)
                    a = h // 2 if kind == "sb" else h
                    if u >= 2:
                        pe.wait_ge(att_first[kind], u - 1)
                    for c in range(0, n, 512):
                        w = min(512, n - c)
                        ins = pe.matmul(ps[:, 2 * (u % 2) + c // 512, 0:w], qT[q, a, t * P:(t + 1) * P],
                                        kT[q, a, c:c + w], start=True, stop=True)
                    ins.then_inc(att_scores[kind], 1)

                def turn(u):
                    t, h = UNITS[u]
                    pe.wait_ge(att_probs[kind] if kind == "sb" else att_first[kind], u + 1)
                    if u >= 1:
                        pe.wait_ge(attT_ready[kind], u)
                    src = att if kind == "sb" else expd
                    for j in range(t + 1):
                        ins = pe.transpose(ps[:, 4 + j // 4, (j % 4) * P:(j % 4 + 1) * P],
                                           src[:, u % 2, j * P:(j + 1) * P], ident)
                    ins.then_inc(att_turned[kind], 1)

                def weigh(u):
                    t, h = UNITS[u]
                    pe.wait_ge(attT_ready[kind], u + 1)
                    if h == 0 and t >= 2:
                        pe.wait_ge(att_done[kind], t - 1)
                    for j in range(t + 1):
                        ins = pe.matmul(ps[:, 6 + t % 2, h * HD:(h + 1) * HD],
                                        attT[:, u % 2, j * P:(j + 1) * P], v[:, j, h * HD:(h + 1) * HD],
                                        start=(j == 0), stop=(j == t))
                    ins.then_inc(att_out[kind], 1)

                scores(0)
                for u in range(len(UNITS)):
                    if u + 1 < len(UNITS):
                        scores(u + 1)
                    if u >= 1:
                        weigh(u - 1)
                    turn(u)
                weigh(len(UNITS) - 1)
                phase_over(pe, phase)

            def forget_sums():
                for half in range(2):
                    pe.wait_ge(page_ready, half + 1)
                    pe.matmul(ps[:, 6 + half, 0:HA], const("later_page"), page_sum[:, half, :, 0],
                              start=True, stop=True).then_inc(page_carry, 1)
                for h in range(HA):
                    pe.wait_ge(forget_part, 2)
                    if h >= 2:
                        pe.wait_ge(forget_ready, h - 1)
                    for half in range(2):
                        ins = pe.transpose(ps[:, h % 2, half * P:(half + 1) * P], page_sum[:, half, h, :],
                                           ident)
                    ins.then_inc(forget_turned, 1)
                pe.wait_ge(forget_ready, HA)

            def decode(phase, L):
                kind = KIND[phase]
                s = dec[kind]
                if kind == "fox":
                    forget_sums()
                for c, at in enumerate((0, 2 * HD, 4 * HD, HD, 3 * HD)):
                    pe.transpose(ps[:, 0, c * ROWS:(c + 1) * ROWS], q_new[:, at:at + P], ident[0:ROWS, 0:ROWS])
                for c in range(3):
                    w = min(P, DA - c * P)
                    ins = pe.transpose(ps[0:w, 1, c * ROWS:(c + 1) * ROWS], k_new[:, c * P:c * P + w],
                                       ident[0:ROWS, 0:ROWS])
                ins.then_inc(s["new_turned"], 1)
                pe.sem_inc(s["v_used"], 2)
                pe.wait_ge(s["new_ready"], 1)
                for c in range(3):
                    ins = pe.matmul(ps[0:ROWS, 2, c * P:(c + 1) * P], kT_new[:, c, :], qd[:, :, c, :],
                                    start=True, stop=True)
                ins.then_inc(s["new_scored"], 1)

                def is_first(b):
                    return isinstance(b, int) and b == 0

                def turn_blocks(b, blocks):
                    for n in blocks:
                        g, kk = n // 5, n % 5
                        if kk == 0:
                            pe.wait_ge(s[f"k{g % 2}"], PG8 * 16 * (b * 2 + g // 2 + 1))
                        if not is_first(b) or n >= 2:
                            by_act = (n - 2) % BLOCKS in ACT_BLOCKS
                            pe.wait_ge(s["kt_act" if by_act else "kt_dve"],
                                       taken(ACT_BLOCKS if by_act else DVE_BLOCKS, b, n - 2))
                        for m in range(4):
                            at = (5 * m + kk) * P
                            ins = pe.transpose(ps[:, n % 2, m * P:(m + 1) * P], ringK[:, g % 2, at:at + P],
                                               ident)
                        ins.then_inc(s["kt_ready"], 1)

                def score(b, g):
                    n = 5 * g + 4
                    pe.wait_ge(s["kt_act"], taken(ACT_BLOCKS, b, n))
                    if not is_first(b) or any(m <= n for m in DVE_BLOCKS):
                        pe.wait_ge(s["kt_dve"], taken(DVE_BLOCKS, b, n))
                    if g == 0:
                        pe.wait_ge(s["q_ready"], b + 1)
                    if not is_first(b) or g >= 2:
                        pe.wait_ge(s["rows_out"], 5 * b + g - (1 if g >= 2 else 0) if g else 5 * b)
                    if g == 1 and not is_first(b):
                        pe.wait_ge(s["soft_ready"], b)
                    for kk in range(5):
                        bank = 3 if kk == 4 else (5 if g % 2 else 2)
                        q = 32 * (g if kk == 4 else kk)
                        ins = pe.matmul(ps[q:q + 32, bank, :], q_now[:, kk, :], kT_d[:, (5 * g + kk) % SLOTS, :],
                                        start=True, stop=True, tile_position=(0, q), skip_group_check=True)
                    ins.then_inc(s["scores_done"], 1)

                def turn_rows(b, j):
                    pe.wait_ge(s["rows_out"], 5 * b + j + 1)
                    if j >= 2:
                        pe.wait_ge(s["z_drained"], 5 * b + j - 1)
                    elif not is_first(b):
                        pe.wait_ge(s["soft_ready"], b)
                    for m in range(4):
                        ins = pe.transpose(ps[:, 6 + j % 2, m * P:(m + 1) * P],
                                           z_rows[:, 2 if j == 4 else j % 2, m * P:(m + 1) * P], ident)
                    ins.then_inc(s["z_turned"], 1)

                def fold_first(b):
                    if kind == "fox":
                        pe.wait_ge(s["soft_in"], b + 1)
                        pe.transpose(ps[:, 6, 0:P], row_max[:], ident).then_inc(s["fold_ready"], 1)

                def fold(b):
                    if kind == "sb":
                        pe.wait_ge(s["sum_ready"], b + 1)
                        for c in range(3):
                            cols = slice(c * 440, c * 440 + 440)
                            pe.matmul(ps[:, 5 + c, 0:440], const("earlier"), soft[:, cols], start=True, stop=False)
                            ins = pe.matmul(ps[:, 5 + c, 0:440], const("negones"), later[:, cols], start=False,
                                            stop=True)
                        ins.then_inc(s["expo_ready"], 1)
                    else:
                        pe.wait_ge(s["fold_out"], b + 1)
                        pe.matmul(ps[:, 6, P:P + HI], ones[0:HI, :], small[0:HI, 120:120 + HI], start=True,
                                  stop=True).then_inc(s["bias_ready"], 1)

                def weigh(b, g):
                    pr = probs.rearrange("p (h i s) -> p h i s", h=HA, i=NEW)

                    def out(h):
                        q = 32 * (h % 4)
                        return ps[q:q + NEW, 4, (h // 4) * HD:(h // 4 + 1) * HD]

                    if g == 0:
                        pe.wait_ge(s["probs_ready"], b + 1)
                        pe.wait_ge(s["o_emptied"], b + 1)
                    pe.wait_ge(v_in[kind][g % 2], PG8 * 16 * (b * 2 + g // 2 + 1 + L * SEQS * 2))
                    for p in range(PG8):
                        for h in range(HA):
                            c = p * DA + h * HD
                            ins = pe.matmul(out(h), pr[:, h, :, g * PG8 + p], ringV[:, g % 2, c:c + HD],
                                            start=(g == 0 and p == 0), stop=False,
                                            tile_position=(0, 32 * (h % 4)), skip_group_check=True)
                    ins.then_inc(s["v_used"], 1)
                    if g < GROUPS - 1:
                        return
                    for h in range(HA):
                        ins = pe.matmul(out(h), pr[0:ROWS, h, :, PAGES], v_new[:, h * HD:(h + 1) * HD],
                                        start=False, stop=True, tile_position=(0, 32 * (h % 4)),
                                        skip_group_check=True)
                    if kind == "fox":
                        pe.wait_ge(s["den_ready"], b + 1)
                        for h in range(HA):
                            q = 32 * (h % 4)
                            ins = pe.matmul(ps[q:q + NEW, 4, P + h // 4:P + h // 4 + 1],
                                            small[:, 40 + h * NEW:40 + (h + 1) * NEW], ones[:, 0:1],
                                            start=True, stop=True, tile_position=(0, q),
                                            skip_group_check=True)
                    ins.then_inc(s["pv_done"], 1)

                def sequence(b, before=None):
                    turn_blocks(b, range(0, 5))
                    if before is not None:
                        fold_first(before)
                    turn_blocks(b, range(5, 7))
                    score(b, 0)
                    if before is not None:
                        fold(before)
                    turn_blocks(b, range(7, 10))
                    turn_rows(b, 0)
                    turn_blocks(b, range(10, 12))
                    score(b, 1)
                    turn_blocks(b, range(12, 15))
                    if before is not None:
                        weigh(before, 0)
                    turn_rows(b, 1)
                    turn_blocks(b, range(15, 17))
                    score(b, 2)
                    turn_blocks(b, range(17, 20))
                    if before is not None:
                        weigh(before, 1)
                    turn_rows(b, 2)
                    score(b, 3)
                    if before is not None:
                        weigh(before, 2)
                    turn_rows(b, 3)
                    turn_rows(b, 4)
                    if before is not None:
                        weigh(before, 3)

                sequence(0)
                with pe.Fori(1, SEQS) as b:
                    sequence(b, b - 1)
                fold_first(SEQS - 1)
                fold(SEQS - 1)
                for g in range(GROUPS):
                    weigh(SEQS - 1, g)
                phase_over(pe, phase)

            with pe.Fori(0, DEPTH) as L:
                norm(NORM1)
                project(PROJ_R)
                retention()
                project(PROJ_S)
                attention(ATT_S)
                decode(DEC_S, L)
                project(PROJ_F)
                attention(ATT_F)
                decode(DEC_F, L)
                for t in range(TILES):
                    R = rows(t)
                    if t >= 2:
                        pe.wait_ge(mixed_out, t - 1)
                    for k in range(KC):
                        ins = pe.transpose(ps[:, 2 * (t % 2) + k // 4, (k % 4) * P:(k % 4) * P + R],
                                           O[0:R, t, k * P:(k + 1) * P], ident[0:R, 0:R])
                    ins.then_inc(mixed_turned, 1)
                phase_over(pe, MIXED)
                project(OUT)
                norm(NORM2)
                pe.wait_ge(p_in, 32)
                for t in range(TILES):
                    R = rows(t)
                    if t >= 2:
                        pe.wait_ge(p_out, t - 1)
                    for k in range(2):
                        ins = pe.transpose(ps[:, 3 + t % 2, k * P:k * P + R],
                                           p_nat[0:R, t, k * P:(k + 1) * P], ident[0:R, 0:R])
                    ins.then_inc(p_turned, 1)
                phase_over(pe, PLE_T)
                project(GATED)
                layer_over(pe, L)

        @block.scalar
        def _(act):
            act.wait_ge(consts_in, 32)
            act.wait_ge(set_up, 3)
            act.wait_ge(x_in, 32)

            def norm(phase):
                for t in range(TILES):
                    m, R = NORMS[phase] * TILES + t, rows(t)
                    act.activation(junk[0:R], O[0:R, t, :], ACT.Square, accum_out=small[0:R, 200 + t:201 + t])\
                        .then_inc(squared, 1)
                    act.wait_ge(squared, m + 1)
                    act.activation(small[0:R, 210 + t:211 + t], small[0:R, 200 + t:201 + t], ACT.Sqrt,
                                   bias=eps[0:R], scale=1.0 / D).then_inc(rooted, 1)
                phase_over(act, phase)

            def turned_to(seg, t):
                m, R = turn_index(seg, t), rows(t)
                act.wait_ge(turned, m + 1)
                bank = 3 + 2 * (m % 2)
                if seg[0] == "f":
                    dst = qT_f if seg == "fq" else kT_f
                    ins = act.activation(
                        dst[0:HD + 1, :, t * P:(t + 1) * P],
                        bank2(bank, HA * P)[0:HD + 1].rearrange("p (h n) -> p h n", h=HA), ACT.Copy)
                elif seg[0] == "r":
                    dst = qT_r if seg == "rq" else kT_r
                    ins = act.activation(
                        dst[:, :, t * P:t * P + R],
                        ps[:, bank, 0:QP * P].rearrange("p (c n) -> p c n", c=QP)[:, :, 0:R], ACT.Copy)
                else:
                    dst = qT_s if seg == "sq" else kT_s
                    src = ps[:, bank, 0:QP * P].rearrange("p (c n) -> p c n", c=QP)
                    act.activation(dst[:, 0:2, t * P:(t + 1) * P], src[:, 0:2], ACT.Copy)
                    ins = act.activation(dst[0:HD, 2, t * P:(t + 1) * P], src[0:HD, 2], ACT.Copy)
                ins.then_inc(turned_out, 1)

            def project(phase, L):
                for seg in PROJ_SEGS[phase]:
                    i = ALL_SEGS.index(seg)
                    for t in range(TILES):
                        n, R, N = i * TILES + t, rows(t), SEG_W.get(seg, 512)
                        src = ps[0:R, n % 3, 0:N]
                        if seg in GATE_AT:
                            act.wait_ge(proj_ready, n + 1)
                            w = DR if seg == "rg" else DA
                            act.activation(O[0:R, t, GATE_AT[seg]:GATE_AT[seg] + w], src[:, 0:w], ACT.Sigmoid)\
                                .then_inc(sigmoid_ready, 1)
                        elif seg in ("rv", "sv", "fv"):
                            act.wait_ge(proj_ready, n + 1)
                            dst = v_r[0:R, t] if seg == "rv" else v_new[:] if t == SAMPLE else \
                                (v_s if seg == "sv" else v_f)[:, t]
                            act.activation(dst, src, ACT.Copy).then_inc(emptied_act, 1)
                        elif seg in ("sq", "sk"):
                            act.wait_ge(proj_ready, n + 1)
                            m = turn_index(seg, t)
                            scale = HD ** -0.5 if seg == "sq" else 1.0
                            if t == SAMPLE:
                                dst = q_new[:, 0:DA] if seg == "sq" else k_new[:]
                                if seg == "sq":
                                    act.activation(q_new[:, DA:DA + HD], src[:, 0:HD], ACT.Copy, scale=scale)
                            else:
                                dst = nat[:, m % 2, 0:DA]
                                act.wait_ge(turned, m - 1)
                                if seg == "sk" and t >= 2:
                                    act.wait_ge(k_saved[t % 2], L * 16 * (10, 8)[t % 2] + 16 * (t // 2))
                            act.activation(dst, src, ACT.Copy, scale=scale).then_inc(emptied_act, 1)
                        elif seg in ("fq", "fk"):
                            act.wait_ge(proj_ready, n + 1)
                            m = turn_index(seg, t)
                            if not (seg == "fq" and t < 2) and t < SAMPLE:
                                act.wait_ge(turned, m - 1)
                            if t == SAMPLE:
                                act.wait_ge(turned, m - 1)
                            if seg == "fk":
                                if t == 0:
                                    act.wait_ge(nat_ready, nat_count("fq", SAMPLE))
                                if t >= 2:
                                    act.wait_ge(k_saved[t % 2], L * 16 * (10, 8)[t % 2] + 16 * ((5, 4)[t % 2] + t // 2))
                            act.activation(aug[0:R, m % 2, :, 0:HD], src.rearrange("p (h d) -> p h d", h=HA),
                                           ACT.Copy).then_inc(emptied_act, 1)
                            u = (0 if seg == "fq" else TILES) + t
                            act.wait_ge(head_sums, u + 1)
                            act.activation(small[0:R, 10:15], small[0:R, 5:10], ACT.Sqrt, bias=eps[0:R],
                                           scale=1.0 / HD).then_inc(head_roots, 1)
                        elif seg[:2] == "pg":
                            act.wait_ge(proj_ready, n + 1)
                            if seg == "pg1":
                                act.wait_ge(emptied_dve, evac_count("pe0", t))
                            act.activation(gate[0:R, t, :], src, ACT.Sigmoid).then_inc(emptied_act, 1)
                        if t >= 1 and t - 1 < TURNED.get(seg, 0):
                            turned_to(seg, t - 1)
                    if TURNED.get(seg, 0) == TILES:
                        turned_to(seg, TILES - 1)
                    if seg == "fg":
                        act.wait_ge(logit_ready, 1)
                        act.activation(ltmp, ltmp, ACT.Exp).then_inc(logf_act, 1)
                        act.wait_ge(logf_act, 1)
                        act.activation(ltmp, ltmp, ACT.Ln, bias=1.0).then_inc(logf_act, 1)
                phase_over(act, phase)

            def retention():
                for t in range(TILES):
                    R = rows(t)
                    act.wait_ge(centred_r, t + 1)
                    act.activation(ret_sq[0:R], ret_o[0:R], ACT.Square).then_inc(squares_r, 1)
                    act.wait_ge(sums_r, t + 1)
                    act.activation(small[0:R, 20:26], small[0:R, 30:36], ACT.Sqrt, bias=eps[0:R],
                                   scale=1.0 / HD).then_inc(roots_r, 1)
                phase_over(act, RET)

            def attention(phase):
                kind = KIND[phase]

                def first(u):
                    t, h = UNITS[u]
                    n = (t + 1) * P
                    if kind == "sb":
                        act.wait_ge(att_scores[kind], u + 1)
                        if u >= 2:
                            act.wait_ge(att_probs[kind], u - 1)
                        act.activation(sig[:, u % 2, 0:n], bank2(2 * (u % 2), n), ACT.Sigmoid)\
                            .then_inc(att_first[kind], 1)
                    else:
                        act.wait_ge(att_max, u + 1)
                        if u >= 2:
                            act.wait_ge(att_turned[kind], u - 1)
                        if h == 0 and t >= 2:
                            act.wait_ge(att_done[kind], t - 1)
                        act.activation(expd[:, u % 2, 0:n], bank2(2 * (u % 2), n), ACT.Exp,
                                       bias=small[:, 40 + u % 4:41 + u % 4],
                                       accum_out=small[:, 50 + (t % 2) * HA + h:51 + (t % 2) * HA + h])\
                            .then_inc(att_first[kind], 1)

                def to_sbuf(u):
                    t, h = UNITS[u]
                    act.wait_ge(att_turned[kind], u + 1)
                    if u >= 2:
                        act.wait_ge(att_out[kind], u - 1)
                    n = (t + 1) * P
                    act.activation(attT[:, u % 2, 0:n], bank2(4, n), ACT.Copy).then_inc(attT_ready[kind], 1)

                first(0)
                for u in range(len(UNITS)):
                    if u + 1 < len(UNITS):
                        first(u + 1)
                    to_sbuf(u)
                phase_over(act, phase)

            def decode(phase):
                kind = KIND[phase]
                s = dec[kind]

                def take_blocks(b, blocks):
                    for n in blocks:
                        act.wait_ge(s["kt_ready"], b * BLOCKS + n + 1)
                        if n >= SLOTS:
                            act.wait_ge(s["scores_done"], b * GROUPS + (n - SLOTS) // 5 + 1)
                        elif not isinstance(b, int):
                            act.wait_ge(s["scores_done"], b * GROUPS + (n - SLOTS + BLOCKS) // 5 + 1 - GROUPS)
                        act.activation(kT_d[:, n % SLOTS, :], ps[:, n % 2, :], ACT.Copy).then_inc(s["kt_act"], 1)

                def take_rows(b, j):
                    act.wait_ge(s["scores_done"], b * GROUPS + min(j, 3) + 1)
                    if not isinstance(b, int) or 2 <= j < 4:
                        act.wait_ge(s["z_turned"], 5 * b + (j - 1 if 2 <= j < 4 else (j - 1 if j < 2 else 0)))
                    act.activation(z_rows[:, 2 if j == 4 else j % 2, :],
                                   ps[:, 3 if j == 4 else (5 if j % 2 else 2), :], ACT.Copy)\
                        .then_inc(s["rows_out"], 1)

                def soften(b):
                    if kind == "sb":
                        act.wait_ge(s["soft_in"], b + 1)
                        act.activation(soft, soft, ACT.Exp).then_inc(s["soft_act"], 1)
                        act.wait_ge(s["soft_act"], b * 2 + 1)
                        act.activation(soft, soft, ACT.Ln, bias=1.0).then_inc(s["soft_act"], 1)

                def exponentiate(b):
                    act.wait_ge(s["soft_ready"], b + 1)
                    act.wait_ge(s["o_emptied"], b + 1)
                    act.activation(probs, zs, ACT.Exp).then_inc(s["probs_ready"], 1)

                def sequence(b, before=None):
                    if before is not None:
                        soften(before)
                    take_blocks(b, range(0, 7))
                    take_rows(b, 0)
                    take_blocks(b, (8,))
                    if before is not None:
                        exponentiate(before)
                    take_blocks(b, (10, 12))
                    take_rows(b, 1)
                    take_blocks(b, (14, 16))
                    take_rows(b, 2)
                    take_blocks(b, (18,))
                    take_rows(b, 3)
                    take_rows(b, 4)

                sequence(0)
                with act.Fori(1, SEQS) as b:
                    sequence(b, b - 1)
                soften(SEQS - 1)
                exponentiate(SEQS - 1)
                phase_over(act, phase)

            with act.Fori(0, DEPTH) as L:
                norm(NORM1)
                project(PROJ_R, L)
                retention()
                project(PROJ_S, L)
                attention(ATT_S)
                decode(DEC_S)
                project(PROJ_F, L)
                attention(ATT_F)
                decode(DEC_F)
                for t in range(1, TILES, 2):
                    R = rows(t)
                    act.wait_ge(mixed_turned, t + 1)
                    act.wait_ge(mixed_out, t)
                    act.activation(xT[:, :, t * P:t * P + R],
                                   bank2(2 * (t % 2)).rearrange("p (k n) -> p k n", k=KC)[:, :, 0:R],
                                   ACT.Copy).then_inc(mixed_out, 1)
                phase_over(act, MIXED)
                project(OUT, L)
                norm(NORM2)
                for t in range(TILES):
                    R = rows(t)
                    act.wait_ge(p_turned, t + 1)
                    act.activation(pT[:, :, t * P:t * P + R],
                                   ps[:, 3 + t % 2, 0:2 * P].rearrange("p (k n) -> p k n", k=2)[:, :, 0:R],
                                   ACT.Copy).then_inc(p_out, 1)
                phase_over(act, PLE_T)
                project(GATED, L)
                layer_over(act, L)

        @block.vector
        def _(dve):
            dve.wait_ge(consts_in, 32)
            dve.wait_ge(set_up, 3)
            dve.wait_ge(x_in, 32)
            link = Steps(dve, steps_sem)

            def bc(ap, shape):
                return ap.unsqueeze(len(shape) - 1).broadcast_to(shape)

            def norm(phase):
                def scale(t):
                    m, R = NORMS[phase] * TILES + t, rows(t)
                    dve.wait_ge(rooted, m + 1)
                    link(dve.reciprocal(small[0:R, 220 + t:221 + t], small[0:R, 210 + t:211 + t]))
                    if m >= 2:
                        dve.wait_ge(norm_turned, m - 1)
                    dve.tensor_scalar(scaled[0:R, m % 2, :], O[0:R, t, :], small[0:R, 220 + t:221 + t], None,
                                      ALU.mult).then_inc(scaled_ready, 1)

                def out(t):
                    m, R = NORMS[phase] * TILES + t, rows(t)
                    dve.wait_ge(norm_turned, m + 1)
                    dve.tensor_tensor(xT[:, :, t * P:t * P + R],
                                      bank2(2 * (m % 2)).rearrange("p (k n) -> p k n", k=KC)[:, :, 0:R],
                                      bc(gT[:, NORMS[phase], :], [P, KC, R]), ALU.mult).then_inc(norm_out, 1)

                for t in range(TILES):
                    scale(t)
                    if t >= 1:
                        out(t - 1)
                out(SAMPLE)
                phase_over(dve, phase)

            def project(phase):
                for seg in PROJ_SEGS[phase]:
                    i = ALL_SEGS.index(seg)
                    if seg == "fg":
                        link(dve.memset(logit, 0.0))
                        link(dve.memset(logf_padded[:, 0:NT - 1], 0.0))
                    for t in range(TILES):
                        n, R = i * TILES + t, rows(t)
                        src = ps[0:R, n % 3, :]
                        if seg in ("rq", "rk"):
                            m = turn_index(seg, t)
                            new = t == SAMPLE
                            xh = src[:, 0:DR].rearrange("p (h c d) -> p h c d", h=HR, c=2)
                            ra = rot_a[0:R].rearrange("p (h d) -> p h d", h=HR)
                            rb = rot_b[0:R].rearrange("p (h c d) -> p h c d", h=HR, c=2)
                            cosb = cos_t[0:R, t, :].unsqueeze(1).broadcast_to([R, HR, HD])
                            dve.wait_ge(proj_ready, n + 1)
                            link(dve.tensor_tensor(ra, src[:, 0:DR].rearrange("p (h d) -> p h d", h=HR), cosb,
                                                   ALU.mult))
                            sinb = sin_t[0:R, t, :].rearrange("p (c d) -> p c d", c=2)
                            for c in range(2):
                                ins = dve.tensor_tensor(rb[:, :, c, :], xh[:, :, 1 - c, :],
                                                        sinb[:, c, :].unsqueeze(1).broadcast_to([R, HR, HD // 2]),
                                                        ALU.mult)
                                ins.then_inc(*((emptied_dve, 1) if c else (steps_sem, 1)))
                            link.n += 1
                            dve.wait_ge(steps_sem, link.base + link.n)
                            dve.wait_ge(emptied_dve, evac_count(seg, t))
                            if m >= 2:
                                dve.wait_ge(turned, m - 1)
                            dve.tensor_tensor(nat[0:R, m % 2, :], rot_a[0:R], rot_b[0:R], ALU.add)\
                                .then_inc(nat_ready, 1)
                            dve.wait_ge(nat_ready, nat_count(seg, t))
                            if seg == "rk":
                                decay = const("key_decay_new" if new else "key_decay")
                                link(dve.tensor_tensor(
                                    kd_r[0:R, t].rearrange("p (h d) -> p h d", h=HR),
                                    nat[0:R, m % 2, :].rearrange("p (h d) -> p h d", h=HR),
                                    bc(decay[0:R], [R, HR, HD]), ALU.mult))
                        elif seg in GATE_AT:
                            w = DR if seg == "rg" else DA
                            gates = {"rg": 0, "sg": 1, "fg": 2}[seg]
                            dve.wait_ge(proj_ready, n + 1)
                            dve.wait_ge(sigmoid_ready, gates * TILES + t + 1)
                            if seg == "fg":
                                link(dve.tensor_tensor(logit[0:R, t, :], src[:, DA:DA + HA], b_f_b[0:R], ALU.add))
                            out = O[0:R, t, GATE_AT[seg]:GATE_AT[seg] + w]
                            dve.tensor_tensor(out, out, src[:, 0:w], ALU.mult).then_inc(emptied_dve, 1)
                        elif seg in ("fq", "fk"):
                            m = turn_index(seg, t)
                            dve.wait_ge(emptied_act, evac_count(seg, t))
                            x = aug[0:R, m % 2, :, 0:HD]
                            link(dve.tensor_tensor(squares[0:R], x, x, ALU.mult))
                            dve.tensor_reduce(small[0:R, 5:10], squares[0:R], AX, ALU.add).then_inc(head_sums, 1)
                            last = aug[0:R, m % 2, :, HD:HD + 1]
                            if seg == "fq":
                                link(dve.memset(last, 1.0))
                            else:
                                link(dve.tensor_copy(last, neg_c[0:R, t, :].unsqueeze(2)))
                            u = (0 if seg == "fq" else TILES) + t
                            dve.wait_ge(head_roots, u + 1)
                            link(dve.reciprocal(small[0:R, 15:20], small[0:R, 10:15]))
                            link(dve.tensor_tensor(x, x, bc(small[0:R, 15:20], [R, HA, HD]), ALU.mult))
                            g = (g_fq_b if seg == "fq" else g_fk_b)[0:R].unsqueeze(1).broadcast_to([R, HA, HD])
                            if t < SAMPLE:
                                dst = x
                            else:
                                dst = (q_new[:, 0:DA] if seg == "fq" else k_new[:]).rearrange("p (h d) -> p h d", h=HA)
                            if t == SAMPLE and seg == "fq":
                                link(dve.tensor_tensor(q_new[:, DA:DA + HD], x[:, 0, :], g_fq_b[0:R], ALU.mult))
                            dve.tensor_tensor(dst, x, g, ALU.mult).then_inc(nat_ready, 1)
                            dve.wait_ge(nat_ready, nat_count(seg, t))
                        elif seg[:3] == "out":
                            m = (i - ALL_SEGS.index("out0")) * TILES + t
                            c = int(seg[-1])
                            dve.wait_ge(proj_ready, n + 1)
                            dve.wait_ge(x_half_in[m % 2], 16 * (m // 2 + 1))
                            dve.tensor_tensor(O[0:R, t, c * 512:(c + 1) * 512], src, x_half[0:R, m % 2, :], ALU.add)\
                                .then_inc(emptied_dve, 1)
                        elif seg[:2] == "pe":
                            c = int(seg[-1])
                            dve.wait_ge(proj_ready, n + 1)
                            dve.wait_ge(emptied_act, evac_count("pg" + seg[-1], t))
                            dve.tensor_tensor(gated[0:R, t % 2, :], src, gate[0:R, t, :], ALU.mult)\
                                .then_inc(emptied_dve, 1)
                            dve.wait_ge(emptied_dve, evac_count(seg, t))
                            out = O[0:R, t, c * 512:(c + 1) * 512]
                            link(dve.tensor_tensor(out, out, gated[0:R, t % 2, :], ALU.add))
                    if seg == "fg":
                        dve.scalar_tensor_tensor(ltmp, logit, -1.0, logit, ALU.mult, ALU.min).then_inc(logit_ready, 1)
                        dve.wait_ge(logf_act, 2)
                        dve.scalar_tensor_tensor(logf, logit, 0.0, ltmp, ALU.min, ALU.subtract)\
                            .then_inc(logf_ready, 1)
                        dve.wait_ge(cum_ready, 1)
                        link(dve.tensor_copy(neg_c[:, 0:NT, :], ps[:, 7, 0:NT * HA].rearrange(
                            "p (t h) -> p t h", h=HA)))
                        link(dve.tensor_copy(neg_c[0:ROWS, SAMPLE, :], ps[0:ROWS, 7, 64:64 + HA]))
                phase_over(dve, phase)

            def retention():
                def mask(t, h):
                    u, R, new = t * HR + h, rows(t), t == SAMPLE
                    dve.wait_ge(scores_r, u + 1)
                    if u >= 2:
                        dve.wait_ge(inner_r, u - 1)
                    grow = const("col_grow_new" if new else "col_grow")[0:R, h:h + 1]
                    upto = const("upto_new" if new else "upto")[0:R, 0:R]
                    dve.scalar_tensor_tensor(masked[0:R, u % 2, 0:R], ps[0:R, u % 2, 0:R], grow, upto, ALU.mult,
                                             ALU.mult).then_inc(masked_r, 1)

                def update(t):
                    dve.wait_ge(kv_r, t + 1)
                    kv = ps[:, 4 + t % 2, 0:QP * P].rearrange("p (c n) -> p c n", c=QP)
                    if t > 0:
                        dve.wait_ge(state_r, t)
                        link(dve.tensor_tensor(state, state, bc(const("chunk_decay"), [P, QP, HD]), ALU.mult))
                    for h2 in range(2):
                        q = slice(h2 * HD, (h2 + 1) * HD)
                        mine = kv[q, :, h2 * HD:(h2 + 1) * HD]
                        if t > 0:
                            ins = dve.tensor_tensor(state[q], state[q], mine, ALU.add)
                        else:
                            ins = dve.tensor_copy(state[q], mine)
                        if h2 == 0:
                            link(ins)
                    ins.then_inc(state_r, 1)

                def group_norm(t):
                    R, new = rows(t), t == SAMPLE
                    dve.wait_ge(inner_r, HR * (t + 1))
                    grow = const("row_grow_new" if new else "row_grow")
                    o = ret_o[0:R]
                    if new:
                        out = ps[0:R, 2, 0:DR].rearrange("p (h d) -> p h d", h=HR)
                        link(dve.tensor_tensor(o, out, ret_sq[0:R], ALU.add))
                        dve.tensor_tensor(o, o, bc(grow[0:R], [R, HR, HD]), ALU.mult).then_inc(ret_emptied, 1)
                    else:
                        for h2 in range(2):
                            out = ps[:, 2 + t % 2 + 4 * h2, 0:QP * HD].rearrange("p (c d) -> p c d", c=QP)
                            ins = dve.tensor_tensor(
                                o.rearrange("p (c a) d -> p c a d", a=2)[:, :, h2, :], out,
                                bc(grow.rearrange("p (c a) -> p c a", a=2)[:, :, h2], [P, QP, HD]), ALU.mult)
                            if h2 == 0:
                                link(ins)
                        ins.then_inc(ret_emptied, 1)
                    dve.wait_ge(ret_emptied, t + 1)
                    link(dve.tensor_reduce(small[0:R, 36:42], o, AX, ALU.add))
                    link(dve.tensor_scalar(small[0:R, 36:42], small[0:R, 36:42], 1.0 / HD, None, ALU.mult))
                    dve.tensor_tensor(o, o, bc(small[0:R, 36:42], [R, HR, HD]), ALU.subtract).then_inc(centred_r, 1)
                    dve.wait_ge(squares_r, t + 1)
                    dve.tensor_reduce(small[0:R, 30:36], ret_sq[0:R], AX, ALU.add).then_inc(sums_r, 1)
                    dve.wait_ge(roots_r, t + 1)
                    link(dve.reciprocal(small[0:R, 42:48], small[0:R, 20:26]))
                    link(dve.tensor_tensor(o, o, bc(small[0:R, 42:48], [R, HR, HD]), ALU.mult))
                    mixed = O[0:R, t, 0:DR]
                    link(dve.tensor_tensor(mixed, mixed, g_ret_b[0:R], ALU.mult))
                    link(dve.tensor_tensor(mixed, mixed, o.rearrange("p h d -> p (h d)"), ALU.mult))

                for t in range(NT):
                    for h in range(HR):
                        mask(t, h)
                    update(t)
                    group_norm(t)
                for h in range(HR):
                    mask(SAMPLE, h)
                own = const("own_seq")[0:ROWS]
                for h in range(HR):
                    dve.wait_ge(cross_ready, h + 1)
                    dve.tensor_tensor(cross[0:ROWS], ps[0:ROWS, 6 + h % 2, :].rearrange("p (b e) -> p b e", b=SEQS),
                                      bc(own, [ROWS, SEQS, HD]), ALU.mult).then_inc(cross_emptied, 1)
                    dve.wait_ge(cross_emptied, h + 1)
                    link(dve.tensor_reduce(ret_sq[0:ROWS, h, :], cross[0:ROWS].rearrange("p b e -> p e b"), AX,
                                           ALU.add))
                group_norm(SAMPLE)
                for h in range(HR):
                    pr, q = h // 2, slice((h % 2) * HD, (h % 2) * HD + HD)
                    if h >= 2:
                        dve.wait_ge(new_state_ready, h - 1)
                    dve.tensor_tensor(v_seq[0:ROWS, h % 2, :].rearrange("p (b e) -> p b e", b=SEQS),
                                      v_r[0:ROWS, SAMPLE, h * HD:(h + 1) * HD].unsqueeze(1).broadcast_to(
                                          [ROWS, SEQS, HD]),
                                      bc(own, [ROWS, SEQS, HD]), ALU.mult).then_inc(v_seq_ready, 1)
                    dve.wait_ge(new_state_ready, h + 1)
                    mine = s0[q, pr].rearrange("p b e -> p (b e)")
                    dve.scalar_tensor_tensor(mine, mine, const("chunk_decay_new")[q, pr:pr + 1],
                                             ps[q, 4 + h % 2, :], ALU.mult, ALU.add).then_inc(new_state_out, 1)
                phase_over(dve, RET)

            def attention(phase):
                kind = KIND[phase]
                if kind == "sb":
                    link(dve.memset(prod[:, SEQ:SEQ + 1], 1.0))

                def stick(u):
                    t, h = UNITS[u]
                    n = (t + 1) * P
                    s = sig[:, u % 2, 0:n]
                    r, e = rest[:, 0:n], SEQ - n
                    dve.wait_ge(att_first[kind], u + 1)
                    link(dve.tensor_tensor(s[:, t * P:n], s[:, t * P:n], const("before"), ALU.mult))
                    link(dve.tensor_scalar(r, s, -1.0, 1.0, ALU.mult, ALU.add))
                    dve.wait_ge(att_probs[kind], u)
                    link(dve.tensor_tensor_scan(prod[:, e:SEQ][:, ::-1], r[:, ::-1], r[:, ::-1], 1.0, ALU.mult,
                                                ALU.bypass))
                    if u >= 2:
                        dve.wait_ge(att_turned[kind], u - 1)
                    dve.tensor_tensor(att[:, u % 2, 0:n], s, prod[:, e + 1:SEQ + 1], ALU.mult)\
                        .then_inc(att_probs[kind], 1)

                def largest(u):
                    t, h = UNITS[u]
                    n = (t + 1) * P
                    dve.wait_ge(att_scores[kind], u + 1)
                    diag = bank2(2 * (u % 2), n)[:, t * P:n]
                    link(dve.tensor_tensor(diag, diag, const("after_neg"), ALU.add))
                    if u >= 4:
                        dve.wait_ge(att_first[kind], u - 3)
                    dve.tensor_reduce(small[:, 40 + u % 4:41 + u % 4], bank2(2 * (u % 2), n), AX, ALU.max,
                                      negate=True).then_inc(att_max, 1)

                def finish(t):
                    dve.wait_ge(att_out[kind], HA * (t + 1))
                    at = DR if kind == "sb" else DR + DA
                    out = O[:, t, at:at + DA]
                    o = ps[:, 6 + t % 2, 0:DA]
                    if kind == "fox":
                        link(dve.reciprocal(small[:, 60:65], small[:, 50 + (t % 2) * HA:50 + (t % 2 + 1) * HA]))
                        o3 = out.rearrange("p (h d) -> p h d", h=HA)
                        link(dve.tensor_tensor(o3, o3, bc(small[:, 60:65], [P, HA, HD]), ALU.mult))
                    dve.tensor_tensor(out, out, o, ALU.mult).then_inc(att_done[kind], 1)

                for u, (t, h) in enumerate(UNITS):
                    (stick if kind == "sb" else largest)(u)
                    if h == 2 and t >= 1:
                        finish(t - 1)
                finish(NT - 1)
                phase_over(dve, phase)

            def forget_sums(L):
                for half in range(2):
                    dve.wait_ge(logf_in, 16 * (L + 1))
                    for h in range(HA):
                        x = page_logf[:, half, :, h][:, ::-1]
                        ins = dve.tensor_tensor_scan(page_sum[:, half, h, :][:, ::-1], ones, x, 0.0, ALU.mult,
                                                     ALU.add)
                        if h < HA - 1:
                            link(ins)
                    ins.then_inc(page_ready, 1)
                    dve.wait_ge(page_ready, half + 1)
                    dve.wait_ge(page_carry, half + 1)
                    link(dve.tensor_tensor(page_sum[:, half], page_sum[:, half],
                                           page_logf[:, half].rearrange("p s h -> p h s"), ALU.subtract))
                    dve.tensor_tensor(page_sum[:, half], page_sum[:, half],
                                      bc(ps[:, 6 + half, 0:HA], [P, HA, P]), ALU.add).then_inc(forget_part, 1)
                for h in range(HA):
                    dve.wait_ge(forget_turned, h + 1)
                    dve.tensor_copy(forget[:, h, :], ps[:, h % 2, 0:2 * P]).then_inc(forget_ready, 1)

            def decode(phase, L):
                kind = KIND[phase]
                s = dec[kind]
                if kind == "fox":
                    forget_sums(L)
                link(dve.memset(qd, 0.0))
                link(dve.memset(kT_new, 0.0))
                link(dve.memset(row_max[:], 0.0))
                link(dve.memset(q_now, 0.0))
                dve.memset(ps[:, 4, :], 1.0).then_inc(s["o_emptied"], 1)
                dve.wait_ge(s["o_emptied"], 1)
                zr = zs.rearrange("p (r s) -> p r s", s=SLOT)
                z4 = zs.rearrange("p (h i s) -> p h i s", h=HA, i=NEW)
                link(dve.memset(zr[ROWS:P, :, PAGES:SLOT], NEG))
                neg = const("new_neg_" + kind, SEQS, NEW)[0:ROWS]
                for h in range(HA):
                    link(dve.tensor_copy(new_bias[0:ROWS, :, h, :], neg))
                if kind == "fox":
                    for h in range(HA):
                        link(dve.tensor_scalar(new_bias[0:ROWS, :, h, :], new_bias[0:ROWS, :, h, :],
                                               neg_c[0:ROWS, SAMPLE, h:h + 1], None, ALU.add))
                dve.wait_ge(s["new_turned"], 1)
                qsrc = ps[:, 0, 0:5 * ROWS].rearrange("p (c b i) -> p b c i", c=5, b=SEQS)
                link(dve.tensor_copy(qd[0:HD, :, :, 0:NEW], qsrc[0:HD]))
                link(dve.tensor_copy(qd[HD:P, :, :, NEW:2 * NEW], qsrc[HD:P]))
                link(dve.tensor_copy(kT_new[:, 0:2, :], ps[:, 1, 0:2 * ROWS].rearrange("p (c n) -> p c n", c=2)))
                dve.tensor_copy(kT_new[0:HD, 2, :], ps[0:HD, 1, 2 * ROWS:3 * ROWS]).then_inc(s["new_ready"], 1)

                dve.wait_ge(s["new_ready"], 1)
                dve.wait_ge(s["new_scored"], 1)
                new_z = ps[0:ROWS, 2, 0:3 * P].rearrange("p (c b x) -> p b c x", c=3, b=SEQS)
                new_rows = new_bias[0:ROWS].rearrange("p b h i -> p b (h i)")
                for c in range(3):
                    to = new_rows[:, :, 2 * NEW * c:min(HI, 2 * NEW * (c + 1))]
                    link(dve.tensor_tensor(to, to, new_z[:, :, c, 0:to.shape[2]], ALU.add))

                def queries(b, first=False):
                    if not first:
                        dve.wait_ge(s["scores_done"], b * GROUPS)
                    dve.tensor_copy(q_now[:, :, 0:2 * NEW], qd[:, b]).then_inc(s["q_ready"], 1)

                def take_blocks(b, blocks):
                    for n in blocks:
                        dve.wait_ge(s["kt_ready"], b * BLOCKS + n + 1)
                        if n >= SLOTS:
                            dve.wait_ge(s["scores_done"], b * GROUPS + (n - SLOTS) // 5 + 1)
                        elif not isinstance(b, int):
                            dve.wait_ge(s["scores_done"], b * GROUPS + (n - SLOTS + BLOCKS) // 5 + 1 - GROUPS)
                        dve.tensor_copy(kT_d[:, n % SLOTS, :], ps[:, n % 2, :]).then_inc(s["kt_dve"], 1)

                def drain(b, j):
                    dve.wait_ge(s["z_turned"], 5 * b + j + 1)
                    if j == 0 and not isinstance(b, int):
                        dve.wait_ge(s["probs_ready"], b)
                    by_pair = zr[:, :, 0:PAGES].rearrange("p r (g m two) -> p g r m two", g=GROUPS, two=2)
                    src = ps[:, 6 + j % 2, :].rearrange("p (m k r) -> p k r m", m=4, k=4)
                    if j == 4:
                        for g in range(GROUPS):
                            ins = dve.tensor_copy(by_pair[:, g, 3 * NEW:, :, 1], src[:, g, 0:2 * NEW])
                    else:
                        for kk in range(2):
                            dve.tensor_copy(by_pair[:, j, 2 * NEW * kk:2 * NEW * (kk + 1), :, 0],
                                            src[:, kk, 0:2 * NEW])
                        dve.tensor_copy(by_pair[:, j, 4 * NEW:, :, 0], src[:, 2, 0:NEW])
                        dve.tensor_copy(by_pair[:, j, 0:NEW, :, 1], src[:, 2, NEW:2 * NEW])
                        ins = dve.tensor_copy(by_pair[:, j, NEW:3 * NEW, :, 1], src[:, 3, 0:2 * NEW])
                    ins.then_inc(s["z_drained"], 1)

                def soften_first(b):
                    link(dve.tensor_copy(zr[0:ROWS, :, PAGES], new_rows[:, b]))
                    dve.wait_ge(s["z_drained"], 5 * b + 5)
                    if kind == "sb":
                        dve.scalar_tensor_tensor(soft, zs, -1.0, zs, ALU.mult, ALU.min).then_inc(s["soft_in"], 1)
                    else:
                        fb = forget[:, :, bass.ds(b * PAGES, PAGES)].unsqueeze(2).broadcast_to(
                            [P, HA, NEW, PAGES])
                        link(dve.tensor_tensor(z4[:, :, :, 0:PAGES], z4[:, :, :, 0:PAGES], fb, ALU.add))
                        dve.tensor_reduce(row_max[:, 0:HI], zr, AX, ALU.max).then_inc(s["soft_in"], 1)

                def soften(b):
                    if kind == "sb":
                        dve.wait_ge(s["soft_act"], 2 * b + 2)
                        link(dve.scalar_tensor_tensor(soft, zs, 0.0, soft, ALU.max, ALU.add))
                        dve.tensor_tensor_scan(later[:, ::-1], reset[:, ::-1], soft[:, ::-1], 0.0, ALU.mult,
                                               ALU.add).then_inc(s["sum_ready"], 1)
                    else:
                        dve.wait_ge(s["fold_ready"], b + 1)
                        link(dve.tensor_reduce(small[0:HI, 180:181], ps[0:HI, 6, 0:P], AX, ALU.max, negate=True))
                        dve.tensor_scalar(small[0:HI, 120:120 + HI], ident[0:HI, 0:HI], small[0:HI, 180:181], None,
                                          ALU.mult).then_inc(s["fold_out"], 1)

                def exponents(b):
                    if kind == "sb":
                        dve.wait_ge(s["expo_ready"], b + 1)
                        z3 = zs.rearrange("p (c n) -> p c n", c=3)
                        dve.tensor_tensor(z3, z3, ps[:, 5:8, 0:440], ALU.add).then_inc(s["soft_ready"], 1)
                    else:
                        dve.wait_ge(s["bias_ready"], b + 1)
                        dve.tensor_tensor(zr, zr, bc(ps[:, 6, P:P + HI], [P, HI, SLOT]), ALU.add)\
                            .then_inc(s["soft_ready"], 1)

                def denominators(b):
                    if kind == "fox":
                        dve.wait_ge(s["probs_ready"], b + 1)
                        dve.tensor_reduce(small[:, 40:40 + HI], probs.rearrange("p (r s) -> p r s", s=SLOT), AX,
                                          ALU.add).then_inc(s["den_ready"], 1)

                def take(b):
                    dve.wait_ge(s["pv_done"], b + 1)
                    o = ps[:, 4, 0:P].rearrange("p (a d) -> p a d", a=2)
                    if kind == "sb":
                        dve.tensor_copy(decoded[:, b], o).then_inc(s["o_emptied"], 1)
                    else:
                        link(dve.reciprocal(small[:, 182:184], ps[:, 4, P:P + 2]))
                        dve.tensor_tensor(decoded[:, b], o, bc(small[:, 182:184], [P, 2, HD]), ALU.mult)\
                            .then_inc(s["o_emptied"], 1)

                def sequence(b, before=None):
                    queries(b, before is None)
                    if before is not None:
                        soften(before)
                        exponents(before)
                    take_blocks(b, (7, 9))
                    drain(b, 0)
                    if before is not None:
                        denominators(before)
                    take_blocks(b, (11, 13))
                    drain(b, 1)
                    take_blocks(b, (15, 17))
                    drain(b, 2)
                    take_blocks(b, (19,))
                    drain(b, 3)
                    drain(b, 4)
                    soften_first(b)
                    if before is not None:
                        take(before)

                sequence(0)
                first = link.n - DECODE_STEPS[kind]
                with dve.Fori(1, SEQS) as b:
                    link.turn(b, DECODE_STEPS[kind], first)
                    sequence(b, b - 1)
                    assert link.n == DECODE_STEPS[kind], (kind, link.n)
                link.turn(SEQS, DECODE_STEPS[kind], first)
                soften(SEQS - 1)
                exponents(SEQS - 1)
                denominators(SEQS - 1)
                take(SEQS - 1)
                link.base, link.n = 0, link.base + link.n
                dve.wait_ge(s["loaded"], 16)
                at = DR if kind == "sb" else DR + DA
                out = O[0:ROWS, SAMPLE, at:at + DA]
                link(dve.tensor_tensor(out, out, work[0:ROWS, 0:DA], ALU.mult))
                phase_over(dve, phase)

            with dve.Fori(0, DEPTH) as L:
                link.base, link.n = 0, 0
                dve.wait_ge(vec_loaded, 6 * 16)
                link(dve.tensor_scalar(g_fq_b[:], g_fq_b[:], HD ** -0.5, None, ALU.mult))
                norm(NORM1)
                project(PROJ_R)
                retention()
                project(PROJ_S)
                attention(ATT_S)
                decode(DEC_S, L)
                project(PROJ_F)
                attention(ATT_F)
                decode(DEC_F, L)
                for t in range(0, TILES, 2):
                    R = rows(t)
                    dve.wait_ge(mixed_turned, t + 1)
                    if t >= 1:
                        dve.wait_ge(mixed_out, t)
                    dve.tensor_copy(xT[:, :, t * P:t * P + R],
                                    bank2(2 * (t % 2)).rearrange("p (k n) -> p k n", k=KC)[:, :, 0:R])\
                        .then_inc(mixed_out, 1)
                phase_over(dve, MIXED)
                project(OUT)
                norm(NORM2)
                phase_over(dve, PLE_T)
                project(GATED)
                layer_over(dve, L)


_INS = ["x_prompt", "x_sample", "state_ret", "cache_sb_k", "cache_sb_v", "cache_fox_k", "cache_fox_v",
        "cache_fox_logf", "page_table", "p_prompt", "p_sample", "g_norm", "w_in", "b_f", "g_ret_gn",
        "g_fox_q", "g_fox_k", "w_out", "w_pe", "g_pe", "w_pg"]
_OUTS = [(1, SEQ, D), (SEQS, NEW, D), (DEPTH, 1, HR, HD, HD), (DEPTH, SEQS, HR, HD, HD),
         (DEPTH, 1, SEQ, HA, HD), (DEPTH, 1, SEQ, HA, HD), (DEPTH, SEQS, NEW, HA, HD),
         (DEPTH, SEQS, NEW, HA, HD), (DEPTH, 1, SEQ, HA, HD), (DEPTH, 1, SEQ, HA, HD),
         (DEPTH, 1, SEQ, HA), (DEPTH, SEQS, NEW, HA, HD), (DEPTH, SEQS, NEW, HA, HD),
         (DEPTH, SEQS, NEW, HA)]


def kernel(**inputs):
    import concourse.bacc as _bacc
    from concourse import mybir as _mybir
    from concourse.bass_utils import run_bass_kernel_spmd as _run

    nc = _bacc.Bacc("TRN2", target_bir_lowering=False, num_devices=1)
    arrays, args = {}, []
    for name in _INS:
        a = np.ascontiguousarray(inputs[name])
        arrays[f"in_{name}_dram"] = a
        args.append(nc.dram_tensor(f"in_{name}_dram", a.shape, _mybir.dt.from_np(a.dtype),
                                   kind="ExternalInput").ap())
    consts = np.concatenate(list(tables().values()), axis=1)
    arrays["in_consts_dram"] = consts
    args.append(nc.dram_tensor("in_consts_dram", consts.shape, F32, kind="ExternalInput").ap())
    for i, shape in enumerate(_OUTS):
        args.append(nc.dram_tensor(f"out_{i}_dram", shape, F32, kind="ExternalOutput").ap())
    step_program(nc, *args)
    r = _run(nc, [arrays], core_ids=[0])
    return tuple(r.results[0][f"out_{i}_dram"] for i in range(len(_OUTS)))
```

```python
from contextlib import ExitStack

import numpy as np

import concourse.bass as bass
from concourse import mybir

F32 = mybir.dt.float32
BF16 = mybir.dt.bfloat16
I32 = mybir.dt.int32
ALU = mybir.AluOpType
ACT = mybir.ActivationFunctionType
AX = mybir.AxisListType.X

P = 128
D = 1024
KC = D // P
SEQ = 1024
NT = SEQ // P
SAMPLE = NT
TILES = NT + 1
DEPTH = 2
SEQS, NEW = 8, 8
ROWS = SEQS * NEW
HD = 64
HR, HA = 6, 5
DR, DA = HR * HD, HA * HD
PAGES = 32
PAST = PAGES * P
PLE = 256
EPS = 1e-6
NEG = -1e30
PG8 = 8
GROUPS = PAGES // PG8
HI = HA * NEW
SLOT = PAGES + 1
QP = HR // 2

SEG_NAMES = ["rq", "rk", "rv", "rg", "sq", "sk", "sv", "sg", "fg", "fq", "fk", "fv"]
SEG_COL = dict(rq=0, rk=DR, rv=2 * DR, rg=3 * DR, sq=4 * DR, sk=4 * DR + DA, sv=4 * DR + 2 * DA,
               sg=4 * DR + 3 * DA, fq=4 * DR + 4 * DA, fk=4 * DR + 5 * DA, fv=4 * DR + 6 * DA,
               fg=4 * DR + 7 * DA)
SEG_W = {s: DR if s[0] == "r" else DA for s in SEG_NAMES}
SEG_W["fg"] = DA + HA
ALL_SEGS = SEG_NAMES + ["out0", "out1", "pg0", "pe0", "pg1", "pe1"]
DVE_EVACUATES = {"rq", "rk", "rg", "sg", "fg", "out0", "out1", "pe0", "pe1"}
TURNED = {"rq": TILES, "rk": TILES, "sq": NT, "sk": NT, "fq": NT, "fk": NT}
GATE_AT = {"rg": 0, "sg": DR, "fg": DR + DA}


X_LOADS = [(0, 1), (1, 3), (3, 5), (5, NT), (NT, TILES)]
LOAD_OF = [next(i for i, (a, b) in enumerate(X_LOADS) if a <= t < b) for t in range(TILES)]


def rows(t):
    return ROWS if t == SAMPLE else P


def evac_count(seg, t):
    same = (seg in DVE_EVACUATES)
    before = [s for s in ALL_SEGS[:ALL_SEGS.index(seg)] if (s in DVE_EVACUATES) == same]
    return len(before) * TILES + t + 1


def turn_index(seg, t):
    return sum(n for s, n in TURNED.items() if ALL_SEGS.index(s) < ALL_SEGS.index(seg)) + t


def nat_count(seg, t):
    made = ["rq", "rk", "fq", "fk"]
    return TILES * made.index(seg) + t + 1


def tables():
    j, i = np.arange(P)[:, None], np.arange(P)[None, :]
    r = np.arange(P)
    log_g = np.log1p(-np.exp2(-5.0 - np.arange(HR)))
    inv = 10000.0 ** (-np.arange(HD // 2) / (HD // 2))
    pos = np.zeros((P, TILES))
    pos[:, :NT] = r[:, None] + P * np.arange(NT)[None, :]
    pos[:, SAMPLE] = PAST + r % NEW
    ang = pos[:, :, None].astype(np.float32) * inv.astype(np.float32)[None, None, :]
    ang = ang.astype(np.float64)
    b, k = r // NEW, r % NEW
    pair_head = 2 * np.arange(QP)[None, :] + (r // HD)[:, None]
    t = {}
    t["ident"] = np.eye(P)
    t["earlier"] = j < i
    t["negones"] = -np.ones((P, P))
    t["ones"] = np.ones((P, P))
    t["neg_upto"] = -1.0 * (j <= i)
    t["later_page"] = (j // PAGES == i // PAGES) & (j > i)
    t["neg_upto_new"] = (-1.0 * ((j // NEW == i // NEW) & (j <= i)))[:, :ROWS]
    t["cos"] = np.concatenate([np.cos(ang), np.cos(ang)], -1)
    t["sin"] = np.concatenate([-np.sin(ang), np.sin(ang)], -1)
    t["row_grow"] = np.exp((r[:, None] + 1.0) * log_g)
    t["col_grow"] = np.exp(-(r[:, None] + 1.0) * log_g) / 8
    t["key_decay"] = np.exp((P - 1.0 - r[:, None]) * log_g) / 8
    t["row_grow_new"] = np.exp((k[:, None] + 1.0) * log_g)
    t["col_grow_new"] = np.exp(-(k[:, None] + 1.0) * log_g) / 8
    t["key_decay_new"] = np.exp((NEW - 1.0 - k[:, None]) * log_g) / 8
    t["chunk_decay"] = np.exp(P * log_g)[pair_head]
    t["chunk_decay_new"] = np.exp(NEW * log_g)[pair_head]
    t["upto"] = j <= i
    t["upto_new"] = ((j // NEW == i // NEW) & (j <= i))[:, :ROWS]
    t["own_seq"] = b[:, None] == np.arange(SEQS)[None, :]
    t["before"] = i < j
    t["after_neg"] = np.where(i > j, NEG, 0.0)
    q = np.arange(NEW)[None, None, :]
    same = b[:, None, None] == np.arange(SEQS)[None, :, None]
    t["new_neg_sb"] = np.where(same & (k[:, None, None] < q), 0.0, NEG)
    t["new_neg_fox"] = np.where(same & (k[:, None, None] <= q), 0.0, NEG)
    return {n: np.asarray(v, np.float32).reshape(P, -1) for n, v in t.items()}


def table_places():
    at, places = 0, {}
    for name, v in tables().items():
        places[name] = (at, v.shape[1])
        at += v.shape[1]
    return places, at


STORES = 2 + QP + TILES + 2 + TILES

BLOCKS = 5 * GROUPS
SLOTS = 8
BY_ACT = 4
DVE_BLOCKS = (2, 3, 11, 13, 15, 17, 19)

DECODE_STEPS = {"sb": 2, "fox": 4}


def taken(engine_blocks, b, n):
    if n < 0:
        b, n = b - 1, n + BLOCKS
    return b * len(engine_blocks) + sum(m <= n for m in engine_blocks)


def is_first(b):
    return isinstance(b, int) and b == 0


ACT_BLOCKS = tuple(n for n in range(BLOCKS) if n not in DVE_BLOCKS)


class Steps:

    def __init__(self, eng, sem):
        self.eng, self.sem, self.n, self.base = eng, sem, 0, 0

    def __call__(self, ins):
        self.n += 1
        ins.then_inc(self.sem, 1)
        self.eng.wait_ge(self.sem, self.base + self.n)

    def turn(self, b, per, first):
        self.base, self.n = b * per + first, 0


def step_program(nc, x_prompt, x_sample, state_ret, cache_sb_k, cache_sb_v, cache_fox_k,
                 cache_fox_v, cache_fox_logf, page_table, p_prompt, p_sample, g_norm, w_in, b_f,
                 g_ret_gn, g_fox_q, g_fox_k, w_out, w_pe, g_pe, w_pg, consts,
                 y_prompt, y_sample, rs_prompt, rs_sample, sbk_prompt, sbv_prompt, sbk_sample,
                 sbv_sample, foxk_prompt, foxv_prompt, foxl_prompt, foxk_sample, foxv_sample,
                 foxl_sample):
    n_pool = cache_sb_k.shape[1]
    residual_dram = nc.dram_tensor("residual_scratch", (TILES * P, D), F32, kind="Internal").ap()
    decoded_dram = nc.dram_tensor("decoded_scratch", (2, ROWS, DA), F32, kind="Internal").ap()
    logf_dram = nc.dram_tensor("logf_scratch", (SEQS * PAGES, P * HA), F32, kind="Internal").ap()
    places, n_consts = table_places()

    with ExitStack() as ctx:
        def sb(name, shape, dt=F32):
            return ctx.enter_context(nc.sbuf_tensor(name, shape, dt))

        def sem(name):
            return ctx.enter_context(nc.semaphore(name))

        xT = sb("xT", [P, KC, SEQ + ROWS])
        O = sb("O", [P, TILES, D])
        W = [sb(f"W{i}", [P, KC, 512]) for i in range(2)]
        C = sb("C", [P, n_consts])
        reset = sb("reset", [P, HI * SLOT], BF16)
        pages = sb("pages", [1, SEQS * PAGES], I32)
        gT = sb("gT", [P, 2, KC])
        g_ret_b = sb("g_ret_b", [P, DR])
        g_fq_b = sb("g_fq_b", [P, HD])
        g_fk_b = sb("g_fk_b", [P, HD])
        b_f_b = sb("b_f_b", [P, HA])
        eps = sb("eps", [P, 1])
        small = sb("small", [P, 256])
        row_max = sb("row_max", [P, P])
        q_new = sb("q_new", [ROWS, DA + HD])
        k_new = sb("k_new", [ROWS, DA])
        v_new = sb("v_new", [ROWS, DA])
        branch = sb("branch", [P, 15520])
        work = sb("work", [P, 5504])

        def cut(region, at, *shape):
            n = int(np.prod(shape))
            v = region[:, at:at + n]
            if len(shape) == 2:
                v = v.rearrange("p (a b) -> p a b", a=shape[0])
            if len(shape) == 3:
                v = v.rearrange("p (a b c) -> p a b c", a=shape[0], b=shape[1])
            if len(shape) == 4:
                v = v.rearrange("p (a b c d) -> p a b c d", a=shape[0], b=shape[1], c=shape[2])
            return v

        def const(name, *shape):
            at, n = places[name]
            return cut(C, at, *shape) if shape else C[:, at:at + n]

        ident = const("ident")
        ones = const("ones")
        cos_t, sin_t = const("cos", TILES, HD), const("sin", TILES, HD)

        TR = SEQ + ROWS
        qT_r, kT_r = cut(branch, 0, QP, TR), cut(branch, QP * TR, QP, TR)
        v_r = cut(branch, 2 * QP * TR, TILES, DR)
        kd_r = cut(branch, 2 * QP * TR + TILES * DR, TILES, DR)
        at = 2 * QP * TR + 2 * TILES * DR
        s0 = cut(branch, at, QP, SEQS, HD)
        states = cut(branch, at + QP * SEQS * HD, 2, QP, HD)
        qT_s, kT_s = cut(branch, 0, QP, SEQ), cut(branch, QP * SEQ, QP, SEQ)
        v_s = cut(branch, 2 * QP * SEQ, NT, DA)
        at = 2 * QP * SEQ + NT * DA
        sig = cut(branch, at, 2, SEQ)
        att = cut(branch, at + 2 * SEQ, 2, SEQ)
        rest = branch[:, at + 4 * SEQ:at + 5 * SEQ]
        prod = branch[:, at + 5 * SEQ:at + 6 * SEQ + 1]
        qT_f, kT_f = cut(branch, 0, HA, SEQ), cut(branch, HA * SEQ, HA, SEQ)
        v_f = cut(branch, 2 * HA * SEQ, NT, DA)
        junk = branch[:, 10000:10000 + D]
        scaled = cut(work, 3072, 2, D)
        nat = cut(work, 0, 2, DR)
        rot_a, rot_b = work[:, 768:768 + DR], work[:, 1152:1152 + DR]
        aug = cut(work, 1536, 2, HA, HD + 1)
        squares = cut(work, 2200, HA, HD)
        logit = cut(work, 2600, TILES, HA)
        ltmp = cut(work, 2650, TILES, HA)
        logf_padded = cut(work, 2700, NT - 1 + TILES, HA)
        logf = logf_padded[:, NT - 1:]
        neg_c = cut(small, 64, TILES, HA)
        masked = cut(work, 2560, 3, P)
        ret_o, ret_sq = cut(work, 256, HR, HD), cut(work, 640, HR, HD)
        cross = cut(work, 1024, SEQS, HD)
        v_seq = cut(work, 1536, 2, SEQS * HD)
        expd = cut(work, 0, 2, SEQ)
        attT = cut(work, 2 * SEQ, 2, SEQ)
        spare = W[1][:].rearrange("p k n -> p (k n)")
        ringK = [spare[:, 0:PG8 * DA], branch[:, 0:PG8 * DA]]
        kT_d = [branch[:, PG8 * DA + n * 512:PG8 * DA + (n + 1) * 512] for n in range(5)] + \
            [spare[:, PG8 * DA + n * 512:PG8 * DA + (n + 1) * 512] for n in range(SLOTS - 5)]
        ringV = cut(branch, 2 * PG8 * DA, 2, PG8 * DA)
        at = 4 * PG8 * DA
        NZ = HI * SLOT
        zs = branch[:, at:at + NZ]
        soft = branch[:, at + NZ:at + 2 * NZ]
        later = branch[:, at + 2 * NZ:at + 3 * NZ]
        probs = branch[:, at + 3 * NZ:at + 4 * NZ]
        z_rows = cut(work, 0, 3, 512)
        q_now = cut(work, 1536, 5, 32)
        qd = cut(work, 2048, SEQS, 5, 2 * NEW)
        kT_new = cut(work, 2688, 3, ROWS)
        decoded = cut(work, 2880, SEQS, 2, HD)
        forget = cut(work, 3904, HA, SEQS * PAGES)
        new_bias = cut(work, 5184, SEQS, HA, NEW)
        page_logf = cut(work, 4096, 2, P, HA)
        page_sum = cut(branch, 12800, 2, HA, P)
        decoded_rows = {"sb": work[0:ROWS, 3904:3904 + DA], "fox": work[0:ROWS, 2048:2048 + DA]}
        x_half = cut(work, 0, 2, 512)
        p_nat = cut(branch, 0, TILES, PLE)
        pT = cut(branch, TILES * PLE, 2, TR)
        gate = cut(branch, TILES * PLE + 2 * TR, TILES, 512)
        gated = cut(work, 1024, 2, 512)

        ps = ctx.enter_context(nc.psum_tensor("ps", [P, 8, 512], F32))

        arrived = sem("arrived")
        layer_go = sem("layer_go")
        consts_in = sem("consts_in")
        set_up = sem("set_up")
        x_in = [sem(f"x_in{i}") for i in range(len(X_LOADS))]
        y_out = sem("y_out")
        first_w = sem("first_w")
        x_saved = sem("x_saved")
        k_saved = [sem(f"k_saved{i}") for i in range(2)]
        saved = sem("saved")
        logf_gathered = sem("logf_gathered")
        logf_in = sem("logf_in")
        stored = {k: sem(f"stored_{k}") for k in ("sb", "fox")}
        v_in = {k: [sem(f"v_in{i}_{k}") for i in range(2)] for k in ("sb", "fox")}
        phase_sem = sem("phase_sem")
        w_loaded = [sem(f"w_loaded{i}") for i in range(2)]
        vec_loaded = sem("vec_loaded")
        pool_ready = sem("pool_ready")
        squared = sem("squared")
        rooted = sem("rooted")
        scaled_ready = sem("scaled_ready")
        norm_turned = sem("norm_turned")
        norm_out = sem("norm_out")
        proj_ready = sem("proj_ready")
        emptied_dve = sem("emptied_dve")
        emptied_act = sem("emptied_act")
        nat_ready = sem("nat_ready")
        turned = sem("turned")
        turned_out = sem("turned_out")
        sigmoid_ready = sem("sigmoid_ready")
        head_sums = sem("head_sums")
        head_roots = sem("head_roots")
        logit_ready = sem("logit_ready")
        logf_act = sem("logf_act")
        logf_ready = sem("logf_ready")
        cum_ready = sem("cum_ready")
        neg_c_ready = sem("neg_c_ready")
        scores_r = sem("scores_r")
        masked_r = sem("masked_r")
        inner_r = sem("inner_r")
        ret_emptied = sem("ret_emptied")
        kv_r = sem("kv_r")
        state_r = sem("state_r")
        centred_r = sem("centred_r")
        squares_r = sem("squares_r")
        sums_r = sem("sums_r")
        roots_r = sem("roots_r")
        state_in = sem("state_in")
        cross_ready = sem("cross_ready")
        cross_emptied = sem("cross_emptied")
        v_seq_ready = sem("v_seq_ready")
        new_state_ready = sem("new_state_ready")
        new_state_out = sem("new_state_out")
        att_scores = {k: sem(f"att_scores_{k}") for k in ("sb", "fox")}
        att_first = {k: sem(f"att_first_{k}") for k in ("sb", "fox")}
        att_probs = {"sb": sem("att_probs_sb")}
        att_max = sem("att_max")
        att_emptied = sem("att_emptied")
        att_turned = {k: sem(f"att_turned_{k}") for k in ("sb", "fox")}
        attT_ready = {k: sem(f"attT_ready_{k}") for k in ("sb", "fox")}
        att_out = {k: sem(f"att_out_{k}") for k in ("sb", "fox")}
        att_done = {k: sem(f"att_done_{k}") for k in ("sb", "fox")}
        steps_sem = sem("steps_sem")
        dec = {}
        for k in ("sb", "fox"):
            dec[k] = {n: sem(f"{n}_{k}") for n in (
                "k0", "k1", "v_last0", "v_last1", "new_turned", "new_ready", "new_scored", "q_ready", "kt_ready",
                "kt_act", "kt_dve", "scores_done", "rows_out", "z_turned", "z_drained", "fold_ready", "fold_out", "bias_ready",
                "soft_in", "soft_act", "soft_ready", "sum_ready", "expo_ready", "probs_ready",
                "v_used", "pv_done", "o_emptied", "loaded", "den_ready")}
        page_ready = sem("page_ready")
        page_carry = sem("page_carry")
        forget_part = sem("forget_part")
        forget_turned = sem("forget_turned")
        forget_ready = sem("forget_ready")
        mixed_turned = sem("mixed_turned")
        sample_mixed = sem("sample_mixed")
        mixed_out = sem("mixed_out")
        x_half_in = [sem(f"x_half_in{i}") for i in range(2)]
        p_in = sem("p_in")
        p_turned = sem("p_turned")
        p_out = sem("p_out")
        pool_waits = sem("pool_waits")
        last_sem = sem("last_sem")

        def phase_over(eng, n):
            eng.drain().then_inc(phase_sem, 1)
            eng.wait_ge(phase_sem, 4 * (n + 1))

        def layer_over(eng, L):
            eng.drain().then_inc(arrived, 1)
            eng.wait_ge(layer_go, L + 1)

        PROJ_R, RET, PROJ_S, ATT_S, DEC_S, PROJ_F, ATT_F, DEC_F = range(8)
        PROJ_SEGS = {PROJ_R: SEG_NAMES[0:4], PROJ_S: SEG_NAMES[4:8], PROJ_F: SEG_NAMES[8:12]}
        OUT_SEGS, GATED_SEGS = ["out0", "out1"], ["pg0", "pe0", "pg1", "pe1"]
        KIND = {ATT_S: "sb", ATT_F: "fox", DEC_S: "sb", DEC_F: "fox"}
        CACHE = {"sb": (cache_sb_k, cache_sb_v), "fox": (cache_fox_k, cache_fox_v)}
        RET_BANKS = (0, 1, 5)
        UNITS = [(t, NT - 1 - t, h) for t in reversed(range(NT)) for h in range(HA)]

        def bank2(first, n=1024):
            return ps[:, first:first + 2, :].rearrange("p b c -> p (b c)")[:, 0:n]

        block = ctx.enter_context(nc.Block())

        @block.sync
        def _(sp):
            sp.dma_start(O[:, 0, :], x_prompt[0, 0:P]).then_inc(x_in[0], 16)
            sp.dma_start(C[:], consts).then_inc(consts_in, 16)
            sp.dma_start(pages[:], page_table.rearrange("b p -> (b p)").unsqueeze(0)).then_inc(consts_in, 16)
            sp.wait_ge(consts_in, 32)

            def load_weights(L, seg):
                i = ALL_SEGS.index(seg)
                if i >= 2:
                    sp.wait_ge(proj_ready, TILES * (i - 1))
                if seg in SEG_COL:
                    n = SEG_W[seg]
                    src = w_in[L, :, SEG_COL[seg]:SEG_COL[seg] + n]
                    kc = KC
                else:
                    n, c = 512, int(seg[-1])
                    src = {"ou": w_out, "pg": w_pg, "pe": w_pe}[seg[:2]][L, :, c * 512:(c + 1) * 512]
                    kc = PLE // P if seg[:2] == "pe" else KC
                sp.dma_start(W[i % 2][:, 0:kc, 0:n], src.rearrange("(k p) n -> p k n", p=P))\
                    .then_inc(w_loaded[i % 2], 16)

            def load_k(L, kind, b, g, pages_of_group=PG8):
                cache = CACHE[kind][0]
                s = dec[kind]
                if not (isinstance(b, int) and 4 * b + g < 2):
                    sp.wait_ge(s["kt_ready"], b * 20 + 5 * (g - 1))
                for p in range(pages_of_group):
                    at = b * PAGES + g * PG8 + p
                    pg = sp.value_load(pages[0:1, bass.ds(at, 1)])
                    sp.dma_start(ringK[g % 2][:, p * DA:(p + 1) * DA],
                                 cache[L, bass.ds(pg, 1)].rearrange("a s h d -> s (a h d)"))\
                        .then_inc(s[f"k{g % 2}"], 16)

            def decode_loads(L, kind):
                s = dec[kind]
                sp.wait_ge(proj_ready, TILES * (8 if kind == "sb" else 12))
                load_k(L, kind, 0, 0)
                sp.wait_ge(phase_sem, 4 * ((ATT_S if kind == "sb" else ATT_F) + 1))
                for g in range(1, GROUPS):
                    load_k(L, kind, 0, g, PG8 - BY_ACT)
                with sp.Fori(1, SEQS) as b:
                    for g in range(GROUPS):
                        load_k(L, kind, b, g)
                for g in range(2, GROUPS):
                    sp.wait_ge(s["kt_ready"], (SEQS - 1) * BLOCKS + 5 * (g + 1))
                    for p in range(PG8):
                        at = (SEQS - 1) * PAGES + g * PG8 + p
                        pg = sp.value_load(pages[0:1, at:at + 1])
                        sp.dma_start(ringK[g % 2][:, p * DA:(p + 1) * DA],
                                     CACHE[kind][1][L, bass.ds(pg, 1)].rearrange("a s h d -> s (a h d)"))\
                            .then_inc(s[f"v_last{g % 2}"], 16)

            def load_decoded(L, kind):
                sp.wait_ge(stored[kind], 16 * HA * (L + 1))
                sp.dma_start(decoded_rows[kind], decoded_dram[0 if kind == "sb" else 1])\
                    .then_inc(dec[kind]["loaded"], 16)

            def load_first(layer):
                sp.dma_start(W[0][:, :, 0:DR], w_in[layer, :, 0:DR].rearrange("(k p) n -> p k n", p=P))\
                    .then_inc(first_w, 16)
                sp.dma_start(gT[:, 0, :], g_norm[layer].rearrange("(k p) -> p k", p=P),
                             allow_slow_non_contiguous=True).then_inc(first_w, 16)

            load_first(0)
            with sp.Fori(0, DEPTH) as L:
                for dst, src in (
                        (gT[:, 1, :], g_pe[L].rearrange("(k p) -> p k", p=P)),
                        (g_ret_b[:], g_ret_gn[L].partition_broadcast(P)),
                        (g_fq_b[:], g_fox_q[L].partition_broadcast(P)),
                        (g_fk_b[:], g_fox_k[L].partition_broadcast(P)),
                        (b_f_b[:], b_f[L].partition_broadcast(P))):
                    sp.dma_start(dst, src, allow_slow_non_contiguous=True).then_inc(vec_loaded, 16)
                load_weights(L, "rk")
                for pr in range(QP):
                    sp.dma_start(s0[:, pr], state_ret[L, :, 2 * pr:2 * pr + 2].rearrange(
                        "b h d e -> (h d) b e")).then_inc(state_in, 16)
                for seg in SEG_NAMES[2:9]:
                    load_weights(L, seg)
                decode_loads(L, "sb")
                sp.wait_ge(phase_sem, 4 * (DEC_S + 1))
                load_weights(L, "fq")
                load_decoded(L, "sb")
                for seg in ALL_SEGS[10:13]:
                    load_weights(L, seg)
                decode_loads(L, "fox")
                sp.wait_ge(phase_sem, 4 * (DEC_F + 1))
                load_weights(L, "out1")
                sp.dma_start(p_nat[:, 0:NT, :], p_prompt[L, 0].rearrange("(t p) c -> p t c", p=P))\
                    .then_inc(p_in, 16)
                sp.dma_start(p_nat[0:ROWS, SAMPLE, :], p_sample[L].rearrange("b s c -> (b s) c"))\
                    .then_inc(p_in, 16)
                sp.wait_ge(x_saved, 32 * (L + 1))
                for n in range(2 * TILES):
                    c, t = n // TILES, n % TILES
                    if n == 2:
                        load_decoded(L, "fox")
                    if n >= 2:
                        sp.wait_ge(emptied_dve, evac_count("out0", 0) + n - 2)
                    sp.dma_start(x_half[0:rows(t), n % 2, :], residual_dram[
                        t * P:t * P + rows(t), c * 512:(c + 1) * 512]).then_inc(x_half_in[n % 2], 16)
                    if n == TILES + 1:
                        load_weights(L, "pg0")
                for seg in ALL_SEGS[15:18]:
                    load_weights(L, seg)
                assert DEPTH == 2
                sp.wait_ge(proj_ready, TILES * (ALL_SEGS.index("pg1") + 1))
                load_first(DEPTH - 1)
                sp.wait_ge(arrived, 4 * (L + 1))
                sp.sem_inc(last_sem, 1)
                sp.sem_clear(range(phase_sem.num, last_sem.num + 1))
                sp.sem_inc(layer_go, 1)
            sp.wait_ge(first_w, 32 * (DEPTH + 1))

        @block.gpsimd
        def _(pool):
            def await_dma(done, value):
                pool.wait_ge(done, value)
                pool.sem_inc(pool_waits, 1)

            nc.gpsimd.memset(eps[:], EPS).then_inc(set_up, 1)
            nc.gpsimd.memset(reset[:], 1.0).then_inc(set_up, 1)
            pool.wait_ge(set_up, 2)
            nc.gpsimd.memset(reset[:].rearrange("p (r s) -> p r s", s=SLOT)[:, :, SLOT - 1:SLOT],
                             0.0).then_inc(set_up, 1)
            for i, (a, b) in list(enumerate(X_LOADS))[1:-1]:
                pool.dma_start(O[:, a:b, :], x_prompt[0, a * P:b * P].rearrange("(t p) d -> p t d", p=P))\
                    .then_inc(x_in[i], 16)
            pool.dma_start(O[0:ROWS, SAMPLE, :], x_sample.rearrange("b s d -> (b s) d")).then_inc(x_in[-1], 16)
            pool.wait_ge(consts_in, 32)
            for arrived_x in x_in:
                pool.wait_ge(arrived_x, 16)
            with pool.Fori(0, DEPTH) as L:
                stores = 0
                pool.dma_start(residual_dram[0:SEQ].rearrange("(t p) d -> p t d", p=P),
                               O[:, 0:NT, :]).then_inc(x_saved, 16)
                pool.dma_start(residual_dram[SEQ:SEQ + ROWS], O[0:ROWS, SAMPLE, :]).then_inc(x_saved, 16)
                pool.sem_inc(phase_sem, 1)
                with pool.Fori(0, SEQS * PAGES) as p:
                    pg = pool.value_load(pages[0:1, bass.ds(p, 1)])
                    pool.dma_start(logf_dram[bass.ds(p, 1)],
                                   cache_fox_logf[L, bass.ds(pg, 1)].rearrange("a s h -> a (s h)"))\
                        .then_inc(logf_gathered, 16)
                pool.wait_ge(state_r, NT)
                for h2 in range(2):
                    pool.dma_start(rs_prompt[L, 0].rearrange("(pr h) d e -> h d pr e", h=2)[h2],
                                   states[h2 * HD:(h2 + 1) * HD, (NT - 1) % 2]).then_inc(saved, 16)
                    stores += 1
                pool.wait_ge(new_state_out, HR)
                for pr in range(QP):
                    pool.dma_start(rs_sample[L, :, 2 * pr:2 * pr + 2].rearrange("b h d e -> (h d) b e"),
                                   s0[:, pr]).then_inc(saved, 16)
                    stores += 1
                await_dma(saved, L * 16 * STORES + 16 * stores)
                phase_over(pool, RET)

                def store_kv(seg, t, src, prompt, sample, done, ready, count):
                    pool.wait_ge(ready, count)
                    if t == SAMPLE:
                        dst = sample[L].rearrange("b s h d -> (b s) (h d)")
                    else:
                        dst = prompt[L, 0, t * P:(t + 1) * P].rearrange("p h d -> p (h d)")
                    pool.dma_start(dst, src).then_inc(done, 16)

                for t in range(TILES):
                    src = k_new[:] if t == SAMPLE else nat[:, turn_index("sk", t) % 2, 0:DA]
                    store_kv("sk", t, src, sbk_prompt, sbk_sample, k_saved[t % 2],
                             emptied_act, evac_count("sk", t))
                for t in range(TILES):
                    src = v_new[:] if t == SAMPLE else v_s[:, t]
                    store_kv("sv", t, src, sbv_prompt, sbv_sample, saved, emptied_act,
                             evac_count("sv", t))
                    stores += 1
                await_dma(k_saved[0], L * 160 + 16 * 5)
                await_dma(k_saved[1], L * 128 + 16 * 4)
                await_dma(saved, L * 16 * STORES + 16 * stores)
                phase_over(pool, PROJ_S)
                phase_over(pool, ATT_S)

                def load_values(kind):
                    cache = CACHE[kind][1]
                    def load_group(b, g):
                        await_dma(dec[kind]["v_used"], b * GROUPS + g + 1)
                        for p in range(PG8):
                            at = b * PAGES + g * PG8 + p
                            pg = pool.value_load(pages[0:1, bass.ds(at, 1)])
                            pool.dma_start(ringV[:, g % 2, p * DA:(p + 1) * DA],
                                           cache[L, bass.ds(pg, 1)].rearrange("a s h d -> s (a h d)"))\
                                .then_inc(v_in[kind][g % 2], 16)

                    with pool.Fori(0, SEQS - 1) as b:
                        for g in range(GROUPS):
                            load_group(b, g)
                    for g in range(2):
                        load_group(SEQS - 1, g)

                def decoded_store(kind):
                    pool.wait_ge(dec[kind]["o_emptied"], SEQS + 1)
                    dst = decoded_dram[0 if kind == "sb" else 1].rearrange("(b i) c -> i b c", b=SEQS)
                    for h in range(HA):
                        q = 32 * (h % 4)
                        pool.dma_start(dst[:, :, h * HD:(h + 1) * HD], decoded[q:q + NEW, :, h // 4, :])\
                            .then_inc(stored[kind], 16)

                load_values("sb")
                phase_over(pool, DEC_S)
                decoded_store("sb")
                pool.wait_ge(logf_ready, 1)
                pool.dma_start(foxl_prompt[L, 0].rearrange("(t p) h -> p t h", p=P), logf[:, 0:NT, :])\
                    .then_inc(saved, 16)
                pool.dma_start(foxl_sample[L].rearrange("b s h -> (b s) h"), logf[0:ROWS, SAMPLE, :])\
                    .then_inc(saved, 16)
                stores += 2
                for t in range(TILES):
                    src = k_new[:].rearrange("p (h d) -> p h d", h=HA) if t == SAMPLE else \
                        aug[:, turn_index("fk", t) % 2, :, 0:HD]
                    pool.wait_ge(nat_ready, nat_count("fk", t))
                    dst = foxk_sample[L].rearrange("b s h d -> (b s) h d") if t == SAMPLE else \
                        foxk_prompt[L, 0, t * P:(t + 1) * P]
                    pool.dma_start(dst, src).then_inc(k_saved[t % 2], 16)
                for t in range(TILES):
                    src = v_new[:] if t == SAMPLE else v_f[:, t]
                    store_kv("fv", t, src, foxv_prompt, foxv_sample, saved, emptied_act,
                             evac_count("fv", t))
                    stores += 1
                await_dma(k_saved[0], L * 160 + 16 * 10)
                await_dma(k_saved[1], L * 128 + 16 * 8)
                await_dma(saved, L * 16 * STORES + 16 * stores)
                phase_over(pool, PROJ_F)
                await_dma(logf_gathered, 16 * SEQS * PAGES * (L + 1))
                pool.dma_start(page_logf.rearrange("p a s h -> p a (s h)"),
                               logf_dram.rearrange("(a p) n -> p a n", p=P)).then_inc(logf_in, 16)
                phase_over(pool, ATT_F)
                load_values("fox")
                phase_over(pool, DEC_F)
                decoded_store("fox")
                assert stores == STORES
                layer_over(pool, L)
            pool.dma_start(y_prompt[0].rearrange("(t p) d -> p t d", p=P), O[:, 0:NT, :]).then_inc(y_out, 16)
            pool.dma_start(y_sample.rearrange("b s d -> (b s) d"), O[0:ROWS, SAMPLE, :]).then_inc(y_out, 16)
            pool.wait_ge(y_out, 32)

        @block.tensor
        def _(pe):
            pe.wait_ge(consts_in, 32)
            pe.wait_ge(set_up, 3)

            def turn_normed(norm, t):
                m, R = norm * TILES + t, rows(t)
                pe.wait_ge(scaled_ready, m + 1)
                if m >= 1:
                    pe.wait_ge(norm_out, m)
                for k in range(KC):
                    ins = pe.transpose(ps[:, 6 + k // 4, (k % 4) * P:(k % 4) * P + R],
                                       scaled[0:R, m % 2, k * P:(k + 1) * P], ident[0:R, 0:R])
                ins.then_inc(norm_turned, 1)

            def turn_mixed(t):
                R = rows(t)
                if t >= 1:
                    pe.wait_ge(mixed_out, t)
                if t == SAMPLE:
                    pe.wait_ge(sample_mixed, 1)
                for k in range(KC):
                    ins = pe.transpose(ps[:, 6 + k // 4, (k % 4) * P:(k % 4) * P + R],
                                       O[0:R, t, k * P:(k + 1) * P], ident[0:R, 0:R])
                ins.then_inc(mixed_turned, 1)

            def segment_tile(seg, t, L):
                i = ALL_SEGS.index(seg)
                n = i * TILES + t
                R, N = rows(t), SEG_W.get(seg, 512)
                if t == 0 and seg == "rq":
                    pe.wait_ge(first_w, 32 * (L + 1))
                elif t == 0:
                    pe.wait_ge(w_loaded[i % 2], 16 * ((i - 1) // 2 + 1))
                if seg == "out0":
                    pe.wait_ge(mixed_out, t + 1)
                if seg in ("rq", "pg0"):
                    pe.wait_ge(norm_out, (TILES if seg == "pg0" else 0) + t + 1)
                if n >= 3:
                    s3, t3 = ALL_SEGS[(n - 3) // TILES], (n - 3) % TILES
                    pe.wait_ge(emptied_dve if s3 in DVE_EVACUATES else emptied_act, evac_count(s3, t3))
                src = pT if seg[:2] == "pe" else xT
                kc = PLE // P if seg[:2] == "pe" else KC
                for k in range(kc):
                    ins = pe.matmul(ps[0:R, n % 3, 0:N], src[:, k, t * P:t * P + R],
                                    W[i % 2][:, k, 0:N], start=(k == 0), stop=(k == kc - 1))
                ins.then_inc(proj_ready, 1)

            def turn_tile(seg, t):
                m, R = turn_index(seg, t), rows(t)
                if seg[0] == "s":
                    pe.wait_ge(emptied_act, evac_count(seg, t))
                else:
                    pe.wait_ge(nat_ready, nat_count(seg, t))
                if m >= 2:
                    pe.wait_ge(turned_out, m - 1)
                bank = 3 + 2 * (m % 2)
                if seg[0] == "f":
                    for h in range(HA):
                        ins = pe.transpose(ps[0:HD + 1, bank + h // 4, (h % 4) * P:(h % 4) * P + R],
                                           aug[0:R, m % 2, h, :], ident[0:R, 0:R])
                else:
                    for c in range(QP):
                        w = min(P, SEG_W[seg] - c * P)
                        ins = pe.transpose(ps[0:w, bank, c * P:c * P + R],
                                           nat[0:R, m % 2, c * P:c * P + w], ident[0:R, 0:R])
                ins.then_inc(turned, 1)

            def project(segs, L):
                for seg in segs:
                    for t in range(TILES):
                        if seg == "rq" and t < SAMPLE:
                            turn_normed(0, t + 1)
                        if seg == "out0" and t < SAMPLE:
                            turn_mixed(t + 1)
                        segment_tile(seg, t, L)
                        if seg == "out1" and t >= 2:
                            turn_normed(1, t - 2)
                        if t >= 1 and t - 1 < TURNED.get(seg, 0):
                            turn_tile(seg, t - 1)
                    if TURNED.get(seg, 0) == TILES:
                        turn_tile(seg, TILES - 1)
                    if seg == "fg":
                        pe.wait_ge(logf_ready, 1)
                        padded = logf_padded.rearrange("p t h -> p (t h)")
                        lf = padded[:, (NT - 1) * HA:]
                        out = ps[:, 7, 0:NT * HA]
                        pe.matmul(out, const("neg_upto"), lf[:, 0:NT * HA], start=True, stop=False)
                        for d in range(1, NT):
                            pe.matmul(out, const("negones"),
                                      padded[:, (NT - 1 - d) * HA:(2 * NT - 1 - d) * HA],
                                      start=False, stop=(d == NT - 1))
                        pe.matmul(ps[0:ROWS, 7, 64:64 + HA], const("neg_upto_new")[0:ROWS],
                                  lf[0:ROWS, NT * HA:], start=True, stop=True).then_inc(cum_ready, 1)

            def retention():
                units = [(t, h) for t in range(TILES) for h in range(HR)]

                def at(h):
                    return h // 2, slice((h % 2) * HD, (h % 2) * HD + HD)

                def scores(u):
                    t, h = units[u]
                    pr, q = at(h)
                    R = rows(t)
                    if u >= 3:
                        pe.wait_ge(masked_r, u - 2)
                    pe.matmul(ps[0:R, RET_BANKS[u % 3], 0:R], kT_r[q, pr, t * P:t * P + R],
                              qT_r[q, pr, t * P:t * P + R], start=True, stop=True).then_inc(scores_r, 1)

                scores(0)
                scores(1)
                for u, (t, h) in enumerate(units):
                    pr, q = at(h)
                    R = rows(t)
                    if u + 2 < len(units):
                        scores(u + 2)
                    if h == 2 and t < SAMPLE:
                        if t >= 1:
                            pe.wait_ge(state_r, t)
                        for c in range(QP):
                            ins = pe.matmul(ps[:, 4, c * P:(c + 1) * P],
                                            kd_r[:, t, c * P:(c + 1) * P], v_r[:, t, c * P:(c + 1) * P],
                                            start=True, stop=True)
                        ins.then_inc(kv_r, 1)
                    pe.wait_ge(masked_r, u + 1)
                    if h == 0 and t >= 2:
                        pe.wait_ge(ret_emptied, t - 1)
                    with_state = 0 < t < SAMPLE
                    bank, c = (2, h) if t == SAMPLE else (2 + t % 2 + 4 * (h % 2), h // 2)
                    out = ps[0:R, bank, c * HD:(c + 1) * HD]
                    ins = pe.matmul(out, masked[0:R, u % 3, 0:R], v_r[0:R, t, h * HD:(h + 1) * HD],
                                    start=True, stop=not with_state)
                    if with_state:
                        if h == 0:
                            pe.wait_ge(state_r, t)
                        ins = pe.matmul(out, qT_r[q, pr, t * P:t * P + R], states[q, (t - 1) % 2, pr, :],
                                        start=False, stop=True)
                    ins.then_inc(inner_r, 1)
                pe.wait_ge(state_in, 16 * QP)
                for h in range(HR):
                    pr, q = at(h)
                    if h >= 2:
                        pe.wait_ge(cross_emptied, h - 1)
                    pe.matmul(ps[0:ROWS, 6 + h % 2, :], qT_r[q, pr, SEQ:TR],
                              s0[q, pr].rearrange("p b e -> p (b e)"), start=True, stop=True)\
                        .then_inc(cross_ready, 1)
                for h in range(HR):
                    pr, q = at(h)
                    pe.wait_ge(v_seq_ready, h + 1)
                    if h >= 2:
                        pe.wait_ge(new_state_out, h - 1)
                    if h < 2:
                        pe.wait_ge(state_r, NT)
                    pe.matmul(ps[q, 4 + h % 2, :], kd_r[0:ROWS, SAMPLE, h * HD:(h + 1) * HD],
                              v_seq[0:ROWS, h % 2, :], start=True, stop=True,
                              tile_position=(0, q.start)).then_inc(new_state_ready, 1)
                phase_over(pe, RET)

            def attention(phase):
                kind = KIND[phase]
                qT, kT, v = (qT_s, kT_s, v_s) if kind == "sb" else (qT_f, kT_f, v_f)

                def scores(u):
                    t, i, h = UNITS[u]
                    n = (t + 1) * P
                    q = slice((h % 2) * HD, (h % 2) * HD + HD) if kind == "sb" else slice(0, HD + 1)
                    a = h // 2 if kind == "sb" else h
                    if u >= 2:
                        pe.wait_ge(att_first[kind], u - 1)
                    for c in range(0, n, 512):
                        w = min(512, n - c)
                        ins = pe.matmul(ps[:, 2 * (u % 2) + c // 512, 0:w], qT[q, a, t * P:(t + 1) * P],
                                        kT[q, a, c:c + w], start=True, stop=True)
                    ins.then_inc(att_scores[kind], 1)

                def turn(u):
                    t, i, h = UNITS[u]
                    pe.wait_ge(att_probs[kind] if kind == "sb" else att_first[kind], u + 1)
                    if u >= 1:
                        pe.wait_ge(attT_ready[kind], u)
                    src = att if kind == "sb" else expd
                    for j in range(t + 1):
                        ins = pe.transpose(ps[:, 4 + j // 4, (j % 4) * P:(j % 4 + 1) * P],
                                           src[:, u % 2, j * P:(j + 1) * P], ident)
                    ins.then_inc(att_turned[kind], 1)

                def weigh(u):
                    t, i, h = UNITS[u]
                    pe.wait_ge(attT_ready[kind], u + 1)
                    if h == 0 and i >= 2:
                        pe.wait_ge(att_done[kind], i - 1)
                    for j in range(t + 1):
                        ins = pe.matmul(ps[:, 6 + t % 2, h * HD:(h + 1) * HD],
                                        attT[:, u % 2, j * P:(j + 1) * P], v[:, j, h * HD:(h + 1) * HD],
                                        start=(j == 0), stop=(j == t))
                    ins.then_inc(att_out[kind], 1)

                scores(0)
                for u in range(len(UNITS)):
                    if u + 1 < len(UNITS):
                        scores(u + 1)
                    if u >= 1:
                        weigh(u - 1)
                    turn(u)
                weigh(len(UNITS) - 1)
                phase_over(pe, phase)

            def forget_sums():
                for half in range(2):
                    pe.wait_ge(page_ready, half + 1)
                    pe.matmul(ps[:, 6 + half, 0:HA], const("later_page"), page_sum[:, half, :, 0],
                              start=True, stop=True).then_inc(page_carry, 1)
                for h in range(HA):
                    pe.wait_ge(forget_part, 2)
                    if h >= 2:
                        pe.wait_ge(forget_ready, h - 1)
                    for half in range(2):
                        ins = pe.transpose(ps[:, h % 2, half * P:(half + 1) * P], page_sum[:, half, h, :],
                                           ident)
                    ins.then_inc(forget_turned, 1)
                pe.wait_ge(forget_ready, HA)

            def decode(phase, L):
                kind = KIND[phase]
                s = dec[kind]
                if kind == "fox":
                    forget_sums()
                for c, at in enumerate((0, 2 * HD, 4 * HD, HD, 3 * HD)):
                    pe.transpose(ps[:, 0, c * ROWS:(c + 1) * ROWS], q_new[:, at:at + P], ident[0:ROWS, 0:ROWS])
                for c in range(3):
                    w = min(P, DA - c * P)
                    ins = pe.transpose(ps[0:w, 1, c * ROWS:(c + 1) * ROWS], k_new[:, c * P:c * P + w],
                                       ident[0:ROWS, 0:ROWS])
                ins.then_inc(s["new_turned"], 1)
                pe.sem_inc(s["v_used"], 2)
                pe.wait_ge(s["new_ready"], 1)
                for c in range(3):
                    ins = pe.matmul(ps[0:ROWS, 2, c * P:(c + 1) * P], kT_new[:, c, :], qd[:, :, c, :],
                                    start=True, stop=True)
                ins.then_inc(s["new_scored"], 1)

                def turn_blocks(b, blocks):
                    for n in blocks:
                        g, kk = n // 5, n % 5
                        if kk == 0:
                            pe.wait_ge(s[f"k{g % 2}"], PG8 * 16 * (b * 2 + g // 2 + 1))
                        if not is_first(b) or n >= 2:
                            by_act = (n - 2) % BLOCKS in ACT_BLOCKS
                            pe.wait_ge(s["kt_act" if by_act else "kt_dve"],
                                       taken(ACT_BLOCKS if by_act else DVE_BLOCKS, b, n - 2))
                        for m in range(4):
                            at = (5 * m + kk) * P
                            ins = pe.transpose(ps[:, n % 2, m * P:(m + 1) * P], ringK[g % 2][:, at:at + P],
                                               ident)
                        ins.then_inc(s["kt_ready"], 1)

                def score(b, g):
                    n = 5 * g + 4
                    pe.wait_ge(s["kt_act"], taken(ACT_BLOCKS, b, n))
                    if not is_first(b) or any(m <= n for m in DVE_BLOCKS):
                        pe.wait_ge(s["kt_dve"], taken(DVE_BLOCKS, b, n))
                    if g == 0:
                        pe.wait_ge(s["q_ready"], b + 1)
                    if not is_first(b) or g >= 2:
                        pe.wait_ge(s["rows_out"], 5 * b + g - (1 if g >= 2 else 0) if g else 5 * b)
                    if g == 1 and not is_first(b):
                        pe.wait_ge(s["soft_ready"], b)
                    for kk in range(5):
                        bank = 3 if kk == 4 else (5 if g % 2 else 2)
                        q = 32 * (g if kk == 4 else kk)
                        ins = pe.matmul(ps[q:q + 32, bank, :], q_now[:, kk, :], kT_d[(5 * g + kk) % SLOTS],
                                        start=True, stop=True, tile_position=(0, q), skip_group_check=True)
                    ins.then_inc(s["scores_done"], 1)

                def turn_rows(b, j):
                    pe.wait_ge(s["rows_out"], 5 * b + j + 1)
                    if j >= 2:
                        pe.wait_ge(s["z_drained"], 5 * b + j - 1)
                    elif not is_first(b):
                        pe.wait_ge(s["soft_ready"], b)
                    for m in range(4):
                        ins = pe.transpose(ps[:, 6 + j % 2, m * P:(m + 1) * P],
                                           z_rows[:, 2 if j == 4 else j % 2, m * P:(m + 1) * P], ident)
                    ins.then_inc(s["z_turned"], 1)

                def fold_first(b):
                    if kind == "fox":
                        pe.wait_ge(s["soft_in"], b + 1)
                        pe.transpose(ps[:, 6, 0:P], row_max[:], ident).then_inc(s["fold_ready"], 1)

                def fold(b):
                    if kind == "sb":
                        pe.wait_ge(s["sum_ready"], b + 1)
                        for c in range(3):
                            cols = slice(c * 440, c * 440 + 440)
                            pe.matmul(ps[:, 5 + c, 0:440], const("earlier"), soft[:, cols], start=True, stop=False)
                            ins = pe.matmul(ps[:, 5 + c, 0:440], const("negones"), later[:, cols], start=False,
                                            stop=True)
                        ins.then_inc(s["expo_ready"], 1)
                    else:
                        pe.wait_ge(s["fold_out"], b + 1)
                        pe.matmul(ps[:, 6, P:P + HI], ones[0:HI, :], small[0:HI, 120:120 + HI], start=True,
                                  stop=True).then_inc(s["bias_ready"], 1)

                def weigh(b, g):
                    pr = probs.rearrange("p (h i s) -> p h i s", h=HA, i=NEW)

                    def out(h):
                        q = 32 * (h % 4)
                        return ps[q:q + NEW, 4, (h // 4) * HD:(h // 4 + 1) * HD]

                    if g == 0:
                        pe.wait_ge(s["probs_ready"], b + 1)
                        pe.wait_ge(s["o_emptied"], b + 1)
                    if isinstance(b, int) and b == SEQS - 1 and g >= 2:
                        values = ringK[g % 2]
                        pe.wait_ge(s[f"v_last{g % 2}"], PG8 * 16)
                    else:
                        values = ringV[:, g % 2]
                        pe.wait_ge(v_in[kind][g % 2], PG8 * 16 * (b * 2 + g // 2 + 1 + L * (SEQS * 2 - 1)))
                    for p in range(PG8):
                        for h in range(HA):
                            c = p * DA + h * HD
                            ins = pe.matmul(out(h), pr[:, h, :, g * PG8 + p], values[:, c:c + HD],
                                            start=(g == 0 and p == 0), stop=False,
                                            tile_position=(0, 32 * (h % 4)), skip_group_check=True)
                    ins.then_inc(s["v_used"], 1)
                    if g < GROUPS - 1:
                        return
                    for h in range(HA):
                        ins = pe.matmul(out(h), pr[0:ROWS, h, :, PAGES], v_new[:, h * HD:(h + 1) * HD],
                                        start=False, stop=True, tile_position=(0, 32 * (h % 4)),
                                        skip_group_check=True)
                    if kind == "fox":
                        pe.wait_ge(s["den_ready"], b + 1)
                        for h in range(HA):
                            q = 32 * (h % 4)
                            ins = pe.matmul(ps[q:q + NEW, 4, P + h // 4:P + h // 4 + 1],
                                            small[:, 40 + h * NEW:40 + (h + 1) * NEW], ones[:, 0:1],
                                            start=True, stop=True, tile_position=(0, q),
                                            skip_group_check=True)
                    ins.then_inc(s["pv_done"], 1)

                def sequence(b, before=None, two_before=None):
                    turn_blocks(b, range(0, 5))
                    if before is not None:
                        fold_first(before)
                    turn_blocks(b, range(5, 8))
                    if two_before is not None:
                        weigh(two_before, 3)
                    score(b, 0)
                    turn_blocks(b, range(8, 10))
                    if before is not None:
                        fold(before)
                    turn_blocks(b, range(10, 13))
                    turn_rows(b, 0)
                    score(b, 1)
                    turn_blocks(b, range(13, 15))
                    if before is not None:
                        weigh(before, 0)
                    turn_rows(b, 1)
                    turn_blocks(b, range(15, 18))
                    score(b, 2)
                    turn_blocks(b, range(18, 20))
                    if before is not None:
                        weigh(before, 1)
                    turn_rows(b, 2)
                    score(b, 3)
                    turn_rows(b, 3)
                    turn_rows(b, 4)
                    if before is not None:
                        weigh(before, 2)

                sequence(0)
                sequence(1, 0)
                with pe.Fori(2, SEQS) as b:
                    sequence(b, b - 1, b - 2)
                fold_first(SEQS - 1)
                weigh(SEQS - 2, 3)
                fold(SEQS - 1)
                for g in range(GROUPS):
                    weigh(SEQS - 1, g)
                phase_over(pe, phase)

            with pe.Fori(0, DEPTH) as L:
                turn_normed(0, 0)
                project(PROJ_SEGS[PROJ_R], L)
                phase_over(pe, PROJ_R)
                retention()
                project(PROJ_SEGS[PROJ_S], L)
                phase_over(pe, PROJ_S)
                attention(ATT_S)
                decode(DEC_S, L)
                project(PROJ_SEGS[PROJ_F], L)
                phase_over(pe, PROJ_F)
                attention(ATT_F)
                decode(DEC_F, L)
                turn_mixed(0)
                project(OUT_SEGS[0:1], L)
                pe.wait_ge(p_in, 32)
                for t in range(TILES):
                    R = rows(t)
                    if t >= 2:
                        pe.wait_ge(p_out, t - 1)
                    for k in range(2):
                        ins = pe.transpose(ps[:, 3 + t % 2, k * P:k * P + R],
                                           p_nat[0:R, t, k * P:(k + 1) * P], ident[0:R, 0:R])
                    ins.then_inc(p_turned, 1)
                project(OUT_SEGS[1:], L)
                turn_normed(1, NT - 1)
                turn_normed(1, SAMPLE)
                pe.wait_ge(p_out, TILES)
                project(GATED_SEGS, L)
                layer_over(pe, L)

        @block.scalar
        def _(act):
            act.wait_ge(consts_in, 32)
            act.wait_ge(set_up, 3)

            def root(norm, t):
                if t < TILES:
                    m, R = norm * TILES + t, rows(t)
                    if norm == 0:
                        act.wait_ge(x_in[LOAD_OF[t]], 16)
                    else:
                        act.wait_ge(emptied_dve, evac_count("out1", t))
                    act.activation(junk[0:R], O[0:R, t, :], ACT.Square, accum_out=small[0:R, 200 + t:201 + t])\
                        .then_inc(squared, 1)
                    act.wait_ge(squared, m + 1)
                    act.activation(small[0:R, 210 + t:211 + t], small[0:R, 200 + t:201 + t], ACT.Sqrt,
                                   bias=eps[0:R], scale=1.0 / D).then_inc(rooted, 1)

            def turned_to(seg, t):
                m, R = turn_index(seg, t), rows(t)
                act.wait_ge(turned, m + 1)
                bank = 3 + 2 * (m % 2)
                if seg[0] == "f":
                    dst = qT_f if seg == "fq" else kT_f
                    ins = act.activation(
                        dst[0:HD + 1, :, t * P:(t + 1) * P],
                        bank2(bank, HA * P)[0:HD + 1].rearrange("p (h n) -> p h n", h=HA), ACT.Copy)
                elif seg[0] == "r":
                    dst = qT_r if seg == "rq" else kT_r
                    ins = act.activation(
                        dst[:, :, t * P:t * P + R],
                        ps[:, bank, 0:QP * P].rearrange("p (c n) -> p c n", c=QP)[:, :, 0:R], ACT.Copy)
                else:
                    dst = qT_s if seg == "sq" else kT_s
                    src = ps[:, bank, 0:QP * P].rearrange("p (c n) -> p c n", c=QP)
                    act.activation(dst[:, 0:2, t * P:(t + 1) * P], src[:, 0:2], ACT.Copy)
                    ins = act.activation(dst[0:HD, 2, t * P:(t + 1) * P], src[0:HD, 2], ACT.Copy)
                ins.then_inc(turned_out, 1)

            def project(segs, L):
                for seg in segs:
                    i = ALL_SEGS.index(seg)
                    for t in range(TILES):
                        n, R, N = i * TILES + t, rows(t), SEG_W.get(seg, 512)
                        src = ps[0:R, n % 3, 0:N]
                        if seg == "rq":
                            root(0, t + 3)
                        if seg == "out1":
                            root(1, t)
                        if seg == "rg" and t == 0:
                            act.wait_ge(x_saved, 32 * (L + 1))
                        if seg in GATE_AT:
                            act.wait_ge(proj_ready, n + 1)
                            w = DR if seg == "rg" else DA
                            act.activation(O[0:R, t, GATE_AT[seg]:GATE_AT[seg] + w], src[:, 0:w], ACT.Sigmoid)\
                                .then_inc(sigmoid_ready, 1)
                        elif seg in ("rv", "sv", "fv"):
                            act.wait_ge(proj_ready, n + 1)
                            dst = v_r[0:R, t] if seg == "rv" else v_new[:] if t == SAMPLE else \
                                (v_s if seg == "sv" else v_f)[:, t]
                            act.activation(dst, src, ACT.Copy).then_inc(emptied_act, 1)
                        elif seg in ("sq", "sk"):
                            act.wait_ge(proj_ready, n + 1)
                            m = turn_index(seg, t)
                            scale = HD ** -0.5 if seg == "sq" else 1.0
                            if t == SAMPLE:
                                dst = q_new[:, 0:DA] if seg == "sq" else k_new[:]
                                if seg == "sq":
                                    act.activation(q_new[:, DA:DA + HD], src[:, 0:HD], ACT.Copy, scale=scale)
                            else:
                                dst = nat[:, m % 2, 0:DA]
                                act.wait_ge(turned, m - 1)
                                if seg == "sk" and t >= 2:
                                    act.wait_ge(k_saved[t % 2], L * 16 * (10, 8)[t % 2] + 16 * (t // 2))
                            act.activation(dst, src, ACT.Copy, scale=scale).then_inc(emptied_act, 1)
                        elif seg in ("fq", "fk"):
                            act.wait_ge(proj_ready, n + 1)
                            m = turn_index(seg, t)
                            if not (seg == "fq" and t < 2) and t < SAMPLE:
                                act.wait_ge(turned, m - 1)
                            if t == SAMPLE:
                                act.wait_ge(turned, m - 1)
                            if seg == "fk":
                                if t == 0:
                                    act.wait_ge(nat_ready, nat_count("fq", SAMPLE))
                                if t >= 2:
                                    act.wait_ge(k_saved[t % 2], L * 16 * (10, 8)[t % 2] + 16 * ((5, 4)[t % 2] + t // 2))
                            act.activation(aug[0:R, m % 2, :, 0:HD], src.rearrange("p (h d) -> p h d", h=HA),
                                           ACT.Copy).then_inc(emptied_act, 1)
                            u = (0 if seg == "fq" else TILES) + t
                            act.wait_ge(head_sums, u + 1)
                            act.activation(small[0:R, 10:15], small[0:R, 5:10], ACT.Sqrt, bias=eps[0:R],
                                           scale=1.0 / HD).then_inc(head_roots, 1)
                        elif seg[:2] == "pg":
                            act.wait_ge(proj_ready, n + 1)
                            if seg == "pg1":
                                act.wait_ge(emptied_dve, evac_count("pe0", t))
                            act.activation(gate[0:R, t, :], src, ACT.Sigmoid).then_inc(emptied_act, 1)
                        if t >= 1 and t - 1 < TURNED.get(seg, 0):
                            turned_to(seg, t - 1)
                    if TURNED.get(seg, 0) == TILES:
                        turned_to(seg, TILES - 1)
                    if seg == "fg":
                        act.wait_ge(logit_ready, 1)
                        act.activation(ltmp, ltmp, ACT.Exp).then_inc(logf_act, 1)
                        act.wait_ge(logf_act, 1)
                        act.activation(ltmp, ltmp, ACT.Ln, bias=1.0).then_inc(logf_act, 1)

            def retention():
                for t in range(TILES):
                    R = rows(t)
                    act.wait_ge(centred_r, t + 1)
                    act.activation(ret_sq[0:R], ret_o[0:R], ACT.Square).then_inc(squares_r, 1)
                    act.wait_ge(sums_r, t + 1)
                    act.activation(small[0:R, 20:26], small[0:R, 30:36], ACT.Sqrt, bias=eps[0:R],
                                   scale=1.0 / HD).then_inc(roots_r, 1)
                phase_over(act, RET)

            def attention(phase):
                kind = KIND[phase]

                def first(u):
                    t, i, h = UNITS[u]
                    n = (t + 1) * P
                    if kind == "sb":
                        act.wait_ge(att_scores[kind], u + 1)
                        if u >= 2:
                            act.wait_ge(att_probs[kind], u - 1)
                        act.activation(sig[:, u % 2, 0:n], bank2(2 * (u % 2), n), ACT.Sigmoid)\
                            .then_inc(att_first[kind], 1)
                    else:
                        act.wait_ge(att_max, u + 1)
                        if u >= 2:
                            act.wait_ge(att_turned[kind], u - 1)
                        if h == 0 and i >= 2:
                            act.wait_ge(att_done[kind], i - 1)
                        act.activation(expd[:, u % 2, 0:n], bank2(2 * (u % 2), n), ACT.Exp,
                                       bias=small[:, 40 + u % 4:41 + u % 4],
                                       accum_out=small[:, 50 + (t % 2) * HA + h:51 + (t % 2) * HA + h])\
                            .then_inc(att_first[kind], 1)

                def to_sbuf(u):
                    t, i, h = UNITS[u]
                    act.wait_ge(att_turned[kind], u + 1)
                    if u >= 2:
                        act.wait_ge(att_out[kind], u - 1)
                    n = (t + 1) * P
                    act.activation(attT[:, u % 2, 0:n], bank2(4, n), ACT.Copy).then_inc(attT_ready[kind], 1)

                first(0)
                for u in range(len(UNITS)):
                    if u + 1 < len(UNITS):
                        first(u + 1)
                    to_sbuf(u)
                phase_over(act, phase)

            def decode(phase, L):
                kind = KIND[phase]
                s = dec[kind]

                def bring_keys(g):
                    if g >= 2:
                        act.wait_ge(s["kt_ready"], 5 * (g - 1))
                    for p in range(PG8 - BY_ACT, PG8):
                        at = g * PG8 + p
                        pg = act.value_load(pages[0:1, at:at + 1])
                        nc.scalar.dma_start(ringK[g % 2][:, p * DA:(p + 1) * DA],
                                            CACHE[kind][0][L, bass.ds(pg, 1)].rearrange("a s h d -> s (a h d)"))\
                            .then_inc(s[f"k{g % 2}"], 16)

                def take_blocks(b, blocks):
                    for n in blocks:
                        act.wait_ge(s["kt_ready"], b * BLOCKS + n + 1)
                        if n >= SLOTS:
                            act.wait_ge(s["scores_done"], b * GROUPS + (n - SLOTS) // 5 + 1)
                        elif not is_first(b):
                            act.wait_ge(s["scores_done"], b * GROUPS + (n - SLOTS + BLOCKS) // 5 + 1 - GROUPS)
                        act.activation(kT_d[n % SLOTS], ps[:, n % 2, :], ACT.Copy).then_inc(s["kt_act"], 1)

                def take_rows(b, j):
                    act.wait_ge(s["scores_done"], b * GROUPS + min(j, 3) + 1)
                    if not is_first(b) or 2 <= j < 4:
                        act.wait_ge(s["z_turned"], 5 * b + (j - 1 if 2 <= j < 4 else (j - 1 if j < 2 else 0)))
                    act.activation(z_rows[:, 2 if j == 4 else j % 2, :],
                                   ps[:, 3 if j == 4 else (5 if j % 2 else 2), :], ACT.Copy)\
                        .then_inc(s["rows_out"], 1)

                def soften(b):
                    if kind == "sb":
                        act.wait_ge(s["soft_in"], b + 1)
                        act.activation(soft, soft, ACT.Exp).then_inc(s["soft_act"], 1)
                        act.wait_ge(s["soft_act"], b * 2 + 1)
                        act.activation(soft, soft, ACT.Ln, bias=1.0).then_inc(s["soft_act"], 1)

                def exponentiate(b):
                    act.wait_ge(s["soft_ready"], b + 1)
                    act.wait_ge(s["o_emptied"], b + 1)
                    act.activation(probs, zs, ACT.Exp).then_inc(s["probs_ready"], 1)

                def sequence(b, before=None):
                    take_blocks(b, (0, 1))
                    if before is not None:
                        soften(before)
                    take_blocks(b, (4,))
                    if is_first(b):
                        bring_keys(2)
                    take_blocks(b, (5, 6, 7))
                    take_rows(b, 0)
                    take_blocks(b, (8, 9))
                    if is_first(b):
                        bring_keys(3)
                    take_blocks(b, (10, 12))
                    if before is not None:
                        exponentiate(before)
                    take_rows(b, 1)
                    take_blocks(b, (14, 16))
                    take_rows(b, 2)
                    take_blocks(b, (18,))
                    take_rows(b, 3)
                    take_rows(b, 4)

                act.preload_act_table_set("natural_log_exp_and_others")
                bring_keys(1)
                sequence(0)
                with act.Fori(1, SEQS) as b:
                    sequence(b, b - 1)
                soften(SEQS - 1)
                exponentiate(SEQS - 1)
                phase_over(act, phase)

            with act.Fori(0, DEPTH) as L:
                for t in range(3):
                    root(0, t)
                project(PROJ_SEGS[PROJ_R], L)
                phase_over(act, PROJ_R)
                retention()
                project(PROJ_SEGS[PROJ_S], L)
                phase_over(act, PROJ_S)
                attention(ATT_S)
                decode(DEC_S, L)
                project(PROJ_SEGS[PROJ_F], L)
                phase_over(act, PROJ_F)
                attention(ATT_F)
                decode(DEC_F, L)
                for t in range(TILES):
                    R = rows(t)
                    act.wait_ge(mixed_turned, t + 1)
                    act.activation(xT[:, :, t * P:t * P + R],
                                   bank2(6).rearrange("p (k n) -> p k n", k=KC)[:, :, 0:R],
                                   ACT.Copy).then_inc(mixed_out, 1)
                for t in range(TILES):
                    R = rows(t)
                    act.wait_ge(p_turned, t + 1)
                    act.activation(pT[:, :, t * P:t * P + R],
                                   ps[:, 3 + t % 2, 0:2 * P].rearrange("p (k n) -> p k n", k=2)[:, :, 0:R],
                                   ACT.Copy).then_inc(p_out, 1)
                project(OUT_SEGS, L)
                project(GATED_SEGS, L)
                layer_over(act, L)

        @block.vector
        def _(dve):
            dve.wait_ge(consts_in, 32)
            dve.wait_ge(set_up, 3)
            link = Steps(dve, steps_sem)

            def bc(ap, shape):
                return ap.unsqueeze(len(shape) - 1).broadcast_to(shape)

            def scale(norm, t):
                m, R = norm * TILES + t, rows(t)
                dve.wait_ge(rooted, m + 1)
                link(dve.reciprocal(small[0:R, 220 + t:221 + t], small[0:R, 210 + t:211 + t]))
                if m >= 2:
                    dve.wait_ge(norm_turned, m - 1)
                dve.tensor_scalar(scaled[0:R, m % 2, :], O[0:R, t, :], small[0:R, 220 + t:221 + t], None,
                                  ALU.mult).then_inc(scaled_ready, 1)

            def normed(norm, t):
                m, R = norm * TILES + t, rows(t)
                dve.wait_ge(norm_turned, m + 1)
                dve.tensor_tensor(xT[:, :, t * P:t * P + R],
                                  bank2(6).rearrange("p (k n) -> p k n", k=KC)[:, :, 0:R],
                                  bc(gT[:, norm, :], [P, KC, R]), ALU.mult).then_inc(norm_out, 1)

            def project(segs):
                for seg in segs:
                    i = ALL_SEGS.index(seg)
                    if seg == "fg":
                        link(dve.memset(logit, 0.0))
                        link(dve.memset(logf_padded[:, 0:NT - 1], 0.0))
                    for t in range(TILES):
                        n, R = i * TILES + t, rows(t)
                        src = ps[0:R, n % 3, :]
                        if seg == "rq" and t + 2 < TILES:
                            scale(0, t + 2)
                        if seg == "rq" and t + 1 < TILES:
                            normed(0, t + 1)
                        if seg in ("rq", "rk"):
                            m = turn_index(seg, t)
                            new = t == SAMPLE
                            xh = src[:, 0:DR].rearrange("p (h c d) -> p h c d", h=HR, c=2)
                            ra = rot_a[0:R].rearrange("p (h d) -> p h d", h=HR)
                            rb = rot_b[0:R].rearrange("p (h c d) -> p h c d", h=HR, c=2)
                            cosb = cos_t[0:R, t, :].unsqueeze(1).broadcast_to([R, HR, HD])
                            dve.wait_ge(proj_ready, n + 1)
                            link(dve.tensor_tensor(ra, src[:, 0:DR].rearrange("p (h d) -> p h d", h=HR), cosb,
                                                   ALU.mult))
                            sinb = sin_t[0:R, t, :].rearrange("p (c d) -> p c d", c=2)
                            for c in range(2):
                                ins = dve.tensor_tensor(rb[:, :, c, :], xh[:, :, 1 - c, :],
                                                        sinb[:, c, :].unsqueeze(1).broadcast_to([R, HR, HD // 2]),
                                                        ALU.mult)
                                ins.then_inc(*((emptied_dve, 1) if c else (steps_sem, 1)))
                            link.n += 1
                            dve.wait_ge(steps_sem, link.base + link.n)
                            dve.wait_ge(emptied_dve, evac_count(seg, t))
                            if m >= 2:
                                dve.wait_ge(turned, m - 1)
                            dve.tensor_tensor(nat[0:R, m % 2, :], rot_a[0:R], rot_b[0:R], ALU.add)\
                                .then_inc(nat_ready, 1)
                            dve.wait_ge(nat_ready, nat_count(seg, t))
                            if seg == "rk":
                                decay = const("key_decay_new" if new else "key_decay")
                                link(dve.tensor_tensor(
                                    kd_r[0:R, t].rearrange("p (h d) -> p h d", h=HR),
                                    nat[0:R, m % 2, :].rearrange("p (h d) -> p h d", h=HR),
                                    bc(decay[0:R], [R, HR, HD]), ALU.mult))
                        elif seg in GATE_AT:
                            w = DR if seg == "rg" else DA
                            gates = {"rg": 0, "sg": 1, "fg": 2}[seg]
                            dve.wait_ge(proj_ready, n + 1)
                            dve.wait_ge(sigmoid_ready, gates * TILES + t + 1)
                            if seg == "fg":
                                link(dve.tensor_tensor(logit[0:R, t, :], src[:, DA:DA + HA], b_f_b[0:R], ALU.add))
                            out = O[0:R, t, GATE_AT[seg]:GATE_AT[seg] + w]
                            dve.tensor_tensor(out, out, src[:, 0:w], ALU.mult).then_inc(emptied_dve, 1)
                        elif seg in ("fq", "fk"):
                            m = turn_index(seg, t)
                            dve.wait_ge(emptied_act, evac_count(seg, t))
                            x = aug[0:R, m % 2, :, 0:HD]
                            link(dve.tensor_tensor(squares[0:R], x, x, ALU.mult))
                            dve.tensor_reduce(small[0:R, 5:10], squares[0:R], AX, ALU.add).then_inc(head_sums, 1)
                            last = aug[0:R, m % 2, :, HD:HD + 1]
                            if seg == "fq":
                                link(dve.memset(last, 1.0))
                            else:
                                link(dve.tensor_copy(last, neg_c[0:R, t, :].unsqueeze(2)))
                            u = (0 if seg == "fq" else TILES) + t
                            dve.wait_ge(head_roots, u + 1)
                            link(dve.reciprocal(small[0:R, 15:20], small[0:R, 10:15]))
                            link(dve.tensor_tensor(x, x, bc(small[0:R, 15:20], [R, HA, HD]), ALU.mult))
                            g = (g_fq_b if seg == "fq" else g_fk_b)[0:R].unsqueeze(1).broadcast_to([R, HA, HD])
                            if t < SAMPLE:
                                dst = x
                            else:
                                dst = (q_new[:, 0:DA] if seg == "fq" else k_new[:]).rearrange("p (h d) -> p h d", h=HA)
                            if t == SAMPLE and seg == "fq":
                                link(dve.tensor_tensor(q_new[:, DA:DA + HD], x[:, 0, :], g_fq_b[0:R], ALU.mult))
                            dve.tensor_tensor(dst, x, g, ALU.mult).then_inc(nat_ready, 1)
                            dve.wait_ge(nat_ready, nat_count(seg, t))
                        elif seg[:3] == "out":
                            if seg == "out0" and t == 4:
                                gate_decoded("fox").then_inc(sample_mixed, 1)
                            m = (i - ALL_SEGS.index("out0")) * TILES + t
                            c = int(seg[-1])
                            dve.wait_ge(proj_ready, n + 1)
                            dve.wait_ge(x_half_in[m % 2], 16 * (m // 2 + 1))
                            dve.tensor_tensor(O[0:R, t, c * 512:(c + 1) * 512], src, x_half[0:R, m % 2, :], ALU.add)\
                                .then_inc(emptied_dve, 1)
                            if c == 1 and t >= 1:
                                scale(1, t - 1)
                            if c == 1 and t >= 2:
                                normed(1, t - 2)
                        elif seg[:2] == "pe":
                            c = int(seg[-1])
                            dve.wait_ge(proj_ready, n + 1)
                            dve.wait_ge(emptied_act, evac_count("pg" + seg[-1], t))
                            dve.tensor_tensor(gated[0:R, t % 2, :], src, gate[0:R, t, :], ALU.mult)\
                                .then_inc(emptied_dve, 1)
                            dve.wait_ge(emptied_dve, evac_count(seg, t))
                            out = O[0:R, t, c * 512:(c + 1) * 512]
                            link(dve.tensor_tensor(out, out, gated[0:R, t % 2, :], ALU.add))
                    if seg == "fg":
                        dve.scalar_tensor_tensor(ltmp, logit, -1.0, logit, ALU.mult, ALU.min).then_inc(logit_ready, 1)
                        dve.wait_ge(logf_act, 2)
                        dve.scalar_tensor_tensor(logf, logit, 0.0, ltmp, ALU.min, ALU.subtract)\
                            .then_inc(logf_ready, 1)
                        dve.wait_ge(cum_ready, 1)
                        link(dve.tensor_copy(neg_c[:, 0:NT, :], ps[:, 7, 0:NT * HA].rearrange(
                            "p (t h) -> p t h", h=HA)))
                        link(dve.tensor_copy(neg_c[0:ROWS, SAMPLE, :], ps[0:ROWS, 7, 64:64 + HA]))

            def retention():
                def mask(t, h):
                    u, R, new = t * HR + h, rows(t), t == SAMPLE
                    dve.wait_ge(scores_r, u + 1)
                    if u >= 3:
                        dve.wait_ge(inner_r, u - 2)
                    grow = const("col_grow_new" if new else "col_grow")[0:R, h:h + 1]
                    upto = const("upto_new" if new else "upto")[0:R, 0:R]
                    dve.scalar_tensor_tensor(masked[0:R, u % 3, 0:R], ps[0:R, RET_BANKS[u % 3], 0:R], grow, upto,
                                             ALU.mult, ALU.mult).then_inc(masked_r, 1)

                def update(t):
                    dve.wait_ge(kv_r, t + 1)
                    kv = ps[:, 4, 0:QP * P].rearrange("p (c n) -> p c n", c=QP)
                    state = states[:, t % 2]
                    if t > 0:
                        dve.wait_ge(state_r, t)
                        dve.wait_ge(inner_r, HR * t)
                        link(dve.tensor_tensor(state, states[:, (t - 1) % 2],
                                               bc(const("chunk_decay"), [P, QP, HD]), ALU.mult))
                    for h2 in range(2):
                        q = slice(h2 * HD, (h2 + 1) * HD)
                        mine = kv[q, :, h2 * HD:(h2 + 1) * HD]
                        if t > 0:
                            ins = dve.tensor_tensor(state[q], state[q], mine, ALU.add)
                        else:
                            ins = dve.tensor_copy(state[q], mine)
                        if h2 == 0:
                            link(ins)
                    ins.then_inc(state_r, 1)

                def centre(t):
                    R, new = rows(t), t == SAMPLE
                    dve.wait_ge(inner_r, HR * (t + 1))
                    grow = const("row_grow_new" if new else "row_grow")
                    o = ret_o[0:R]
                    if new:
                        out = ps[0:R, 2, 0:DR].rearrange("p (h d) -> p h d", h=HR)
                        link(dve.tensor_tensor(o, out, ret_sq[0:R], ALU.add))
                        dve.tensor_tensor(o, o, bc(grow[0:R], [R, HR, HD]), ALU.mult).then_inc(ret_emptied, 1)
                    else:
                        for h2 in range(2):
                            out = ps[:, 2 + t % 2 + 4 * h2, 0:QP * HD].rearrange("p (c d) -> p c d", c=QP)
                            ins = dve.tensor_tensor(
                                o.rearrange("p (c a) d -> p c a d", a=2)[:, :, h2, :], out,
                                bc(grow.rearrange("p (c a) -> p c a", a=2)[:, :, h2], [P, QP, HD]), ALU.mult)
                            if h2 == 0:
                                link(ins)
                        ins.then_inc(ret_emptied, 1)
                    dve.wait_ge(ret_emptied, t + 1)
                    link(dve.tensor_reduce(small[0:R, 36:42], o, AX, ALU.add))
                    link(dve.tensor_scalar(small[0:R, 36:42], small[0:R, 36:42], 1.0 / HD, None, ALU.mult))
                    dve.tensor_tensor(o, o, bc(small[0:R, 36:42], [R, HR, HD]), ALU.subtract).then_inc(centred_r, 1)

                def square_sums(t):
                    R = rows(t)
                    dve.wait_ge(squares_r, t + 1)
                    dve.tensor_reduce(small[0:R, 30:36], ret_sq[0:R], AX, ALU.add).then_inc(sums_r, 1)

                def mix(t):
                    R = rows(t)
                    o = ret_o[0:R]
                    dve.wait_ge(roots_r, t + 1)
                    link(dve.reciprocal(small[0:R, 42:48], small[0:R, 20:26]))
                    link(dve.tensor_tensor(o, o, bc(small[0:R, 42:48], [R, HR, HD]), ALU.mult))
                    mixed = O[0:R, t, 0:DR]
                    link(dve.tensor_tensor(mixed, mixed, g_ret_b[0:R], ALU.mult))
                    link(dve.tensor_tensor(mixed, mixed, o.rearrange("p h d -> p (h d)"), ALU.mult))

                own = const("own_seq")[0:ROWS]

                def own_values(h):
                    if h >= 2:
                        dve.wait_ge(new_state_ready, h - 1)
                    dve.tensor_tensor(v_seq[0:ROWS, h % 2, :].rearrange("p (b e) -> p b e", b=SEQS),
                                      v_r[0:ROWS, SAMPLE, h * HD:(h + 1) * HD].unsqueeze(1).broadcast_to(
                                          [ROWS, SEQS, HD]),
                                      bc(own, [ROWS, SEQS, HD]), ALU.mult).then_inc(v_seq_ready, 1)

                for t in range(TILES):
                    for h in range(HR):
                        mask(t, h)
                        if h == 1 and t >= 1:
                            centre(t - 1)
                        if h == 3 and t < SAMPLE:
                            update(t)
                        if h == 3 and t >= 1:
                            square_sums(t - 1)
                        if h == 4 and t >= 1:
                            mix(t - 1)
                for h in range(HR):
                    dve.wait_ge(cross_ready, h + 1)
                    dve.tensor_tensor(cross[0:ROWS], ps[0:ROWS, 6 + h % 2, :].rearrange("p (b e) -> p b e", b=SEQS),
                                      bc(own, [ROWS, SEQS, HD]), ALU.mult).then_inc(cross_emptied, 1)
                    dve.wait_ge(cross_emptied, h + 1)
                    link(dve.tensor_reduce(ret_sq[0:ROWS, h, :], cross[0:ROWS].rearrange("p b e -> p e b"), AX,
                                           ALU.add))
                own_values(0)
                own_values(1)
                centre(SAMPLE)
                square_sums(SAMPLE)
                mix(SAMPLE)
                for h in range(HR):
                    pr, q = h // 2, slice((h % 2) * HD, (h % 2) * HD + HD)
                    dve.wait_ge(new_state_ready, h + 1)
                    mine = s0[q, pr].rearrange("p b e -> p (b e)")
                    dve.scalar_tensor_tensor(mine, mine, const("chunk_decay_new")[q, pr:pr + 1],
                                             ps[q, 4 + h % 2, :], ALU.mult, ALU.add).then_inc(new_state_out, 1)
                    if h + 2 < HR:
                        own_values(h + 2)
                phase_over(dve, RET)

            def attention(phase, L):
                kind = KIND[phase]
                if kind == "sb":
                    link(dve.memset(prod[:, SEQ:SEQ + 1], 1.0))

                def stick(u):
                    t, i, h = UNITS[u]
                    n = (t + 1) * P
                    s = sig[:, u % 2, 0:n]
                    r, e = rest[:, 0:n], SEQ - n
                    dve.wait_ge(att_first[kind], u + 1)
                    link(dve.tensor_tensor(s[:, t * P:n], s[:, t * P:n], const("before"), ALU.mult))
                    link(dve.tensor_scalar(r, s, -1.0, 1.0, ALU.mult, ALU.add))
                    dve.wait_ge(att_probs[kind], u)
                    link(dve.tensor_tensor_scan(prod[:, e:SEQ][:, ::-1], r[:, ::-1], r[:, ::-1], 1.0, ALU.mult,
                                                ALU.bypass))
                    if u >= 2:
                        dve.wait_ge(att_turned[kind], u - 1)
                    dve.tensor_tensor(att[:, u % 2, 0:n], s, prod[:, e + 1:SEQ + 1], ALU.mult)\
                        .then_inc(att_probs[kind], 1)

                def largest(u):
                    t, i, h = UNITS[u]
                    n = (t + 1) * P
                    dve.wait_ge(att_scores[kind], u + 1)
                    diag = bank2(2 * (u % 2), n)[:, t * P:n]
                    link(dve.tensor_tensor(diag, diag, const("after_neg"), ALU.add))
                    if u >= 4:
                        dve.wait_ge(att_first[kind], u - 3)
                    dve.tensor_reduce(small[:, 40 + u % 4:41 + u % 4], bank2(2 * (u % 2), n), AX, ALU.max,
                                      negate=True).then_inc(att_max, 1)

                def finish(t):
                    dve.wait_ge(att_out[kind], HA * (NT - t))
                    at = DR if kind == "sb" else DR + DA
                    out = O[:, t, at:at + DA]
                    o = ps[:, 6 + t % 2, 0:DA]
                    if kind == "fox":
                        link(dve.reciprocal(small[:, 60:65], small[:, 50 + (t % 2) * HA:50 + (t % 2 + 1) * HA]))
                        o3 = out.rearrange("p (h d) -> p h d", h=HA)
                        link(dve.tensor_tensor(o3, o3, bc(small[:, 60:65], [P, HA, HD]), ALU.mult))
                    dve.tensor_tensor(out, out, o, ALU.mult).then_inc(att_done[kind], 1)

                for u, (t, i, h) in enumerate(UNITS):
                    (stick if kind == "sb" else largest)(u)
                    if h == 2 and i >= 1:
                        finish(t + 1)
                    if kind == "fox" and h == 4 and 1 <= i <= 2:
                        page_sums(L, i - 1)
                finish(0)
                phase_over(dve, phase)

            def page_sums(L, half):
                dve.wait_ge(logf_in, 16 * (L + 1))
                for h in range(HA):
                    x = page_logf[:, half, :, h][:, ::-1]
                    ins = dve.tensor_tensor_scan(page_sum[:, half, h, :][:, ::-1], ones, x, 0.0, ALU.mult,
                                                 ALU.add)
                    if h < HA - 1:
                        link(ins)
                ins.then_inc(page_ready, 1)
                dve.wait_ge(page_ready, half + 1)

            def gate_decoded(kind):
                dve.wait_ge(dec[kind]["loaded"], 16)
                at = DR if kind == "sb" else DR + DA
                out = O[0:ROWS, SAMPLE, at:at + DA]
                return dve.tensor_tensor(out, out, decoded_rows[kind], ALU.mult)

            def forget_sums(L):
                for half in range(2):
                    dve.wait_ge(page_carry, half + 1)
                    link(dve.tensor_tensor(page_sum[:, half], page_sum[:, half],
                                           page_logf[:, half].rearrange("p s h -> p h s"), ALU.subtract))
                    dve.tensor_tensor(page_sum[:, half], page_sum[:, half],
                                      bc(ps[:, 6 + half, 0:HA], [P, HA, P]), ALU.add).then_inc(forget_part, 1)
                for h in range(HA):
                    dve.wait_ge(forget_turned, h + 1)
                    dve.tensor_copy(forget[:, h, :], ps[:, h % 2, 0:2 * P]).then_inc(forget_ready, 1)

            def decode(phase, L):
                kind = KIND[phase]
                s = dec[kind]
                if kind == "fox":
                    forget_sums(L)
                link(dve.memset(qd, 0.0))
                link(dve.memset(kT_new, 0.0))
                link(dve.memset(row_max[:], 0.0))
                link(dve.memset(q_now, 0.0))
                dve.memset(ps[:, 4, :], 1.0).then_inc(s["o_emptied"], 1)
                dve.wait_ge(s["o_emptied"], 1)
                zr = zs.rearrange("p (r s) -> p r s", s=SLOT)
                z4 = zs.rearrange("p (h i s) -> p h i s", h=HA, i=NEW)
                link(dve.memset(zr[ROWS:P, :, PAGES:SLOT], NEG))
                neg = const("new_neg_" + kind, SEQS, NEW)[0:ROWS]
                for h in range(HA):
                    link(dve.tensor_copy(new_bias[0:ROWS, :, h, :], neg))
                if kind == "fox":
                    for h in range(HA):
                        link(dve.tensor_scalar(new_bias[0:ROWS, :, h, :], new_bias[0:ROWS, :, h, :],
                                               neg_c[0:ROWS, SAMPLE, h:h + 1], None, ALU.add))
                dve.wait_ge(s["new_turned"], 1)
                qsrc = ps[:, 0, 0:5 * ROWS].rearrange("p (c b i) -> p b c i", c=5, b=SEQS)
                link(dve.tensor_copy(qd[0:HD, :, :, 0:NEW], qsrc[0:HD]))
                link(dve.tensor_copy(qd[HD:P, :, :, NEW:2 * NEW], qsrc[HD:P]))
                link(dve.tensor_copy(kT_new[:, 0:2, :], ps[:, 1, 0:2 * ROWS].rearrange("p (c n) -> p c n", c=2)))
                dve.tensor_copy(kT_new[0:HD, 2, :], ps[0:HD, 1, 2 * ROWS:3 * ROWS]).then_inc(s["new_ready"], 1)

                dve.wait_ge(s["new_ready"], 1)
                dve.wait_ge(s["new_scored"], 1)
                new_z = ps[0:ROWS, 2, 0:3 * P].rearrange("p (c b x) -> p b c x", c=3, b=SEQS)
                new_rows = new_bias[0:ROWS].rearrange("p b h i -> p b (h i)")
                for c in range(3):
                    to = new_rows[:, :, 2 * NEW * c:min(HI, 2 * NEW * (c + 1))]
                    link(dve.tensor_tensor(to, to, new_z[:, :, c, 0:to.shape[2]], ALU.add))

                def queries(b, first=False):
                    if not first:
                        dve.wait_ge(s["scores_done"], b * GROUPS)
                    dve.tensor_copy(q_now[:, :, 0:2 * NEW], qd[:, b]).then_inc(s["q_ready"], 1)

                def take_blocks(b, blocks):
                    for n in blocks:
                        dve.wait_ge(s["kt_ready"], b * BLOCKS + n + 1)
                        if n >= SLOTS:
                            dve.wait_ge(s["scores_done"], b * GROUPS + (n - SLOTS) // 5 + 1)
                        elif not is_first(b):
                            dve.wait_ge(s["scores_done"], b * GROUPS + (n - SLOTS + BLOCKS) // 5 + 1 - GROUPS)
                        dve.tensor_copy(kT_d[n % SLOTS], ps[:, n % 2, :]).then_inc(s["kt_dve"], 1)

                def drain(b, j):
                    dve.wait_ge(s["z_turned"], 5 * b + j + 1)
                    if j == 0 and not is_first(b):
                        dve.wait_ge(s["probs_ready"], b)
                    by_pair = zr[:, :, 0:PAGES].rearrange("p r (g m two) -> p g r m two", g=GROUPS, two=2)
                    src = ps[:, 6 + j % 2, :].rearrange("p (m k r) -> p k r m", m=4, k=4)
                    if j == 4:
                        for g in range(GROUPS):
                            ins = dve.tensor_copy(by_pair[:, g, 3 * NEW:, :, 1], src[:, g, 0:2 * NEW])
                    else:
                        for kk in range(2):
                            dve.tensor_copy(by_pair[:, j, 2 * NEW * kk:2 * NEW * (kk + 1), :, 0],
                                            src[:, kk, 0:2 * NEW])
                        dve.tensor_copy(by_pair[:, j, 4 * NEW:, :, 0], src[:, 2, 0:NEW])
                        dve.tensor_copy(by_pair[:, j, 0:NEW, :, 1], src[:, 2, NEW:2 * NEW])
                        ins = dve.tensor_copy(by_pair[:, j, NEW:3 * NEW, :, 1], src[:, 3, 0:2 * NEW])
                    ins.then_inc(s["z_drained"], 1)

                def soften_first(b):
                    link(dve.tensor_copy(zr[0:ROWS, :, PAGES], new_rows[:, b]))
                    dve.wait_ge(s["z_drained"], 5 * b + 5)
                    if kind == "sb":
                        dve.scalar_tensor_tensor(soft, zs, -1.0, zs, ALU.mult, ALU.min).then_inc(s["soft_in"], 1)
                    else:
                        fb = forget[:, :, bass.ds(b * PAGES, PAGES)].unsqueeze(2).broadcast_to(
                            [P, HA, NEW, PAGES])
                        link(dve.tensor_tensor(z4[:, :, :, 0:PAGES], z4[:, :, :, 0:PAGES], fb, ALU.add))
                        dve.tensor_reduce(row_max[:, 0:HI], zr, AX, ALU.max).then_inc(s["soft_in"], 1)

                def soften(b):
                    if kind == "sb":
                        dve.wait_ge(s["soft_act"], 2 * b + 2)
                        link(dve.scalar_tensor_tensor(soft, zs, 0.0, soft, ALU.max, ALU.add))
                        dve.tensor_tensor_scan(later[:, ::-1], reset[:, ::-1], soft[:, ::-1], 0.0, ALU.mult,
                                               ALU.add).then_inc(s["sum_ready"], 1)
                    else:
                        dve.wait_ge(s["fold_ready"], b + 1)
                        link(dve.tensor_reduce(small[0:HI, 180:181], ps[0:HI, 6, 0:P], AX, ALU.max, negate=True))
                        dve.tensor_scalar(small[0:HI, 120:120 + HI], ident[0:HI, 0:HI], small[0:HI, 180:181], None,
                                          ALU.mult).then_inc(s["fold_out"], 1)

                def exponents(b):
                    if kind == "sb":
                        dve.wait_ge(s["expo_ready"], b + 1)
                        z3 = zs.rearrange("p (c n) -> p c n", c=3)
                        dve.tensor_tensor(z3, z3, ps[:, 5:8, 0:440], ALU.add).then_inc(s["soft_ready"], 1)
                    else:
                        dve.wait_ge(s["bias_ready"], b + 1)
                        dve.tensor_tensor(zr, zr, bc(ps[:, 6, P:P + HI], [P, HI, SLOT]), ALU.add)\
                            .then_inc(s["soft_ready"], 1)

                def denominators(b):
                    if kind == "fox":
                        dve.wait_ge(s["probs_ready"], b + 1)
                        dve.tensor_reduce(small[:, 40:40 + HI], probs.rearrange("p (r s) -> p r s", s=SLOT), AX,
                                          ALU.add).then_inc(s["den_ready"], 1)

                def take(b):
                    dve.wait_ge(s["pv_done"], b + 1)
                    o = ps[:, 4, 0:P].rearrange("p (a d) -> p a d", a=2)
                    if kind == "sb":
                        dve.tensor_copy(decoded[:, b], o).then_inc(s["o_emptied"], 1)
                    else:
                        link(dve.reciprocal(small[:, 182:184], ps[:, 4, P:P + 2]))
                        dve.tensor_tensor(decoded[:, b], o, bc(small[:, 182:184], [P, 2, HD]), ALU.mult)\
                            .then_inc(s["o_emptied"], 1)

                def sequence(b, before=None, two_before=None):
                    queries(b, before is None)
                    take_blocks(b, (2, 3))
                    if before is not None:
                        soften(before)
                    if two_before is not None:
                        take(two_before)
                    if before is not None:
                        exponents(before)
                    take_blocks(b, (11,))
                    drain(b, 0)
                    if before is not None:
                        denominators(before)
                    take_blocks(b, (13,))
                    drain(b, 1)
                    take_blocks(b, (15, 17, 19))
                    drain(b, 2)
                    drain(b, 3)
                    drain(b, 4)
                    soften_first(b)

                sequence(0)
                sequence(1, 0)
                first = link.n - 2 * DECODE_STEPS[kind]
                with dve.Fori(2, SEQS) as b:
                    link.turn(b, DECODE_STEPS[kind], first)
                    sequence(b, b - 1, b - 2)
                    assert link.n == DECODE_STEPS[kind], (kind, link.n)
                link.turn(SEQS, DECODE_STEPS[kind], first)
                soften(SEQS - 1)
                take(SEQS - 2)
                exponents(SEQS - 1)
                denominators(SEQS - 1)
                take(SEQS - 1)
                link.base, link.n = 0, link.base + link.n
                phase_over(dve, phase)

            with dve.Fori(0, DEPTH) as L:
                link.base, link.n = 0, 0
                dve.wait_ge(first_w, 32 * (L + 1))
                scale(0, 0)
                scale(0, 1)
                normed(0, 0)
                project(PROJ_SEGS[PROJ_R])
                phase_over(dve, PROJ_R)
                dve.wait_ge(vec_loaded, 5 * 16)
                link(dve.tensor_scalar(g_fq_b[:], g_fq_b[:], HD ** -0.5, None, ALU.mult))
                retention()
                project(PROJ_SEGS[PROJ_S])
                phase_over(dve, PROJ_S)
                attention(ATT_S, L)
                decode(DEC_S, L)
                project(PROJ_SEGS[PROJ_F])
                link(gate_decoded("sb"))
                phase_over(dve, PROJ_F)
                attention(ATT_F, L)
                decode(DEC_F, L)
                project(OUT_SEGS)
                scale(1, SAMPLE)
                normed(1, NT - 1)
                normed(1, SAMPLE)
                project(GATED_SEGS)
                layer_over(dve, L)


_INS = ["x_prompt", "x_sample", "state_ret", "cache_sb_k", "cache_sb_v", "cache_fox_k", "cache_fox_v",
        "cache_fox_logf", "page_table", "p_prompt", "p_sample", "g_norm", "w_in", "b_f", "g_ret_gn",
        "g_fox_q", "g_fox_k", "w_out", "w_pe", "g_pe", "w_pg"]
_OUTS = [(1, SEQ, D), (SEQS, NEW, D), (DEPTH, 1, HR, HD, HD), (DEPTH, SEQS, HR, HD, HD),
         (DEPTH, 1, SEQ, HA, HD), (DEPTH, 1, SEQ, HA, HD), (DEPTH, SEQS, NEW, HA, HD),
         (DEPTH, SEQS, NEW, HA, HD), (DEPTH, 1, SEQ, HA, HD), (DEPTH, 1, SEQ, HA, HD),
         (DEPTH, 1, SEQ, HA), (DEPTH, SEQS, NEW, HA, HD), (DEPTH, SEQS, NEW, HA, HD),
         (DEPTH, SEQS, NEW, HA)]


def kernel(**inputs):
    import concourse.bacc as _bacc
    from concourse import mybir as _mybir
    from concourse.bass_utils import run_bass_kernel_spmd as _run

    nc = _bacc.Bacc("TRN2", target_bir_lowering=False, num_devices=1)
    arrays, args = {}, []
    for name in _INS:
        a = np.ascontiguousarray(inputs[name])
        arrays[f"in_{name}_dram"] = a
        args.append(nc.dram_tensor(f"in_{name}_dram", a.shape, _mybir.dt.from_np(a.dtype),
                                   kind="ExternalInput").ap())
    consts = np.concatenate(list(tables().values()), axis=1)
    arrays["in_consts_dram"] = consts
    args.append(nc.dram_tensor("in_consts_dram", consts.shape, F32, kind="ExternalInput").ap())
    for i, shape in enumerate(_OUTS):
        args.append(nc.dram_tensor(f"out_{i}_dram", shape, F32, kind="ExternalOutput").ap())
    step_program(nc, *args)
    r = _run(nc, [arrays], core_ids=[0])
    return tuple(r.results[0][f"out_{i}_dram"] for i in range(len(_OUTS)))
```
